# Optimizing a Trainium2 kernel written in Bass

```python
import jax, jax.numpy as jnp
from jax import lax
import numpy as np
import math

D_MODEL = 1024
BATCH = 1
SEQ = 256
DEPTH = 2

HEAD_DIM = 64
N_Q_HEADS = 12
N_KV_HEADS_A = 4
N_MEM_HEADS = 4
N_MEM = 256
MIX_WIDTH = (N_Q_HEADS + N_MEM_HEADS) * HEAD_DIM
W_IN_A = (N_Q_HEADS + 2 * N_KV_HEADS_A + N_MEM_HEADS) * HEAD_DIM
W_IN_B = (3 * N_Q_HEADS + N_MEM_HEADS) * HEAD_DIM
WINDOW = 128
BLOCK = 128
GRID_W = 64
NA_ROWS_MAX = 8
NA_COLS = 16
D_FF = -(-8 * D_MODEL // (3 * 256)) * 256
N_LAYERS_A = (DEPTH + 1) // 2
N_LAYERS_B = DEPTH // 2
EPS = 1e-6
NEG_INF = -1e30


def rmsnorm(x, g):
    x32 = x.astype(jnp.float32)
    y = x32 * lax.rsqrt(jnp.mean(x32 * x32, axis=-1, keepdims=True) + EPS)
    return (y * g.astype(jnp.float32)).astype(x.dtype)

def alibi_slopes(n_heads):
    return 2.0 ** (-8.0 * jnp.arange(1, n_heads + 1, dtype=jnp.float32) / n_heads)

def windowed_gqa(q, k, v, sink):
    B, S, H, D = q.shape
    Hk = k.shape[2]
    G = H // Hk
    nb = S // BLOCK
    qb = q.reshape(B, nb, BLOCK, Hk, G, D)
    pad = ((0, 0), (BLOCK, BLOCK), (0, 0), (0, 0))
    kp = jnp.pad(k, pad).reshape(B, nb + 2, BLOCK, Hk, D)
    vp = jnp.pad(v, pad).reshape(B, nb + 2, BLOCK, Hk, D)
    kband = jnp.concatenate([kp[:, :-2], kp[:, 1:-1], kp[:, 2:]], axis=2)
    vband = jnp.concatenate([vp[:, :-2], vp[:, 1:-1], vp[:, 2:]], axis=2)
    q_pos = jnp.arange(S).reshape(nb, BLOCK)
    k_pos = jnp.arange(nb)[:, None] * BLOCK - BLOCK + jnp.arange(3 * BLOCK)[None, :]
    dist = jnp.abs(q_pos[:, :, None] - k_pos[:, None, :])
    allowed = (dist <= WINDOW) & (k_pos[:, None, :] >= 0) & (k_pos[:, None, :] < S)
    slopes = alibi_slopes(H).reshape(1, Hk, G, 1, 1, 1)
    s = jnp.einsum('bnikgd,bnukd->bkgniu', qb, kband).astype(jnp.float32) * (D ** -0.5)
    s = s - slopes * dist.astype(jnp.float32)[None, None, None]
    s = jnp.where(allowed[None, None, None], s, NEG_INF)
    sink_col = jnp.broadcast_to(sink.astype(jnp.float32).reshape(1, Hk, G, 1, 1, 1), s.shape[:-1] + (1,))
    p = jax.nn.softmax(jnp.concatenate([s, sink_col], axis=-1), axis=-1)[..., :-1]
    o = jnp.einsum('bkgniu,bnukd->bnikgd', p.astype(v.dtype), vband)
    return o.reshape(B, S, H * D)

def neighbourhood_attn(q, k, v, rpb):
    B, S, H, D = q.shape
    rows = S // GRID_W
    kr = min(NA_ROWS_MAX, rows)
    qg = q.reshape(B, rows, GRID_W, H, D)
    kg = k.reshape(B, rows, GRID_W, H, D)
    vg = v.reshape(B, rows, GRID_W, H, D)
    r = jnp.arange(rows)
    row_start = jnp.clip(r - kr // 2, 0, rows - kr)
    row_idx = row_start[:, None] + jnp.arange(kr)[None, :]
    kband = kg[:, row_idx]
    vband = vg[:, row_idx]
    c = jnp.arange(GRID_W)
    col_start = jnp.clip(c - NA_COLS // 2, 0, GRID_W - NA_COLS)
    in_win = (c[None, :] >= col_start[:, None]) & (c[None, :] < col_start[:, None] + NA_COLS)
    dr_idx = row_idx - r[:, None] + NA_ROWS_MAX - 1
    dc_idx = jnp.clip(c[None, :] - c[:, None], -(NA_COLS - 1), NA_COLS - 1) + NA_COLS - 1
    bias = rpb.astype(jnp.float32)[:, dr_idx][:, :, :, dc_idx]
    bias = bias.transpose(0, 1, 3, 2, 4)
    s = jnp.einsum('brchd,brijhd->bhrcij', qg, kband).astype(jnp.float32) * (D ** -0.5)
    s = s + bias[None]
    s = jnp.where(in_win[None, None, None, :, None, :], s, NEG_INF)
    sh = s.shape
    p = jax.nn.softmax(s.reshape(sh[:-2] + (kr * GRID_W,)), axis=-1).reshape(sh)
    o = jnp.einsum('bhrcij,brijhd->brchd', p.astype(v.dtype), vband)
    return o.reshape(B, S, H * D)

def memory_attn(q, k, v):
    B, S, Hm, D = q.shape
    s = jnp.einsum('bshd,bmhd->bhsm', q, k).astype(jnp.float32) * (D ** -0.5)
    p = jax.nn.softmax(s, axis=-1)
    o = jnp.einsum('bhsm,bmhd->bshd', p.astype(v.dtype), v)
    return o.reshape(B, S, Hm * D)

def first_inputs(seed: int = 0) -> dict:
    key = jax.random.key(seed)
    ks = jax.random.split(key, 16)
    f32 = jnp.float32
    nrm = lambda k, shape, scale: jax.random.normal(k, shape, f32) * scale
    return {
        "x": nrm(ks[0], (BATCH, SEQ, D_MODEL), 1.0),
        "mem": nrm(ks[1], (BATCH, N_MEM, D_MODEL), 1.0),
        "norm_mix": 1.0 + nrm(ks[2], (DEPTH, D_MODEL), 0.02),
        "norm_ffn": 1.0 + nrm(ks[3], (DEPTH, D_MODEL), 0.02),
        "norm_mem": 1.0 + nrm(ks[4], (D_MODEL,), 0.02),
        "norm_final": 1.0 + nrm(ks[5], (D_MODEL,), 0.02),
        "w_in_a": nrm(ks[6], (N_LAYERS_A, D_MODEL, W_IN_A), D_MODEL ** -0.5),
        "sink_a": nrm(ks[7], (N_LAYERS_A, N_Q_HEADS), 0.5),
        "w_in_b": nrm(ks[8], (N_LAYERS_B, D_MODEL, W_IN_B), D_MODEL ** -0.5),
        "rpb_b": nrm(ks[9], (N_LAYERS_B, N_Q_HEADS, 2 * NA_ROWS_MAX - 1, 2 * NA_COLS - 1), 0.3),
        "w_mem_kv": nrm(ks[10], (DEPTH, D_MODEL, 2 * N_MEM_HEADS * HEAD_DIM), D_MODEL ** -0.5),
        "w_out": nrm(ks[11], (DEPTH, MIX_WIDTH, D_MODEL), MIX_WIDTH ** -0.5),
        "w_gate_up": nrm(ks[12], (DEPTH, D_MODEL, 2 * D_FF), D_MODEL ** -0.5),
        "w_down": nrm(ks[13], (DEPTH, D_FF, D_MODEL), D_FF ** -0.5),
    }

def first_block(x, mem, norm_mix, norm_ffn, norm_mem, norm_final, w_in_a, sink_a, w_in_b, rpb_b,
              w_mem_kv, w_out, w_gate_up, w_down):
    B, S, _ = x.shape
    qw = N_Q_HEADS * HEAD_DIM
    kvw = N_KV_HEADS_A * HEAD_DIM
    mw = N_MEM_HEADS * HEAD_DIM
    mem_n = rmsnorm(mem, norm_mem)
    for i in range(DEPTH):
        li = i // 2
        h = rmsnorm(x, norm_mix[i])
        mkv = mem_n @ w_mem_kv[i]
        mk = mkv[..., :mw].reshape(B, N_MEM, N_MEM_HEADS, HEAD_DIM)
        mv = mkv[..., mw:].reshape(B, N_MEM, N_MEM_HEADS, HEAD_DIM)
        if i % 2 == 0:
            proj = h @ w_in_a[li]
            q, k, v, qm = jnp.split(proj, [qw, qw + kvw, qw + 2 * kvw], axis=-1)
            y_tok = windowed_gqa(q.reshape(B, S, N_Q_HEADS, HEAD_DIM),
                                 k.reshape(B, S, N_KV_HEADS_A, HEAD_DIM),
                                 v.reshape(B, S, N_KV_HEADS_A, HEAD_DIM), sink_a[li])
        else:
            proj = h @ w_in_b[li]
            q, k, v, qm = jnp.split(proj, [qw, 2 * qw, 3 * qw], axis=-1)
            y_tok = neighbourhood_attn(q.reshape(B, S, N_Q_HEADS, HEAD_DIM),
                                       k.reshape(B, S, N_Q_HEADS, HEAD_DIM),
                                       v.reshape(B, S, N_Q_HEADS, HEAD_DIM), rpb_b[li])
        y_mem = memory_attn(qm.reshape(B, S, N_MEM_HEADS, HEAD_DIM), mk, mv)
        x = x + jnp.concatenate([y_tok, y_mem], axis=-1) @ w_out[i]
        h = rmsnorm(x, norm_ffn[i])
        gu = h @ w_gate_up[i]
        x = x + (jax.nn.silu(gu[..., :D_FF]) * gu[..., D_FF:]) @ w_down[i]
    return rmsnorm(x, norm_final)


DEPTH_2 = 1

N_HEADS = 8
N_KV_HEADS = 2
IDX_HEADS = 8
IDX_DIM = 64
TOPK_MAX = 256
Q_BLOCK = 64
N_BUCKETS = 32
MAX_DISTANCE = 128
D_RNN = D_MODEL
N_RNN_BLOCKS = 8
RNN_BLOCK = D_RNN // N_RNN_BLOCKS
RNN_CONV = 4
LRU_C = 8.0
D_FF_2 = 2816
FFN_CONV = 3

ATTN_WIDTH = N_HEADS * HEAD_DIM
KV_WIDTH = N_KV_HEADS * HEAD_DIM
SPLITS = (ATTN_WIDTH, KV_WIDTH, KV_WIDTH, IDX_HEADS * IDX_DIM, IDX_DIM, IDX_HEADS, D_RNN, D_RNN, D_MODEL, D_MODEL)
N_IN = 5448


def rms_norm(x, g):
    x32 = x.astype(jnp.float32)
    y = x32 * lax.rsqrt(jnp.mean(x32 * x32, axis=-1, keepdims=True) + EPS)
    return (y * g.astype(jnp.float32)).astype(x.dtype)

def causal_dwconv(x, w, b):
    width = w.shape[0]
    seq = x.shape[1]
    xp = jnp.pad(x, ((0, 0), (width - 1, 0), (0, 0)))
    y = xp[:, 0:seq] * w[0]
    for k in range(1, width):
        y = y + xp[:, k:k + seq] * w[k]
    return y + b

def t5_bucket(rel):
    max_exact = N_BUCKETS // 2
    n = jnp.maximum(rel, 0)
    nf = jnp.maximum(n, 1).astype(jnp.float32)
    large = max_exact + (jnp.log(nf / max_exact) / math.log(MAX_DISTANCE / max_exact)
                         * (N_BUCKETS - max_exact)).astype(jnp.int32)
    large = jnp.minimum(large, N_BUCKETS - 1)
    return jnp.where(n < max_exact, n, large)

def dsa_attention(q, k, v, q_idx, k_idx, w_idx, rel_bias):
    B, S = q.shape[0], q.shape[1]
    n_sel = min(TOPK_MAX, S // 4)
    nb = S // Q_BLOCK
    G = N_HEADS // N_KV_HEADS
    pos = jnp.arange(S, dtype=jnp.int32)
    gather = jax.vmap(lambda t_b, i_b: t_b[i_b])

    def to_blocks(t):
        return jnp.moveaxis(t.reshape((B, nb, Q_BLOCK) + t.shape[2:]), 1, 0)

    def block(args):
        qb, qib, wb, tb = args
        dots = jnp.einsum('bqhd,bsd->bqhs', qib, k_idx).astype(jnp.float32) * (IDX_DIM ** -0.5)
        score = jnp.einsum('bqh,bqhs->bqs', wb.astype(jnp.float32) * (IDX_HEADS ** -0.5), jax.nn.relu(dots))
        causal = pos[None, :] <= tb[:, None]
        score = jnp.where(causal[None], score, -jnp.inf)
        _, sel = lax.top_k(score, n_sel)
        valid = sel <= tb[None, :, None]
        ks = gather(k, sel)
        vs = gather(v, sel)
        qg = qb.reshape(B, Q_BLOCK, N_KV_HEADS, G, HEAD_DIM)
        logits = jnp.einsum('bqhgd,bqnhd->bqhgn', qg, ks).astype(jnp.float32) * (HEAD_DIM ** -0.5)
        bucket = t5_bucket(tb[None, :, None] - sel)
        bias = rel_bias[bucket].astype(jnp.float32)
        bias = bias.reshape(B, Q_BLOCK, n_sel, N_KV_HEADS, G).transpose(0, 1, 3, 4, 2)
        logits = jnp.where(valid[:, :, None, None, :], logits + bias, -jnp.inf)
        p = jax.nn.softmax(logits, axis=-1).astype(vs.dtype)
        o = jnp.einsum('bqhgn,bqnhd->bqhgd', p, vs)
        return o.reshape(B, Q_BLOCK, N_HEADS * HEAD_DIM)

    out = lax.map(block, (to_blocks(q), to_blocks(q_idx), to_blocks(w_idx), pos.reshape(nb, Q_BLOCK)))
    return jnp.moveaxis(out, 0, 1).reshape(B, S, N_HEADS * HEAD_DIM)

def rg_lru(x, w_rg, b_rg, w_ig, b_ig, lam):
    B, S = x.shape[0], x.shape[1]
    xb = x.reshape(B, S, N_RNN_BLOCKS, RNN_BLOCK)
    r = jax.nn.sigmoid(jnp.einsum('bsnc,ncd->bsnd', xb, w_rg).reshape(B, S, D_RNN) + b_rg)
    i = jax.nn.sigmoid(jnp.einsum('bsnc,ncd->bsnd', xb, w_ig).reshape(B, S, D_RNN) + b_ig)
    log_a = -LRU_C * r.astype(jnp.float32) * jax.nn.softplus(-lam.astype(jnp.float32))
    a = jnp.exp(log_a)
    mult = jnp.sqrt(-jnp.expm1(2.0 * log_a))
    u = x.astype(jnp.float32) * i.astype(jnp.float32) * mult

    def combine(left, right):
        a1, b1 = left
        a2, b2 = right
        return a1 * a2, a2 * b1 + b2

    _, h = lax.associative_scan(combine, (a, u), axis=1)
    return h.astype(x.dtype)

def second_inputs(seed: int = 0) -> dict:
    key = jax.random.key(seed)
    ks = jax.random.split(key, 32)
    f32 = jnp.float32

    def nrm(k, shape, scale):
        return jax.random.normal(k, shape, f32) * scale

    L = DEPTH_2
    a0 = jax.random.uniform(ks[13], (L, D_RNN), f32, 0.9, 0.999)
    p = a0 ** (1.0 / LRU_C)
    lam = jnp.log(p) - jnp.log1p(-p)
    return {
        "x": nrm(ks[0], (BATCH, SEQ, D_MODEL), 1.0),
        "c": nrm(ks[1], (BATCH, D_MODEL), 1.0),
        "w_ada": nrm(ks[2], (L, D_MODEL, 6 * D_MODEL), D_MODEL ** -0.5),
        "b_ada": nrm(ks[3], (L, 6 * D_MODEL), 0.02),
        "g_mix": 1.0 + nrm(ks[4], (L, D_MODEL), 0.02),
        "w_in": nrm(ks[5], (L, D_MODEL, N_IN), D_MODEL ** -0.5),
        "b_in": nrm(ks[6], (L, N_IN), 0.01),
        "rel_bias": nrm(ks[7], (N_BUCKETS, N_HEADS), 0.5),
        "conv_rnn_w": nrm(ks[8], (L, RNN_CONV, D_RNN), RNN_CONV ** -0.5),
        "conv_rnn_b": nrm(ks[9], (L, D_RNN), 0.01),
        "w_rg": nrm(ks[10], (L, N_RNN_BLOCKS, RNN_BLOCK, RNN_BLOCK), RNN_BLOCK ** -0.5),
        "b_rg": nrm(ks[11], (L, D_RNN), 0.01),
        "w_ig": nrm(ks[12], (L, N_RNN_BLOCKS, RNN_BLOCK, RNN_BLOCK), RNN_BLOCK ** -0.5),
        "b_ig": nrm(ks[14], (L, D_RNN), 0.01),
        "lru_lambda": lam,
        "w_o_attn": nrm(ks[15], (L, ATTN_WIDTH, D_MODEL), ATTN_WIDTH ** -0.5),
        "w_o_rnn": nrm(ks[16], (L, D_RNN, D_MODEL), D_RNN ** -0.5),
        "w_out": nrm(ks[17], (L, D_MODEL, D_MODEL), D_MODEL ** -0.5),
        "g_ffn": 1.0 + nrm(ks[18], (L, D_MODEL), 0.02),
        "w_up": nrm(ks[19], (L, D_MODEL, 2 * D_FF_2), D_MODEL ** -0.5),
        "conv_ffn_w": nrm(ks[20], (L, FFN_CONV, 2 * D_FF_2), FFN_CONV ** -0.5),
        "conv_ffn_b": nrm(ks[21], (L, 2 * D_FF_2), 0.01),
        "w_down": nrm(ks[22], (L, D_FF_2, D_MODEL), D_FF_2 ** -0.5),
        "g_final": 1.0 + nrm(ks[23], (D_MODEL,), 0.02),
    }

def second_block(x, c, w_ada, b_ada, g_mix, w_in, b_in, rel_bias, conv_rnn_w, conv_rnn_b,
              w_rg, b_rg, w_ig, b_ig, lru_lambda, w_o_attn, w_o_rnn, w_out, g_ffn,
              w_up, conv_ffn_w, conv_ffn_b, w_down, g_final):
    B, S = x.shape[0], x.shape[1]
    cuts = []
    acc = 0
    for width in SPLITS[:-1]:
        acc += width
        cuts.append(acc)
    c_act = jax.nn.silu(c)
    h = x
    for l in range(DEPTH_2):
        mod = jnp.dot(c_act, w_ada[l]) + b_ada[l]
        sh1, sc1, ga1, sh2, sc2, ga2 = [m[:, None, :] for m in jnp.split(mod, 6, axis=-1)]

        xn = rms_norm(h, g_mix[l]) * (1.0 + sc1) + sh1
        proj = jnp.dot(xn, w_in[l]) + b_in[l]
        q, k, v, qi, ki, wi, xr, yr, gate_a, gate_b = jnp.split(proj, cuts, axis=-1)

        attn = dsa_attention(
            q.reshape(B, S, N_HEADS, HEAD_DIM),
            k.reshape(B, S, N_KV_HEADS, HEAD_DIM),
            v.reshape(B, S, N_KV_HEADS, HEAD_DIM),
            qi.reshape(B, S, IDX_HEADS, IDX_DIM), ki, wi, rel_bias)

        xr = causal_dwconv(xr, conv_rnn_w[l], conv_rnn_b[l])
        rnn = rg_lru(xr, w_rg[l], b_rg[l], w_ig[l], b_ig[l], lru_lambda[l]) * jax.nn.gelu(yr)

        merged = (jax.nn.sigmoid(gate_a) * jnp.dot(attn, w_o_attn[l])
                  + jax.nn.sigmoid(gate_b) * jnp.dot(rnn, w_o_rnn[l]))
        h = h + ga1 * jnp.dot(merged, w_out[l])

        xn = rms_norm(h, g_ffn[l]) * (1.0 + sc2) + sh2
        up = causal_dwconv(jnp.dot(xn, w_up[l]), conv_ffn_w[l], conv_ffn_b[l])
        val, gte = jnp.split(up, 2, axis=-1)
        h = h + ga2 * jnp.dot(jax.nn.silu(gte) * val, w_down[l])
    return rms_norm(h, g_final)


def setup_inputs(seed=0):
    out = dict(first_inputs(seed))
    for name, value in second_inputs(seed + 1).items():
        if name != "x":
            out[name + "_2"] = value
    return out


def reference(
    x, mem, norm_mix, norm_ffn, norm_mem, norm_final, w_in_a, sink_a, w_in_b, rpb_b, w_mem_kv,
    w_out, w_gate_up, w_down, c_2, w_ada_2, b_ada_2, g_mix_2, w_in_2, b_in_2, rel_bias_2,
    conv_rnn_w_2, conv_rnn_b_2, w_rg_2, b_rg_2, w_ig_2, b_ig_2, lru_lambda_2, w_o_attn_2,
    w_o_rnn_2, w_out_2, g_ffn_2, w_up_2, conv_ffn_w_2, conv_ffn_b_2, w_down_2, g_final_2,
):
    x = first_block(
        x, mem, norm_mix, norm_ffn, norm_mem, norm_final, w_in_a, sink_a, w_in_b, rpb_b,
        w_mem_kv, w_out, w_gate_up, w_down,
    )
    return second_block(
        x, c_2, w_ada_2, b_ada_2, g_mix_2, w_in_2, b_in_2, rel_bias_2, conv_rnn_w_2,
        conv_rnn_b_2, w_rg_2, b_rg_2, w_ig_2, b_ig_2, lru_lambda_2, w_o_attn_2, w_o_rnn_2,
        w_out_2, g_ffn_2, w_up_2, conv_ffn_w_2, conv_ffn_b_2, w_down_2, g_final_2,
    )


_drawn_inputs = setup_inputs


def setup_inputs(seed=0):
    import zlib

    import numpy as np

    out = dict(_drawn_inputs(seed))
    spreads = {}
    factors = {'norm_mix': 3.747,
     'norm_mem': 8.0,
     'sink_a': 23.712,
     'g_mix_2': 3.053,
     'b_in_2': 4.028,
     'conv_rnn_b_2': 5.561,
     'b_rg_2': 37.489,
     'b_ig_2': 24.359,
     'g_ffn_2': 4.333,
     'conv_ffn_b_2': 22.107,
     'g_final_2': 7.959}
    for name, (base, spread) in spreads.items():
        noise = np.random.default_rng([zlib.crc32(name.encode()), seed]).standard_normal(out[name].shape)
        drawn = base * np.exp(spread * noise) if base else spread * noise
        out[name] = __import__('jax').numpy.asarray(drawn.astype(out[name].dtype))
    for name, factor in factors.items():
        out[name] = (out[name] * factor).astype(out[name].dtype)
    return out
```

```python
from contextlib import ExitStack

import numpy as np

import concourse.bass as bass
from concourse import mybir

F = mybir.dt.float32
R = mybir.dt.float32r
ALU = mybir.AluOpType
ACT = mybir.ActivationFunctionType
AX = mybir.AxisListType.X

D = 1024
DFF = 2816
EPS = 1e-6
BIG = 1e30
TAKEN = -3e38
RAWS, SPLITS = 4, 3


class Engine:

    def __init__(self, sem):
        self.sem, self.n, self.program, self.seen = sem, 0, [], {}

    def wait(self, *tokens):
        for t in tokens:
            if t is None:
                continue
            if isinstance(t, list):
                self.wait(*t)
                continue
            sem, value = t
            if self.seen.get(sem.name, 0) < value:
                self.seen[sem.name] = value
                self.program.append(lambda e, s=sem, v=value: e.wait_ge(s, v))

    def quiet(self, fn, *after):
        self.wait(*after)
        self.program.append(fn)

    def do(self, fn, *after):
        self.wait(*after)
        self.n += 1
        self.program.append(lambda e, f=fn, s=self.sem: f(e).then_inc(s, 1))
        return self.sem, self.n

    def now(self):
        return self.sem, self.n


class Landing:

    def __init__(self, sem):
        self.sem, self.n = sem, 0

    def load(self, queue, out, src, *after):
        queue.wait(*after)
        self.n += 16
        queue.program.append(lambda e, o=out, i=src, s=self.sem: e.dma_start(o, i).then_inc(s, 16))
        return self.sem, self.n


class Ring:

    def __init__(self, items):
        self.items, self.free, self.at = items, [[] for _ in items], -1

    def take(self):
        self.at = (self.at + 1) % len(self.items)
        after, self.free[self.at] = self.free[self.at], []
        return self.at, self.items[self.at], after

    def give(self, slot, *tokens):
        self.free[slot] += list(tokens)


def weight_parts(w, k0, nk, c0, nc_):
    return w[k0 * 128:(k0 + nk) * 128, c0:c0 + nc_].rearrange("(k p) n -> p k n", p=128)


def columns(w, c0, width):
    nk = w.shape[0] // 128
    step = min(nk, 2048 // width)
    return [(weight_parts(w, k, min(step, nk - k), c0, width), k, min(step, nk - k), width) for k in range(0, nk, step)]


def tiles_of(n):
    return [(c, min(512, n - c)) for c in range(0, n, 512)]


def build(nc, a, out):
    ctx = ExitStack()
    with ctx:
        def sb(name, shape, dt=F, scope=ctx):
            return scope.enter_context(nc.sbuf_tensor(name, shape, dt))

        def sem(name):
            return ctx.enter_context(nc.semaphore(name))

        pe, act, dve, pool, sp = (Engine(sem(n)) for n in ("s_pe", "s_act", "s_dve", "s_pool", "s_sp"))
        banks = [ctx.enter_context(nc.psum_tensor(f"bank{i}", [128, 512], F)) for i in range(8)]

        raw = [sb(f"raw{i}", [128, 2048]) for i in range(RAWS)]
        hi_s = [sb(f"hi{i}", [128, 2048], R) for i in range(SPLITS)]
        lo_s = [sb(f"lo{i}", [128, 2048], R) for i in range(SPLITS)]
        xres = sb("xres", [128, 2, D])
        nrm = sb("nrm", [128, 2, D])
        xTh = sb("xTh", [128, 8, 256], R)
        xTl = sb("xTl", [128, 8, 256], R)
        const = sb("const", [128, 1408])
        ident = const[:, 0:128]
        dist = const[:, 128:640].rearrange("p (t k) -> p t k", t=2)
        window = const[:, 640:896]
        causal = const[:, 896:1408].rearrange("p (t k) -> p t k", t=2)
        big = sb("big", [128, 6144])
        gbc = sb("gbc", [128, D])
        rows = sb("rows", [128, 3, 128])
        cols = sb("cols", [128, 128 + 176])
        small = sb("small", [128, 256])
        ones = sb("ones", [128, 128])
        stats = [sb(f"stat{i}", [128, 16]) for i in range(4)]

        first, rowsem, consem, side = (Landing(sem(n)) for n in ("d_x", "d_rows", "d_const", "d_side"))
        rpbsem, relsem, bsem, gsem, scrsem, outsem = (Landing(sem(n)) for n in ("d_rpb", "d_rel", "d_b", "d_g", "d_scr", "d_out"))

        plan = []
        for l in range(2):
            plan += [("mem", x) for x in columns(a["w_mem_kv"][l], 0, 512)]

        def plan_block(w_in, n_in, l):
            p = []
            for c, w in tiles_of(n_in):
                p += [("in", x) for x in columns(w_in, c, w)]
            for c in (0, 512):
                p += [("out", x) for x in columns(a["w_out"][l], c, 512)]
            for c, w in tiles_of(DFF):
                p += [("gu", x) for x in columns(a["w_gate_up"][l], c, w)]
                p += [("gu", x) for x in columns(a["w_gate_up"][l], DFF + c, w)]
            p += [("down", (weight_parts(a["w_down"][l], k, 2, 0, 1024), k, 2, 1024)) for k in range(0, 22, 2)]
            return p

        plan += plan_block(a["w_in_a"][0], 1536, 0)
        second = plan_block(a["w_in_b"][0], 2560, 1)
        w_ada = a["w_ada_2"][0]
        ada = [("ada", (w_ada[k * 128:(k + 1) * 128, c * 2048:(c + 1) * 2048], k, c, 2048)) for k in range(8) for c in range(3)]
        n_gu = next(i for i, p in enumerate(second) if p[0] == "gu")
        mixed = second[:n_gu]
        for i, p in enumerate(second[n_gu:]):
            mixed.append(p)
            if i % 1 == 0 and ada and i >= 1:
                mixed.append(ada.pop(0))
        plan += mixed
        assert not ada
        w_in2 = a["w_in_2"][0]
        IN2 = [("xr", 1352, 512), ("yr", 2376, 512), ("xr", 1864, 512), ("yr", 2888, 512), ("qi", 768, 512), ("kw", 1280, 72),
               ("q", 0, 512), ("kv", 512, 256), ("ga", 3400, 512), ("ga", 3912, 512), ("gb", 4424, 512), ("gb", 4936, 512)]
        for _, c, w in IN2:
            plan += [("in2", x) for x in columns(w_in2, c, w)]
        for c in (0, 512):
            plan += [("orn", x) for x in columns(a["w_o_rnn_2"][0], c, 512)]
        for c in (0, 512):
            plan += [("oat", x) for x in columns(a["w_o_attn_2"][0], c, 512)]
        for c in (0, 512):
            plan += [("out2", x) for x in columns(a["w_out_2"][0], c, 512)]
        for c, w in tiles_of(DFF):
            plan += [("up2", x) for x in columns(a["w_up_2"][0], DFF + c, w)]
            plan += [("up2", x) for x in columns(a["w_up_2"][0], c, w)]
        plan += [("down2", (weight_parts(a["w_down_2"][0], k, 2, 0, 1024), k, 2, 1024)) for k in range(0, 22, 2)]

        slots = [Landing(sem(f"d_raw{i}")) for i in range(RAWS)]
        landed, raw_free, ready, released = {}, {}, {}, {}
        state = {"dma": 0, "split": 0, "use": 0}
        index = {}
        for i, p in enumerate(plan):
            if p[0] != "ada":
                index[i] = len(index)
        order = sorted(index)
        acc_tok = {"t": [None, None, None], "c": None}

        def issue(upto):
            while state["dma"] < min(upto, len(plan)):
                i = state["dma"]
                kind, (src, k0, nk, w) = plan[i]
                n = 2048 if kind == "ada" else nk * w
                dst = raw[i % RAWS][:, 0:n]
                if kind != "ada":
                    dst = dst.rearrange("p (k n) -> p k n", k=nk)
                landed[i] = slots[i % RAWS].load(sp, dst, src, raw_free.get(i - RAWS))
                state["dma"] += 1

        def split(i):
            kind, (_, k0, nk, w) = plan[i]
            if kind == "ada":
                c = nk
                acc = big[:, c * 2048:(c + 1) * 2048]
                t = dve.do(lambda e: e.scalar_tensor_tensor(out=acc, in0=raw[i % RAWS][:, :], scalar=small[:, k0:k0 + 1], in1=acc,
                                                            op0=ALU.mult, op1=ALU.add), landed[i], acc_tok["t"][c], acc_tok["c"])
                acc_tok["t"][c] = t
                raw_free[i] = [t]
                return
            m = index[i]
            s, n = m % SPLITS, nk * w
            src, h, lo = raw[i % RAWS][:, 0:n], hi_s[s][:, 0:n], lo_s[s][:, 0:n]
            before = released.get(m - SPLITS)
            th = act.do(lambda e: e.activation(h, src, ACT.Copy), landed[i], before)
            tl = dve.do(lambda e: e.tensor_tensor(lo, src, h.bitcast(F), ALU.subtract), th, landed[i], before)
            raw_free[i] = [th, tl]
            ready[m] = [th, tl]

        def advance(m):
            upto = order[min(m + SPLITS - 1, len(order) - 1)]
            while state["split"] <= upto:
                issue(state["split"] + 1)
                split(state["split"])
                state["split"] += 1
                issue(state["split"] + RAWS)

        def part(kind):
            m = state["use"]
            state["use"] += 1
            advance(m)
            k, (_, k0, nk, w) = plan[order[m]]
            assert k == kind, (k, kind)
            s = m % SPLITS
            v = [x[s][:, 0:nk * w].rearrange("p (k n) -> p k n", k=nk) for x in (hi_s, lo_s)]
            return m, k0, nk, w, v[0], v[1]

        lin_banks = Ring([(banks[0], banks[1]), (banks[2], banks[3])])
        work = Ring(banks[4:8])

        def linear(kind, parts, xh, xl, after):
            slot, pair, free = lin_banks.take()
            for p in range(parts):
                m, k0, nk, w, h, lo = part(kind)
                pe.wait(ready[m], after, free)
                for k in range(nk):
                    for t in range(2):
                        o = pair[t][:, 0:w]
                        sh, sl = xh[:, k0 + k, t * 128:(t + 1) * 128], xl[:, k0 + k, t * 128:(t + 1) * 128]
                        begin, end = p == 0 and k == 0, p == parts - 1 and k == nk - 1
                        pe.quiet(lambda e, o=o, s=sh, x=h[:, k, :], b=begin: e.matmul(o, s, x, start=b, stop=False))
                        pe.quiet(lambda e, o=o, s=sh, x=lo[:, k, :]: e.matmul(o, s, x, start=False, stop=False))
                        f = lambda e, o=o, s=sl, x=h[:, k, :], d=end: e.matmul(o, s, x, start=False, stop=d)
                        if k == nk - 1 and t == 1:
                            done = pe.do(f)
                        else:
                            pe.quiet(f)
                released[m] = done
            return slot, pair, done

        def down(kind, xh, xl, after):
            s0, p0, f0 = lin_banks.take()
            s1, p1, f1 = lin_banks.take()
            pairs = (p0, p1)
            for p in range(11):
                m, k0, nk, w, h, lo = part(kind)
                pe.wait(ready[m], after, f0, f1)
                for k in range(nk):
                    for t in range(2):
                        sh, sl = xh[:, k0 + k, t * 128:(t + 1) * 128], xl[:, k0 + k, t * 128:(t + 1) * 128]
                        begin, end = p == 0 and k == 0, p == 10 and k == nk - 1
                        for j in range(2):
                            o, xhi, xlo = pairs[j][t][:, :], h[:, k, j * 512:(j + 1) * 512], lo[:, k, j * 512:(j + 1) * 512]
                            pe.quiet(lambda e, o=o, s=sh, x=xhi, b=begin: e.matmul(o, s, x, start=b, stop=False))
                            pe.quiet(lambda e, o=o, s=sh, x=xlo: e.matmul(o, s, x, start=False, stop=False))
                            f = lambda e, o=o, s=sl, x=xhi, d=end: e.matmul(o, s, x, start=False, stop=d)
                            if k == nk - 1 and t == 1 and j == 1:
                                done = pe.do(f)
                            else:
                                pe.quiet(f)
                released[m] = done
            return (s0, s1), pairs, done

        def turn_blocks(bank, blocks, *after):
            pe.wait(*after)
            for i, x in enumerate(blocks):
                f = lambda e, x=x, o=bank[:, i * 128:(i + 1) * 128]: e.transpose(o, x, ident)
                if i == len(blocks) - 1:
                    return pe.do(f)
                pe.quiet(f)

        def turn_split(src, c0, nk, dh, dl, k0, after, before, gain=None, shift=None, tmp=None):
            done, turned = [], None
            for k in range(0, nk, 2):
                n = min(2, nk - k)
                slot, bank, free = work.take()
                turned = turn_blocks(bank, [src[:, t, c0 + (k + j) * 128:c0 + (k + j + 1) * 128] for j in range(n) for t in range(2)],
                                     after, free, t_const)
                if gain is None:
                    o, lo, ps = dh[:, k0 + k:k0 + k + n, :], dl[:, k0 + k:k0 + k + n, :], bank[:, 0:n * 256].rearrange("p (k t) -> p k t", k=n)
                    th = act.do(lambda e, o=o, p=ps: e.activation(o, p, ACT.Copy), turned, before)
                    tl = dve.do(lambda e, o=lo, p=ps, h=o: e.tensor_tensor(o, p, h.bitcast(F), ALU.subtract), th, before)
                    work.give(slot, th, tl)
                    done = [th, tl]
                    continue
                last = []
                parts = [(dh[:, k0 + k + j, :], dl[:, k0 + k + j, :], bank[:, j * 256:(j + 1) * 256], gain[:, k + j:k + j + 1], k + j) for j in range(n)]
                if shift is None:
                    for o, lo, ps, g, _ in parts:
                        th = act.do(lambda e, o=o, p=ps, g=g: e.activation(o, p, ACT.Copy, scale=g), turned, before)
                    for o, lo, ps, g, _ in parts:
                        tl = dve.do(lambda e, o=lo, p=ps, g=g, h=o: e.scalar_tensor_tensor(
                            out=o, in0=p, scalar=g, in1=h.bitcast(F), op0=ALU.mult, op1=ALU.subtract), th, before)
                    last = [th, tl]
                else:
                    for o, lo, ps, g, kk in parts:
                        ts, tb, tf = tmp.take()
                        b = shift[:, kk:kk + 1]
                        t0 = dve.do(lambda e, o=tb, p=ps, g=g, b=b: e.tensor_scalar(o, p, g, b, ALU.mult, ALU.add), turned, tf)
                        th = act.do(lambda e, o=o, p=tb: e.activation(o, p, ACT.Copy), t0, before)
                        tl = dve.do(lambda e, o=lo, p=tb, h=o: e.tensor_tensor(o, p, h.bitcast(F), ALU.subtract), th, before)
                        tmp.give(ts, th, tl)
                        last = [th, tl]
                work.give(slot, *last)
                done = last
            return done, turned

        def inverse_rms(src, junk, after, before):
            st = stats[0]
            for t in range(2):
                sq = act.do(lambda e, t=t: e.activation(junk[:, t, :], src[:, t, :], ACT.Square, accum_out=st[:, t:t + 1]), after, before)
            ms = dve.do(lambda e: e.tensor_scalar(st[:, 2:4], st[:, 0:2], 1.0 / D, EPS, ALU.mult, ALU.add), sq)
            rs = pool.do(lambda e: e.tensor_tensor(st[:, 4:6], st[:, 2:4], st[:, 6:8], ALU.pow), ms, t_half)
            return st, rs, sq

        def norm_turned(src, after, before, gain, shift=None, tmp=None):
            st, rs, sq = inverse_rms(src, nrm, after, before)
            t0 = dve.do(lambda e: e.tensor_scalar(nrm[:, 0, :], src[:, 0, :], st[:, 4:5], None, ALU.mult), rs, sq)
            t1 = act.do(lambda e: e.activation(nrm[:, 1, :], src[:, 1, :], ACT.Copy, scale=st[:, 5:6]), rs, sq)
            return turn_split(nrm, 0, 8, xTh, xTl, 0, [t0, t1], before, gain, shift, tmp)

        memx = big[:, 0:2048].rearrange("p (t d) -> p t d", t=2)
        t_mem = first.load(sp, memx, a["mem"][0].rearrange("(t p) d -> p t d", p=128))
        r = 0
        for name in ("norm_mix", "norm_ffn", "norm_mem", "g_mix_2", "g_ffn_2", "c_2", "conv_rnn_w_2", "conv_rnn_b_2", "b_rg_2", "b_ig_2", "lru_lambda_2"):
            v = a[name]
            if len(v.shape) == 3:
                v = v.rearrange("l n d -> (l n) d")
            v = v.rearrange("l (k p) -> (l k) p", p=128) if len(v.shape) == 2 else v.rearrange("(k p) -> k p", p=128)
            t_rows = rowsem.load(pool, rows[r:r + v.shape[0], 0, :], v)
            r += v.shape[0]
        assert r == 128
        cw = a["conv_ffn_w_2"][0].rearrange("n (k p) -> (n k) p", p=128)
        t_rows = rowsem.load(pool, rows[0:88, 1, :], cw[0:88, :])
        t_rows = rowsem.load(pool, rows[0:44, 2, :], cw[88:132, :])
        t_rows = rowsem.load(pool, rows[44:88, 2, :], a["conv_ffn_b_2"][0].rearrange("(k p) -> k p", p=128))
        sink = small[:, 16:28]
        t_rows = rowsem.load(pool, sink, bass.AP(a["sink_a"].tensor, 0, [[0, 128], [1, 12]]))
        t_const = consem.load(sp, const[:, :], a["constants"])
        issue(RAWS)
        t_x = side.load(pool, xres[:, :, :], a["x"][0].rearrange("(t p) d -> p t d", p=128))
        t_half = pool.do(lambda e: e.memset(stats[0][:, 6:8], -0.5))
        t_ones = pool.do(lambda e: e.memset(ones[:, :], 1.0))

        slot, bank, free = work.take()
        tt = turn_blocks(bank, [rows[:, 0, :]], free, t_rows, t_const)
        for i in (1, 2):
            tt = pe.do(lambda e, b=bank, i=i: e.transpose(b[:, i * 128:i * 128 + 88], rows[0:88, i, :], ident[0:88, 0:88]))
        t_cols = dve.do(lambda e, b=bank: e.tensor_copy(cols[:, 0:128], b[:, 0:128]), tt)
        for i in (1, 2):
            t_cols = dve.do(lambda e, b=bank, i=i: e.tensor_copy(cols[:, 40 + 88 * i:128 + 88 * i], b[:, i * 128:i * 128 + 88]), tt)
        work.give(slot, t_cols)

        def col(i):
            return cols[:, 8 * i:8 * i + 8]

        CVW = lambda n, kt: cols[:, 128 + 44 * n + kt:129 + 44 * n + kt]
        CVB = lambda kt: cols[:, 260 + kt:261 + kt]

        def fence():
            return [e.now() for e in (pe, act, dve, pool)]

        def pairs_turned(src, n, dst, at, scale, after, before):
            for k in range(0, n, 2):
                m = min(2, n - k)
                slot, bank, free = work.take()
                tt = turn_blocks(bank, [src[:, t, (k + j) * 128:(k + j + 1) * 128] for j in range(m) for t in range(2)], after, free, t_const)
                t = act.do(lambda e, o=dst[:, at + k:at + k + m, :], p=bank[:, 0:m * 256].rearrange("p (k t) -> p k t", k=m):
                           e.activation(o, p, ACT.Copy, scale=scale), tt, before)
                work.give(slot, t)
            return t, tt

        def softmax_heads(jobs, s_ring, p_ring, y, before):
            so, po = {}, {}
            stat = Ring(stats[1:4])

            def scores(i):
                q, k, v, finish, sk, c, after = jobs[i]
                slot, bank, free = work.take()
                pe.wait(free, after)
                pe.quiet(lambda e: e.matmul(bank[:, 0:256], q[:, 0:128], k, start=True, stop=True))
                tok = pe.do(lambda e: e.matmul(bank[:, 256:512], q[:, 128:256], k, start=True, stop=True))
                so[i] = (slot, bank[:, :].rearrange("p (t k) -> p t k", t=2), tok)

            def soften(i):
                q, k, v, finish, sk, c, after = jobs[i]
                slot, ps, tok = so[i]
                ss, s, sf = s_ring.take()
                ts, st, tf = stat.take()
                if finish is None:
                    src, t, fin = ps, tok, None
                else:
                    t, fin = finish(s, ps, tok, sf)
                    src = s
                t = dve.do(lambda e: e.tensor_reduce(st[:, 0:2], src[:, :, :], AX, ALU.max), t, tf)
                if sk is None:
                    t = dve.do(lambda e: e.tensor_scalar(st[:, 2:4], st[:, 0:2], -1.0, None, ALU.mult), t)
                else:
                    t = dve.do(lambda e: e.tensor_scalar(st[:, 2:4], st[:, 0:2], sk, -1.0, ALU.max, ALU.mult), t, t_rows)
                for n in range(2):
                    te = act.do(lambda e, n=n: e.activation(s[:, n, :], src[:, n, :], ACT.Exp, bias=st[:, 2 + n:3 + n],
                                                            accum_out=st[:, 4 + n:5 + n]), t, sf)
                work.give(slot, te if fin is None else fin)
                den = st[:, 4:6]
                td = te
                if sk is not None:
                    tk = act.do(lambda e: e.activation(st[:, 6:8], st[:, 2:4], ACT.Exp, bias=sk), t)
                    td = dve.do(lambda e: e.tensor_tensor(st[:, 8:10], st[:, 4:6], st[:, 6:8], ALU.add), te, tk)
                    den = st[:, 8:10]
                tr = dve.do(lambda e, d=den: e.reciprocal(st[:, 10:12], d), td)
                so[i] = (ss, s, te, ts, st, tr)

            def turn(i):
                ss, s, te, ts, st, tr = so[i]
                slot, bank, free = work.take()
                tt = turn_blocks(bank, [s[:, n, kt * 128:(kt + 1) * 128] for kt in range(2) for n in range(2)], te, free)
                s_ring.give(ss, tt)
                ps, p, pf = p_ring.take()
                tp = act.do(lambda e: e.activation(p[:, :, :], bank[:, :].rearrange("p (k q) -> p k q", k=2), ACT.Copy), tt, pf)
                work.give(slot, tp)
                po[i] = (ps, p, tp)

            def values(i):
                q, k, v, finish, sk, c, after = jobs[i]
                ss, s, te, ts, st, tr = so[i]
                ps, p, tp = po[i]
                slot, bank, free = work.take()
                pe.wait(tp, free)
                for n in range(2):
                    for kt in range(2):
                        f = lambda e, n=n, kt=kt: e.matmul(bank[:, n * 64:(n + 1) * 64], p[:, kt, n * 128:(n + 1) * 128], v(kt),
                                                           start=(kt == 0), stop=(kt == 1))
                        if n == 1 and kt == 1:
                            tv = pe.do(f)
                        else:
                            pe.quiet(f)
                p_ring.give(ps, tv)
                ty = dve.do(lambda e: e.tensor_tensor(y[:, :, c:c + 64], bank[:, 0:128].rearrange("p (n d) -> p n d", n=2),
                                                      st[:, 10:12].unsqueeze(2).to_broadcast([128, 2, 64]), ALU.mult), tv, tr, before)
                work.give(slot, ty)
                stat.give(ts, ty)
                return ty

            n = len(jobs)
            for i in range(n + 3):
                if i < n:
                    scores(i)
                if 0 <= i - 1 < n:
                    soften(i - 1)
                if 0 <= i - 2 < n:
                    turn(i - 2)
                if 0 <= i - 3 < n:
                    ty = values(i - 3)
            return ty

        def half_of(x, h):
            return x[64 * (h % 2):64 * (h % 2) + 64, h // 2, :]

        scope = ExitStack()
        mstage = sb("mstage", [128, 2, 256], F, scope)
        mkT = sb("mkT", [128, 4, 256], F, scope)
        mv = sb("mv", [128, 2, 2, 256], F, scope)
        t_xT, t_turn = norm_turned(memx, [t_mem, t_cols], None, col(4))
        t_free_mem = fence()
        free_stage = None
        for l in range(2):
            slot, pair, done = linear("mem", 2, xTh, xTl, t_xT)
            ts = []
            for t in range(2):
                ts.append(act.do(lambda e, t=t, p=pair: e.activation(mstage[:, t, :], p[t][:, 0:256], ACT.Copy), done, free_stage))
                tvv = dve.do(lambda e, t=t, p=pair, l=l: e.tensor_copy(mv[:, l, t, :], p[t][:, 256:512]), ts[t])
            lin_banks.give(slot, *ts, tvv)
            t_mkT, free_stage = pairs_turned(mstage, 2, mkT, 2 * l, 1.0, ts, None)
        t_mv = tvv
        x_free = [done]

        bias = big[:, :].rearrange("p (h t k) -> p h t k", h=12, t=2)
        PITCH = 12 * 15 * 31
        t_rep = scrsem.load(pool, a["scratch_rpb"], bass.AP(a["rpb_b"].tensor, 0, [[0, 64], [1, PITCH]]))
        pool.wait(t_rep)
        for rr in range(4):
            for i in range(4):
                src = bass.AP(a["scratch_rpb"].tensor, (i - rr + 7) * 31 + 15, [[PITCH - 1, 64], [15 * 31, 12], [1, 64]])
                t_rpb = rpbsem.load(pool, bias[(rr % 2) * 64:(rr % 2) * 64 + 64, :, rr // 2, i * 64:(i + 1) * 64], src, t_free_mem)
        for h in range(12):
            for t in range(2):
                t_bias = pool.do(lambda e, h=h, t=t: e.tensor_tensor(bias[:, h, t, :], bias[:, h, t, :], window, ALU.add), t_rpb, t_const)

        def residual(pairs_slots, done, scale=None, tmp=None, tmp_free=None):
            toks = []
            for slot, pair, c in pairs_slots:
                last = []
                for t in range(2):
                    x = xres[:, t, c:c + 512]
                    if scale is None:
                        u = dve.do(lambda e, x=x, p=pair[t]: e.tensor_tensor(x, p[:, :], x, ALU.add), done, toks_x[0])
                    else:
                        m = dve.do(lambda e, p=pair[t], c=c, t=t: e.tensor_tensor(tmp[:, t, :], p[:, :], scale[:, c:c + 512], ALU.mult), done, tmp_free)
                        u = dve.do(lambda e, x=x, t=t: e.tensor_tensor(x, x, tmp[:, t, :], ALU.add), m)
                        tmp_free = u
                    last.append(u)
                lin_banks.give(slot, *last)
                toks += last
            return toks

        toks_x = [t_x]

        def mix(l, t_x, x_free):
            sc = ExitStack()
            t_f = fence()
            nh = 24 if l == 0 else 40
            proj = sb(f"proj{l}", [128, 2, 2, 512], F, sc)
            qT = sb(f"qT{l}", [128, 6, 256], F, sc)
            kT = sb(f"kT{l}", [128, 6, 256], F, sc)
            qmT = sb(f"qmT{l}", [128, 2, 256], F, sc)
            v = sb(f"v{l}", [128, 2, 768], F, sc)
            s_ring = Ring([sb(f"sr{l}{i}", [128, 2, 256], F, sc) for i in range(4)])
            p_ring = Ring([sb(f"pr{l}{i}", [128, 2, 256], F, sc) for i in range(2)])
            t_xT, t_turn = norm_turned(xres, t_x, x_free, col(l))
            stage = Ring([proj[:, 0, :, :], proj[:, 1, :, :]])
            toks = []

            def tile():
                slot, pair, done = linear("in", 2, xTh, xTl, t_xT)
                ss, s, sf = stage.take()
                return slot, pair, done, ss, s, sf

            def keep(pair, done, s, c0, c1, sf, d0=0):
                t0 = act.do(lambda e: e.activation(s[:, 0, d0:d0 + c1 - c0], pair[0][:, c0:c1], ACT.Copy), done, sf, t_f)
                t1 = dve.do(lambda e: e.tensor_copy(s[:, 1, d0:d0 + c1 - c0], pair[1][:, c0:c1]), done, sf, t_f)
                return [t0, t1]

            slot, pair, done, ss, s, sf = tile()
            tk = keep(pair, done, s, 0, 512, sf)
            lin_banks.give(slot, *tk)
            tq, tt = pairs_turned(s, 4, qT, 0, 0.125, tk, t_f)
            stage.give(ss, tt)
            slot, pair, done, ss, s, sf = tile()
            tk = keep(pair, done, s, 0, 512, sf)
            if l == 0:
                tq, tt = pairs_turned(s, 2, qT, 4, 0.125, tk, t_f)
                kd = big_k = sb("kdup", [128, 2, 512], F, sc)
                td = []
                for t in range(2):
                    for u in range(2):
                        td.append(pool.do(lambda e, t=t, u=u, s=s: e.tensor_copy(
                            kd[:, t, :].rearrange("p (h u d) -> p h u d", h=4, u=2)[:, :, u, :],
                            s[:, t, 256:512].rearrange("p (h d) -> p h d", h=4)), tk, t_f))
                lin_banks.give(slot, *tk)
                tkT, tt2 = pairs_turned(kd, 4, kT, 0, 1.0, td, t_f)
                stage.give(ss, tt, *td)
            else:
                lin_banks.give(slot, *tk)
                tq, tt = pairs_turned(s, 2, qT, 4, 0.125, tk, t_f)
                tkT, tt = pairs_turned(s[:, :, 256:512], 2, kT, 0, 1.0, tk, t_f)
                stage.give(ss, tt)
                slot, pair, done, ss, s, sf = tile()
                tk = keep(pair, done, s, 0, 512, sf)
                lin_banks.give(slot, *tk)
                tkT, tt = pairs_turned(s, 4, kT, 2, 1.0, tk, t_f)
                stage.give(ss, tt)
                slot, pair, done, ss, s, sf = tile()
                tv = keep(pair, done, v, 0, 512, None, 0)
                lin_banks.give(slot, *tv)
                stage.give(ss)
            slot, pair, done, ss, s, sf = tile()
            tv2 = keep(pair, done, v, 0, 256, None, 0 if l == 0 else 512)
            tk = keep(pair, done, s, 256, 512, sf)
            lin_banks.give(slot, *tk, *tv2)
            tqm, tt = pairs_turned(s, 2, qmT, 0, 0.125, tk, t_f)
            x_done = done
            jobs = []
            slopes = [2.0 ** (-8.0 * (h + 1) / 12) for h in range(12)]
            for h in range(4):
                jobs.append((half_of(qmT, h), half_of(mkT[:, 2 * l:2 * l + 2, :], h),
                             lambda kt, h=h: mv[:, l, kt, h * 64:(h + 1) * 64], None, None, 768 + 64 * h, [tqm, t_mkT, t_mv]))
            for h in range(12):
                if l == 0:
                    def finish(s, ps, tok, sf, h=h):
                        t = dve.do(lambda e: e.scalar_tensor_tensor(out=s[:, :, :], in0=dist, scalar=-slopes[h], in1=ps, op0=ALU.mult, op1=ALU.add),
                                   tok, sf, t_f, t_const)
                        return t, t
                    kv = h // 3
                    jobs.append((half_of(qT, h), kT[64 * (h % 2):64 * (h % 2) + 64, kv, :],
                                 lambda kt, kv=kv: v[:, kt, kv * 64:(kv + 1) * 64], finish, sink[:, h:h + 1], 64 * h, [tq, tkT, *tv2]))
                else:
                    def finish(s, ps, tok, sf, h=h):
                        t = dve.do(lambda e: e.tensor_tensor(s[:, :, :], ps, bias[:, h, :, :], ALU.add), tok, sf, t_f, t_bias)
                        return t, t
                    jobs.append((half_of(qT, h), half_of(kT, h), lambda kt, h=h: v[:, kt, h * 64:(h + 1) * 64], finish, None, 64 * h,
                                 [tq, tkT, *tv, *tv2]))
            ty = softmax_heads(jobs, s_ring, p_ring, nrm, t_turn)
            t_yT, t_turn2 = turn_split(nrm, 0, 8, xTh, xTl, 0, ty, x_done)
            res = []
            for c in (0, 512):
                slot, pair, done = linear("out", 2, xTh, xTl, t_yT)
                res += residual([(slot, pair, c)], done)
            sc.close()
            return res, [done, t_turn2]

        def ffn(l, t_x, x_free):
            sc = ExitStack()
            t_f = fence()
            hTh = sb(f"hTh{l}", [128, 22, 256], R, sc)
            hTl = sb(f"hTl{l}", [128, 22, 256], R, sc)
            t_xT, t_turn = norm_turned(xres, t_x, x_free, col(2 + l))
            pending = None
            free_h, free_s = [t_turn], [t_turn]
            t_hT = []
            for c, w in tiles_of(DFF):
                parts = 2 if w == 512 else 1
                slot, pair, done = linear("gu", parts, xTh, xTl, t_xT)
                tg = []
                for t in range(2):
                    tg.append(act.do(lambda e, t=t, p=pair, w=w: e.activation(nrm[:, t, 0:w], p[t][:, 0:w], ACT.Silu), done, free_s))
                lin_banks.give(slot, *tg)
                if pending:
                    t_hT, tt = turn_split(nrm, 512, pending[1] // 128, hTh, hTl, pending[0] // 128, pending[2], t_f)
                    free_h = [tt]
                slot, pair, done = linear("gu", parts, xTh, xTl, t_xT)
                tm = []
                for t in range(2):
                    tm.append(dve.do(lambda e, t=t, p=pair, w=w: e.tensor_tensor(nrm[:, t, 512:512 + w], p[t][:, 0:w], nrm[:, t, 0:w], ALU.mult),
                                     done, tg, free_h))
                lin_banks.give(slot, *tm)
                free_s = tm
                pending = (c, w, tm)
            x_done = done
            t_hT, tt = turn_split(nrm, 512, pending[1] // 128, hTh, hTl, pending[0] // 128, pending[2], t_f)
            (s0, s1), pairs, done = down("down", hTh, hTl, t_hT)
            res = residual([(s0, pairs[0], 0), (s1, pairs[1], 512)], done)
            sc.close()
            return res, [x_done, tt]

        t_r, x_free = mix(0, [t_x, t_cols], x_free + [t_turn])
        t_r, x_free = ffn(0, t_r, x_free)
        t_r, x_free = mix(1, t_r, x_free)
        scope.close()
        t_f = fence()
        t0 = act.do(lambda e: e.activation(small[:, 0:8], col(7), ACT.Silu), t_cols)
        tz = pool.do(lambda e: e.memset(big[:, :], 0.0), t_f)
        t_b = gsem.load(pool, big[0:1, :], a["b_ada_2"], tz)
        acc_tok["c"] = [t0, tz, t_b]
        t_g1 = side.load(pool, gbc[:, :], bass.AP(a["norm_final"].tensor, 0, [[0, 128], [1, D]]))
        t_r, x_free = ffn(1, t_r, x_free)
        t_acc = [t for t in acc_tok["t"]]

        st, rs, sq = inverse_rms(xres, nrm, t_r, x_free)
        t_x1 = []
        for t in range(2):
            t_x1.append(dve.do(lambda e, t=t: e.scalar_tensor_tensor(out=xres[:, t, :], in0=xres[:, t, :], scalar=st[:, 4 + t:5 + t], in1=gbc[:, :],
                                                                     op0=ALU.mult, op1=ALU.mult), rs, sq, t_g1))

        slot, bank, free = work.take()
        pe.wait(free, t_acc, t_ones)
        for n, base in enumerate((0, 1024, 3072, 4096)):
            for k in range(8):
                f = lambda e, n=n, k=k, b=base, bank=bank: e.matmul(bank[:, n * 8 + k:n * 8 + k + 1], big[:, b + k * 128:b + (k + 1) * 128],
                                                                    ones[:, 0:1], start=True, stop=True)
                tc = pe.do(f)
        mod = small[:, 32:64]
        t_mod = dve.do(lambda e, b=bank: e.tensor_copy(mod, b[:, 0:32]), tc)
        work.give(slot, t_mod)
        gb = []
        for n, base in enumerate((2048, 2560, 5120, 5632)):
            slot, bank, free = work.take()
            tc = pe.do(lambda e, b=base, bank=bank: e.matmul(bank[:, :], ones[:, :], big[:, b:b + 512], start=True, stop=True), free, t_acc)
            gb.append((slot, bank, tc))
        gates = big[:, 0:2048]
        t_gate = []
        for n, (slot, bank, tc) in enumerate(gb):
            t_gate.append(act.do(lambda e, n=n, b=bank: e.activation(gates[:, n * 512:(n + 1) * 512], b[:, :], ACT.Copy), tc, gb[-1][2]))
            work.give(slot, t_gate[-1])
        gain1, gain2 = small[:, 64:72], small[:, 72:80]
        tg1 = dve.do(lambda e: e.scalar_tensor_tensor(out=gain1, in0=mod[:, 8:16], scalar=1.0, in1=col(5), op0=ALU.add, op1=ALU.mult), t_mod)
        tg2 = dve.do(lambda e: e.scalar_tensor_tensor(out=gain2, in0=mod[:, 24:32], scalar=1.0, in1=col(6), op0=ALU.add, op1=ALU.mult), t_mod)

        lam = col(15)
        sp_ = [small[:, 96 + 8 * i:104 + 8 * i] for i in range(6)]
        t = dve.do(lambda e: e.scalar_tensor_tensor(out=sp_[0], in0=lam, scalar=-1.0, in1=lam, op0=ALU.mult, op1=ALU.min), t_cols)
        t = act.do(lambda e: e.activation(sp_[1], sp_[0], ACT.Exp), t)
        t = dve.do(lambda e: e.tensor_scalar(sp_[2], sp_[1], 2.0, None, ALU.add), t)
        t = dve.do(lambda e: e.reciprocal(sp_[3], sp_[2]), t)
        t = dve.do(lambda e: e.tensor_tensor(sp_[1], sp_[1], sp_[3], ALU.mult), t)
        t = dve.do(lambda e: e.tensor_tensor(sp_[2], sp_[1], sp_[1], ALU.mult), t)
        t = dve.do(lambda e: e.tensor_scalar(sp_[3], sp_[2], 1.0 / 17, 1.0 / 15, ALU.mult, ALU.add), t)
        for n in (13, 11, 9, 7, 5, 3, 1):
            t = dve.do(lambda e: e.tensor_tensor(sp_[3], sp_[3], sp_[2], ALU.mult), t)
            t = dve.do(lambda e, n=n: e.tensor_scalar(sp_[3], sp_[3], 1.0 / n, None, ALU.add), t)
        t = dve.do(lambda e: e.tensor_tensor(sp_[3], sp_[3], sp_[1], ALU.mult), t)
        t = dve.do(lambda e: e.tensor_scalar(sp_[4], lam, -1.0, 0.0, ALU.mult, ALU.max), t)
        t = dve.do(lambda e: e.scalar_tensor_tensor(out=sp_[5], in0=sp_[3], scalar=2.0, in1=sp_[4], op0=ALU.mult, op1=ALU.add), t)
        t_sp = dve.do(lambda e: e.tensor_scalar(sp_[5], sp_[5], -4.0, None, ALU.mult), t)
        halfrate = sp_[5]
        nbr, nbi = small[:, 144:152], small[:, 152:160]
        dve.do(lambda e: e.tensor_scalar(nbr, col(13), -1.0, None, ALU.mult))
        t_nb = dve.do(lambda e: e.tensor_scalar(nbi, col(14), -1.0, None, ALU.mult))

        sc = ExitStack()
        t_f = fence()
        rTh = sb("rTh", [128, 8, 256], R, sc)
        rTl = sb("rTl", [128, 8, 256], R, sc)
        inner = ExitStack()
        acc = sb("acc", [128, 2, 256], F, inner)
        left = sb("left", [128, 2, 256], F, inner)
        p2 = [sb(f"p2r{i}", [128, 2, 256], F, inner) for i in range(2)]
        sgb = sb("sgb", [128, 2, D], F, inner)
        tmp_ring = Ring([p2[i // 2][:, i % 2, :] for i in range(4)])
        st, rs, sq = inverse_rms(xres, nrm, t_x1, [x_free, sq])
        t0 = dve.do(lambda e: e.tensor_scalar(nrm[:, 0, :], xres[:, 0, :], st[:, 4:5], None, ALU.mult), rs, sq)
        t1 = act.do(lambda e: e.activation(nrm[:, 1, :], xres[:, 1, :], ACT.Copy, scale=st[:, 5:6]), rs, sq)
        t_xT, t_turn = turn_split(nrm, 0, 8, xTh, xTl, 0, [t0, t1], [x_free, t_f, tg1, t_mod], gain1, mod[:, 0:8], tmp_ring)
        t_xT_in = t_xT

        onehot = acc[0:32, :, :].rearrange("p t k -> p (t k)")
        rel = sb("rel", [32, 8], F, inner)
        relrow = left[0:8, :, :].rearrange("p t k -> p (t k)")
        t_rel = relsem.load(pool, rel[:, :], a["rel_bias_2"], t_f)
        t_rel = relsem.load(pool, onehot, a["onehot"], t_f)
        slot, bank, free = work.take()
        tb = pe.do(lambda e, b=bank: e.matmul(b[0:8, :], rel[:, :], onehot, start=True, stop=True), free, t_rel)
        tb = dve.do(lambda e, b=bank: e.tensor_copy(relrow, b[0:8, :]), tb, t_f)
        work.give(slot, tb)
        t_scr = scrsem.load(pool, bass.AP(a["scratch"].tensor, 0, [[512, 8], [4096, 128], [1, 512]]),
                            relrow.unsqueeze(1).to_broadcast([8, 128, 512]), tb)

        wrg = sgb[:, :, :].rearrange("p g (n d) -> p g n d", n=8)
        t_wg = gsem.load(pool, wrg[:, 0, :, :], a["w_rg_2"][0].rearrange("n c d -> c n d"), t_f)
        t_wg = gsem.load(pool, wrg[:, 1, :, :], a["w_ig_2"][0].rearrange("n c d -> c n d"), t_f)
        brings = Ring([(gbc[:, i * 512:(i + 1) * 512], Landing(sem(f"d_brow{i}"))) for i in range(2)])
        stage = Ring([sb(f"stage{i}", [128, 2, 512], F, inner) for i in range(2)])
        wi = sb("wi", [128, 2, 8], F, inner)
        temps = [big[:, 2048 + 1024 * i:3072 + 1024 * i].rearrange("p (k t) -> p k t", k=4) for i in range(4)]
        xc, rg, ig, gl = temps
        todo = list(IN2)
        t_big = [tc, t_gate]

        def bias_row(c, w):
            bs, (br, land), bf = brings.take()
            t = land.load(pool, br[:, 0:w], bass.AP(a["b_in_2"].tensor, c, [[0, 128], [1, w]]), bf, t_f)
            return bs, br, t

        nextrow = [bias_row(*todo[0][1:])]

        def project(kind, dst, before):
            what, c, w = todo.pop(0)
            assert what == kind
            bs, br, tb = nextrow[0]
            if todo:
                nextrow[0] = bias_row(*todo[0][1:])
            slot, pair, done = linear("in2", 1 if w <= 256 else 2, xTh, xTl, t_xT)
            toks = []
            for t in range(2):
                toks.append(dve.do(lambda e, t=t, p=pair: e.tensor_tensor(dst[:, t, 0:w], p[t][:, 0:w], br[:, 0:w], ALU.add), done, tb, before, t_f))
            lin_banks.give(slot, *toks)
            brings.give(bs, *toks)
            return toks, done

        def recur(half, free_tmp):
            ss, s, sf = stage.take()
            tx, _ = project("xr", s, sf)
            tcs, banks_x = [], []
            for k in range(0, 4, 2):
                slot, bank, free = work.take()
                tt = turn_blocks(bank, [s[:, t, (k + j) * 128:(k + j + 1) * 128] for j in range(2) for t in range(2)], tx, free)
                for j in range(2):
                    kk = 4 * half + k + j
                    ps, o = bank[:, j * 256:(j + 1) * 256], xc[:, k + j, :]
                    w = [col(8 + n)[:, kk:kk + 1] for n in range(4)]
                    b = col(12)[:, kk:kk + 1]
                    t = act.do(lambda e, o=o, p=ps, w=w, b=b: e.activation(o, p, ACT.Identity, bias=b, scale=w[3]), tt, free_tmp, t_big)
                for j in range(2):
                    kk = 4 * half + k + j
                    ps, o = bank[:, j * 256:(j + 1) * 256], xc[:, k + j, :]
                    w = [col(8 + n)[:, kk:kk + 1] for n in range(4)]
                    for n in (1, 2, 3):
                        t = dve.do(lambda e, o=o, p=ps, w=w, n=n: e.scalar_tensor_tensor(
                            out=o[:, n:], in0=p[:, 0:256 - n], scalar=w[3 - n], in1=o[:, n:], op0=ALU.mult, op1=ALU.add), t)
                    tcs.append(t)
                work.give(slot, t)
            stage.give(ss, tt)
            ss, s, sf = stage.take()
            ty, _ = project("yr", s, sf)
            for k in range(0, 4, 2):
                slot, bank, free = work.take()
                tt = turn_blocks(bank, [s[:, t, (k + j) * 128:(k + j + 1) * 128] for j in range(2) for t in range(2)], ty, free)
                tgl = act.do(lambda e, o=gl[:, k:k + 2, :], p=bank[:, :].rearrange("p (k t) -> p k t", k=2):
                             e.activation(o, p, ACT.Gelu_apprx_tanh), tt, free_tmp, t_big)
                work.give(slot, tgl)
            stage.give(ss, tt)
            for n, (dst, nb) in enumerate(((rg, nbr), (ig, nbi))):
                for k in range(0, 4, 2):
                    slot, bank, free = work.take()
                    pe.wait(free, tcs, t_wg)
                    for j in range(2):
                        kk = 4 * half + k + j
                        tm = pe.do(lambda e, bank=bank, j=j, n=n, kk=kk, k=k: e.matmul(bank[:, j * 256:(j + 1) * 256], wrg[:, n, kk, :], xc[:, k + j, :],
                                                                                       start=True, stop=True))
                    for j in range(2):
                        kk = 4 * half + k + j
                        t = act.do(lambda e, o=dst[:, k + j, :], p=bank[:, j * 256:(j + 1) * 256], b=nb[:, kk:kk + 1]:
                                   e.activation(o, p, ACT.Exp, bias=b, scale=-1.0), tm, t_nb, free_tmp, t_big)
                    work.give(slot, t)
                t = dve.do(lambda e, o=dst: e.tensor_scalar(o, o, 1.0, None, ALU.add), t)
                t = dve.do(lambda e, o=dst: e.reciprocal(o, o), t)
            ti = dve.do(lambda e: e.tensor_tensor(ig, ig, xc, ALU.mult), t)
            for k in range(4):
                kk = 4 * half + k
                t = act.do(lambda e, k=k, kk=kk: e.activation(rg[:, k, :], rg[:, k, :], ACT.Tanh, scale=halfrate[:, kk:kk + 1]), ti, t_sp)
            t2 = dve.do(lambda e: e.tensor_scalar(xc, rg, -1.0, 1.0, ALU.mult, ALU.add), t)
            t2 = dve.do(lambda e: e.reciprocal(xc, xc), t2)
            s2, sqb, sf2 = stage.take()
            sqv = sqb[:, :, :].rearrange("p t (k n) -> p (t k) n", k=2)
            t3 = act.do(lambda e: e.activation(sqv, rg, ACT.Sqrt, scale=-1.0), t, sf2, t_f)
            t4 = dve.do(lambda e: e.scalar_tensor_tensor(out=rg, in0=rg, scalar=1.0, in1=xc, op0=ALU.add, op1=ALU.mult), t2, t3)
            t5 = dve.do(lambda e: e.scalar_tensor_tensor(out=sqv, in0=sqv, scalar=2.0, in1=xc, op0=ALU.mult, op1=ALU.mult), t3, t2)
            t5 = dve.do(lambda e: e.tensor_tensor(ig, ig, sqv, ALU.mult), t5)
            for k in range(4):
                t6 = dve.do(lambda e, k=k: e.tensor_tensor_scan(sqv[:, k, :], rg[:, k, :], ig[:, k, :], 0.0, ALU.mult, ALU.add), t4, t5)
            t7 = dve.do(lambda e: e.tensor_tensor(gl, gl, sqv, ALU.mult), t6, tgl)
            stage.give(s2, t7)
            o, lo = rTh[:, 4 * half:4 * half + 4, :], rTl[:, 4 * half:4 * half + 4, :]
            th = act.do(lambda e: e.activation(o, gl, ACT.Copy), t7, t_f)
            tl = dve.do(lambda e: e.tensor_tensor(lo, gl, o.bitcast(F), ALU.subtract), th, t_f)
            return [th, tl]

        t_rT = recur(0, None)
        t_rT = recur(1, t_rT)
        t_rec = fence()

        rbias = big[:, 2048:6144].rearrange("p (h t k) -> p h t k", h=8, t=2)
        for t in range(2):
            src = bass.AP(a["scratch"].tensor, 255 - 128 * t, [[4095, 128], [512, 8], [1, 256]])
            t_rb = relsem.load(pool, rbias[:, :, t, :], src, t_scr, t_rec)

        qT = sb("q2T", [128, 4, 256], F, inner)
        qiT = sb("qiT", [128, 4, 256], F, inner)
        kT = sb("k2T", [128, 2, 256], F, inner)
        kiT = sb("kiT", [128, 1, 256], F, inner)
        v2 = sb("v2", [128, 2, 128], F, inner)
        ss, s, sf = stage.take()
        tq, _ = project("qi", s, sf)
        tqi, tt = pairs_turned(s, 4, qiT, 0, 0.125, tq, t_f)
        stage.give(ss, tt)
        ss, s, sf = stage.take()
        tk, _ = project("kw", s, sf)
        tw = dve.do(lambda e, s=s: e.tensor_scalar(wi[:, :, :], s[:, :, 64:72], 8.0 ** -0.5, None, ALU.mult), tk, t_f)
        td = pool.do(lambda e, s=s: e.tensor_copy(s[:, :, 128:192], s[:, :, 0:64]), tk)
        td = pool.do(lambda e, s=s: e.tensor_copy(s[:, :, 192:256], s[:, :, 0:64]), tk)
        tki, tt = pairs_turned(s[:, :, 128:256], 1, kiT, 0, 1.0, td, t_f)
        stage.give(ss, tt, tw)
        rl_ring = Ring([sb(f"rl{i}", [128, 2, 256], F, inner) for i in range(2)])
        m8 = small[:, 160:176]
        ta = [None, None]
        for h in range(8):
            slot, bank, free = work.take()
            pe.wait(free, tqi, tki)
            q, k = half_of(qiT, h), kiT[64 * (h % 2):64 * (h % 2) + 64, 0, :]
            pe.quiet(lambda e, q=q, k=k, b=bank: e.matmul(b[:, 0:256], q[:, 0:128], k, start=True, stop=True))
            tm = pe.do(lambda e, q=q, k=k, b=bank: e.matmul(b[:, 256:512], q[:, 128:256], k, start=True, stop=True))
            rs_, rl, rf = rl_ring.take()
            tr = act.do(lambda e, o=rl, b=bank: e.activation(o[:, :, :], b[:, :].rearrange("p (t k) -> p t k", t=2), ACT.Relu), tm, rf, t_f)
            work.give(slot, tr)
            for t in range(2):
                if h == 0:
                    ta[t] = dve.do(lambda e, t=t, o=rl: e.tensor_scalar(acc[:, t, :], o[:, t, :], wi[:, t, 0:1], None, ALU.mult), tr, tw, tb)
                else:
                    ta[t] = dve.do(lambda e, t=t, o=rl, h=h: e.scalar_tensor_tensor(out=acc[:, t, :], in0=o[:, t, :], scalar=wi[:, t, h:h + 1],
                                                                                    in1=acc[:, t, :], op0=ALU.mult, op1=ALU.add), tr, ta[t])
            rl_ring.give(rs_, *ta)
        ss, s, sf = stage.take()
        tq, _ = project("q", s, sf)
        tq, tt = pairs_turned(s, 4, qT, 0, 0.125, tq, t_f)
        stage.give(ss, tt)
        ss, s, sf = stage.take()
        tk, _ = project("kv", s, sf)
        tv = act.do(lambda e, s=s: e.activation(v2[:, :, :], s[:, :, 128:256], ACT.Copy), tk, t_f)
        td = []
        for t in range(2):
            for u in range(2):
                td.append(pool.do(lambda e, t=t, u=u, s=s: e.tensor_copy(
                    s[:, t, 256:512].rearrange("p (h u d) -> p h u d", h=2, u=2)[:, :, u, :],
                    s[:, t, 0:128].rearrange("p (h d) -> p h d", h=2)), tk))
        tk, tt = pairs_turned(s[:, :, 256:512], 2, kT, 0, 1.0, td, t_f)
        stage.give(ss, tt, tv)

        tl = dve.do(lambda e: e.tensor_tensor(left[:, :, :], acc[:, :, :], causal, ALU.add), ta, t_const, t_scr)
        tl = [tl, tl]
        for n in range(8):
            for t in range(2):
                tm = dve.do(lambda e, t=t: e.max(m8[:, 8 * t:8 * t + 8], left[:, t, :]), tl[t])
                tl[t] = dve.do(lambda e, t=t: e.match_replace(left[:, t, :], m8[:, 8 * t:8 * t + 8], left[:, t, :], TAKEN), tm)
        t = dve.do(lambda e: e.tensor_scalar(acc[:, :, :], left[:, :, :], -1e38, BIG, ALU.is_le, ALU.mult), tl)
        t_mask = dve.do(lambda e: e.scalar_tensor_tensor(out=left[:, :, :], in0=acc[:, :, :], scalar=-BIG, in1=causal, op0=ALU.add, op1=ALU.add), t)

        sga = nrm
        tga, tgb = [], []
        for c in (0, 512):
            tp, done = project("ga", sga[:, :, c:c + 512], t_turn)
            for t in range(2):
                tga.append(act.do(lambda e, t=t, c=c: e.activation(sga[:, t, c:c + 512], sga[:, t, c:c + 512], ACT.Sigmoid), tp))
        for c in (0, 512):
            tp, done = project("gb", sgb[:, :, c:c + 512], t_rec)
            for t in range(2):
                tgb.append(act.do(lambda e, t=t, c=c: e.activation(sgb[:, t, c:c + 512], sgb[:, t, c:c + 512], ACT.Sigmoid), tp))
        x_done = done
        tmb = []
        for c in (0, 512):
            slot, pair, done = linear("orn", 2, rTh, rTl, t_rT)
            last = []
            for t in range(2):
                last.append(dve.do(lambda e, t=t, c=c, p=pair: e.tensor_tensor(sgb[:, t, c:c + 512], p[t][:, :], sgb[:, t, c:c + 512], ALU.mult), done, tgb))
            lin_banks.give(slot, *last)
            tmb += last

        _, y, yf = stage.take()
        if y is not stage.items[0]:
            stage.give(1)
            _, y, yf = stage.take()
        other = stage.items[1][:, :, :]
        s_ring = Ring([rl_ring.items[0], rl_ring.items[1], other[:, :, 0:256]])
        s_ring.free = [rl_ring.free[0], rl_ring.free[1], stage.free[1]]
        p_ring = Ring(p2)
        p_ring.free = [list(t_xT_in), list(t_xT_in)]
        jobs = []
        for h in range(8):
            def finish(s, ps, tok, sf, h=h):
                t = dve.do(lambda e: e.tensor_tensor(s[:, :, :], ps, rbias[:, h, :, :], ALU.add), tok, sf, t_rb, t_f)
                u = pool.do(lambda e: e.tensor_tensor(s[:, :, :], s[:, :, :], left[:, :, :], ALU.add), t, t_mask)
                return u, t
            kv = h // 4
            jobs.append((half_of(qT, h), kT[64 * (h % 2):64 * (h % 2) + 64, kv, :], lambda kt, kv=kv: v2[:, kt, kv * 64:(kv + 1) * 64],
                         finish, None, 64 * h, [tq, tk, tv]))
        ty = softmax_heads(jobs, s_ring, p_ring, y, yf + [t_f])
        t_aT, tt = turn_split(y, 0, 4, xTh, xTl, 0, ty, x_done)
        tmg = []
        for c in (0, 512):
            slot, pair, done = linear("oat", 1, xTh, xTl, t_aT)
            last = []
            for t in range(2):
                m = dve.do(lambda e, t=t, c=c, p=pair: e.tensor_tensor(sga[:, t, c:c + 512], p[t][:, :], sga[:, t, c:c + 512], ALU.mult), done, tga)
                last.append(m)
                tmg.append(dve.do(lambda e, t=t, c=c: e.tensor_tensor(sga[:, t, c:c + 512], sga[:, t, c:c + 512], sgb[:, t, c:c + 512], ALU.add), m, tmb))
            lin_banks.give(slot, *last)
        t_mT, tt = turn_split(sga, 0, 8, xTh, xTl, 0, tmg, done)
        res = []
        tf_ = fence()
        for c in (0, 512):
            slot, pair, done = linear("out2", 2, xTh, xTl, t_mT)
            res += residual([(slot, pair, c)], done, gates[:, 0:1024], other, [tf_, res])
        inner.close()
        sc.close()

        t_f = fence()
        hTh = sb("hTh2", [128, 22, 256], R, sc)
        hTl = sb("hTl2", [128, 22, 256], R, sc)
        tmp_ring = Ring([big[:, 2048 + 256 * i:2304 + 256 * i] for i in range(2)])
        t_g2 = side.load(pool, gbc[:, :], bass.AP(a["g_final_2"].tensor, 0, [[0, 128], [1, D]]), t_f)
        st, rs, sq = inverse_rms(xres, nrm, res, tt)
        t0 = dve.do(lambda e: e.tensor_scalar(nrm[:, 0, :], xres[:, 0, :], st[:, 4:5], None, ALU.mult), rs, sq)
        t1 = act.do(lambda e: e.activation(nrm[:, 1, :], xres[:, 1, :], ACT.Copy, scale=st[:, 5:6]), rs, sq)
        t_xT, t_turn = turn_split(nrm, 0, 8, xTh, xTl, 0, [t0, t1], [done, t_f, tg2], gain2, mod[:, 16:24], tmp_ring)
        cring = Ring([big[:, 2560 + 512 * i:3072 + 512 * i].rearrange("p (k t) -> p k t", k=2) for i in range(6)])
        stage = Ring([nrm[:, :, 0:512], nrm[:, :, 512:1024]])
        stage.give(0, t_turn)
        stage.give(1, t_turn)
        t_hT = []

        def convolved(s, k, kt, after):
            slot, bank, free = work.take()
            tt = turn_blocks(bank, [s[:, t, (k + j) * 128:(k + j + 1) * 128] for j in range(2) for t in range(2)], after, free)
            cs, cv, cf = cring.take()
            last = []
            for j in range(2):
                ps, o = bank[:, j * 256:(j + 1) * 256], cv[:, j, :]
                t = act.do(lambda e, o=o, p=ps, q=kt + j: e.activation(o, p, ACT.Identity, bias=CVB(q), scale=CVW(2, q)), tt, cf, t_f)
            for j in range(2):
                ps, o = bank[:, j * 256:(j + 1) * 256], cv[:, j, :]
                for n in (1, 2):
                    t = dve.do(lambda e, o=o, p=ps, n=n, q=kt + j: e.scalar_tensor_tensor(out=o[:, n:], in0=p[:, 0:256 - n], scalar=CVW(2 - n, q),
                                                                                          in1=o[:, n:], op0=ALU.mult, op1=ALU.add), t)
                last.append(t)
            work.give(slot, *last)
            return cs, cv, last, tt

        def raw_tile(w):
            slot, pair, done = linear("up2", 2 if w == 512 else 1, xTh, xTl, t_xT)
            ss, s, sf = stage.take()
            t0 = act.do(lambda e: e.activation(s[:, 0, 0:w], pair[0][:, 0:w], ACT.Copy), done, sf)
            t1 = dve.do(lambda e: e.tensor_copy(s[:, 1, 0:w], pair[1][:, 0:w]), done, sf)
            lin_banks.give(slot, t0, t1)
            return ss, s, [t0, t1], done

        def finish_gate(g, c, w):
            ss, s, ts = g
            made = []
            for k in range(0, w // 128, 2):
                cs, cv, tc, tt = convolved(s, k, 22 + c // 128 + k, ts)
                t = act.do(lambda e, o=cv: e.activation(o, o, ACT.Silu), tc)
                made.append((cs, cv, t))
            stage.give(ss, tt)
            return made

        def finish_value(g, made, c, w):
            ss, s, ts = g
            for k in range(0, w // 128, 2):
                cs, cv, tc, tt = convolved(s, k, c // 128 + k, ts)
                gs, gv, tg = made[k // 2]
                t = dve.do(lambda e, o=cv, g=gv: e.tensor_tensor(o, o, g, ALU.mult), tc, tg)
                kt = c // 128 + k
                o, lo = hTh[:, kt:kt + 2, :], hTl[:, kt:kt + 2, :]
                th = act.do(lambda e, o=o, x=cv: e.activation(o, x, ACT.Copy), t, t_f)
                tl = dve.do(lambda e, o=lo, x=cv, h=o: e.tensor_tensor(o, x, h.bitcast(F), ALU.subtract), th, t_f)
                cring.give(gs, t)
                cring.give(cs, th, tl)
            stage.give(ss, tt)
            return [th, tl]

        waiting = None
        for c, w in tiles_of(DFF):
            ss, s, ts, done = raw_tile(w)
            if waiting:
                t_hT = finish_value(*waiting)
            gate = (ss, s, ts)
            ss, s, ts, done = raw_tile(w)
            made = finish_gate(gate, c, w)
            waiting = ((ss, s, ts), made, c, w)
        t_hT = finish_value(*waiting)
        (s0, s1), pairs, done = down("down2", hTh, hTl, t_hT)
        tf_ = fence()
        res = residual([(s0, pairs[0], 0), (s1, pairs[1], 512)], done, gates[:, 1024:2048], nrm[:, :, 0:512], tf_)

        st, rs, sq = inverse_rms(xres, nrm, res, fence())
        for t in range(2):
            to = dve.do(lambda e, t=t: e.scalar_tensor_tensor(out=nrm[:, t, :], in0=xres[:, t, :], scalar=st[:, 4 + t:5 + t], in1=gbc[:, :],
                                                              op0=ALU.mult, op1=ALU.mult), rs, sq, t_g2)
            t_out = outsem.load(sp, out[0, t * 128:(t + 1) * 128, :], nrm[:, t, :], to)
        sp.wait(t_out)
        pool.wait((scrsem.sem, scrsem.n))

        sc.close()
        block = ctx.enter_context(nc.Block())

        @block.sync
        def _(e):
            for f in sp.program:
                f(e)

        @block.scalar
        def _(e):
            for f in act.program:
                f(e)

        @block.vector
        def _(e):
            for f in dve.program:
                f(e)

        @block.gpsimd
        def _(e):
            for f in pool.program:
                f(e)

        @block.tensor
        def _(e):
            for f in pe.program:
                f(e)


def shape_constants():
    p = np.arange(128)
    key = np.arange(256)
    c = np.zeros((128, 1408), np.float32)
    c[:, 0:128] = np.eye(128)
    for t in range(2):
        q = p + 128 * t
        d = np.abs(q[:, None] - key[None, :])
        c[:, 128 + 256 * t:384 + 256 * t] = np.where(d <= 128, d, 1e33)
        c[:, 896 + 256 * t:1152 + 256 * t] = np.where(key[None, :] <= q[:, None], 0.0, -BIG)
    col, kcol = p % 64, key % 64
    start = np.clip(col - 8, 0, 48)
    inside = (kcol[None, :] >= start[:, None]) & (kcol[None, :] < start[:, None] + 16)
    c[:, 640:896] = np.where(inside, 0.0, -BIG)
    return c


def distance_buckets():
    n = np.arange(256)
    nf = np.maximum(n, 1).astype(np.float32)
    big = 16 + (np.log(nf / np.float32(16)) / np.float32(np.log(8.0)) * np.float32(16)).astype(np.int32)
    b = np.where(n < 16, n, np.minimum(big, 31))
    hot = np.zeros((32, 512), np.float32)
    hot[b[::-1], np.arange(256)] = 1.0
    hot[0, 256:] = 1.0
    return hot


def kernel(**inputs):
    import concourse.bacc as _bacc
    from concourse.bass_utils import run_bass_kernel_spmd as _run

    nc = _bacc.Bacc("TRN2", target_bir_lowering=False, num_devices=1)
    arrays, args = {}, {}
    given = {n: np.ascontiguousarray(v) for n, v in inputs.items()}
    given["constants"] = shape_constants()
    given["onehot"] = distance_buckets()
    for name, v in given.items():
        arrays[f"in_{name}"] = v
        args[name] = nc.dram_tensor(f"in_{name}", v.shape, mybir.dt.from_np(v.dtype), kind="ExternalInput").ap()
    args["scratch"] = nc.dram_tensor("scratch", (128, 8, 512), F, kind="Internal").ap()
    args["scratch_rpb"] = nc.dram_tensor("scratch_rpb", (64, 12 * 15 * 31), F, kind="Internal").ap()
    out = nc.dram_tensor("out_0", (1, 256, 1024), F, kind="ExternalOutput").ap()
    build(nc, args, out)
    r = _run(nc, [arrays], core_ids=[0])
    return r.results[0]["out_0"]
```

```python
from collections import deque
from contextlib import ExitStack

import numpy as np

import concourse.bass as bass
from concourse import mybir

F = mybir.dt.float32
R = mybir.dt.float32r
ALU = mybir.AluOpType
ACT = mybir.ActivationFunctionType
AX = mybir.AxisListType.X

D = 1024
DFF = 2816
EPS = 1e-6
BIG = 1e30
TAKEN = -3e38
RAWS, SPLITS = 4, 3
POOLED = ("gu1", "down1", "up2")


class Engine:

    def __init__(self, sem):
        self.sem, self.n, self.program, self.seen = sem, 0, [], {}

    def wait(self, *tokens):
        for t in tokens:
            if t is None:
                continue
            if isinstance(t, list):
                self.wait(*t)
                continue
            sem, value = t
            if self.seen.get(sem.name, 0) < value:
                self.seen[sem.name] = value
                self.program.append(lambda e, s=sem, v=value: e.wait_ge(s, v))

    def quiet(self, fn, *after):
        self.wait(*after)
        self.program.append(fn)

    def do(self, fn, *after):
        self.wait(*after)
        self.n += 1
        self.program.append(lambda e, f=fn, s=self.sem: f(e).then_inc(s, 1))
        return self.sem, self.n

    def now(self):
        return self.sem, self.n


class Landing:

    def __init__(self, sem):
        self.sem, self.n = sem, 0

    def load(self, queue, out, src, *after):
        queue.wait(*after)
        self.n += 16
        queue.program.append(lambda e, o=out, i=src, s=self.sem: e.dma_start(o, i).then_inc(s, 16))
        return self.sem, self.n


class Ring:

    def __init__(self, items, later):
        self.items, self.free, self.at, self.later = items, [[] for _ in items], -1, later
        self.held = [False] * len(items)

    def take(self):
        while all(self.held):
            self.later.popleft()()
        n = len(self.items)
        at = next(i % n for i in range(self.at + 1, self.at + 1 + n) if not self.held[i % n])
        self.at = at
        self.held[at] = True
        after, self.free[at] = self.free[at], []
        return at, self.items[at], after

    def give(self, slot, *tokens):
        self.held[slot] = False
        self.free[slot] += list(tokens)


def weight_parts(w, k0, nk, c0, nc_):
    return w[k0 * 128:(k0 + nk) * 128, c0:c0 + nc_].rearrange("(k p) n -> p k n", p=128)


def columns(w, c0, width):
    nk = w.shape[0] // 128
    step = min(nk, 2048 // width)
    return [(weight_parts(w, k, min(step, nk - k), c0, width), k, min(step, nk - k), width) for k in range(0, nk, step)]


def tiles_of(n):
    return [(c, min(512, n - c)) for c in range(0, n, 512)]


IN2 = [("qi", 768, 512, ["", "rel", ""]),
       ("kw", 1280, 72, ["qi0", "qi2", ""]),
       ("xr", 1352, 512, ["ki", "", "h0"]),
       ("yr", 2376, 512, ["conv00 h1", "conv02 h2", "h3"]),
       ("xr", 1864, 512, ["gelu00 h4", "gelu02 gate000 h5", "gate002 h6"]),
       ("yr", 2888, 512, ["gate010 gate012 h7", "conv10", "rec0 conv12 top"]),
       ("q", 0, 512, ["gelu10 top0", "scan0 top1", "gelu12 top2"]),
       ("kv", 512, 256, ["half0 bias0 q0 top3", "gate100 gate102 q2 top4", "gate110 gate112 top5"]),
       ("gb", 4424, 512, ["kv top6", "rec1 top7", "scan1 mask"]),
       ("gb", 4936, 512, ["half1 bias1 attend", "s0", "s1"]),
       ("ga", 3400, 512, ["s2", "s3", "s4"]),
       ("ga", 3912, 512, ["s5", "s6", "s7"])]
MIX_TILES = [[(1024, 4), (512, 4), (0, 0)], [(2048, 4), (1536, 0), (512, 0), (1024, 4), (0, 0)]]
UP2 = tiles_of(DFF)[-1:] + tiles_of(DFF)[:-1]
FIRST = [(0, 1), (1, 1), (2, 2), (4, 4)]


def stream_plan(a):
    plan = []
    w = a["w_mem_kv"]
    plan += [("mem", (weight_parts(w[0], k, nk, 0, 512), k, nk, 512)) for k, nk in FIRST]
    plan += [("mem", x) for x in columns(w[1], 0, 512)]

    def block(w_in, l):
        p = []
        for c, _ in MIX_TILES[l]:
            p += [("in", x) for x in columns(w_in, c, 512)]
        for c in (0, 512):
            p += [("out", x) for x in columns(a["w_out"][l], c, 512)]
        for c, w in tiles_of(DFF):
            p += [(f"gu{l}", x) for x in columns(a["w_gate_up"][l], c, w)]
            p += [(f"gu{l}", x) for x in columns(a["w_gate_up"][l], DFF + c, w)]
        for c in (0, 512):
            p += [(f"down{l}", x) for x in columns(a["w_down"][l], c, 512)]
        return p

    plan += block(a["w_in_a"][0], 0)
    w_ada = a["w_ada_2"][0]
    ada = [("ada", (w_ada[k * 128:(k + 1) * 128, c * 2048:(c + 1) * 2048], k, c, 2048)) for k in range(8) for c in range(3)]
    n = 0
    for p in block(a["w_in_b"][0], 1):
        plan.append(p)
        if p[0] in ("gu1", "down1"):
            n += 1
            if n > 4 and n % 6 != 0 and ada:
                plan.append(ada.pop(0))
    assert not ada
    for _, c, w, _ in IN2:
        plan += [("in2", x) for x in columns(a["w_in_2"][0], c, w)]
    for kind, w in (("orn", "w_o_rnn_2"), ("oat", "w_o_attn_2"), ("out2", "w_out_2")):
        for c in (0, 512):
            plan += [(kind, x) for x in columns(a[w][0], c, 512)]
    for c, w in UP2:
        plan += [("up2", x) for x in columns(a["w_up_2"][0], DFF + c, w)]
        plan += [("up2", x) for x in columns(a["w_up_2"][0], c, w)]
    for c in (0, 512):
        plan += [("down2", x) for x in columns(a["w_down_2"][0], c, 512)]
    return plan


def build(nc, a, out):
    ctx = ExitStack()
    with ctx:
        def sb(name, shape, dt=F, scope=ctx):
            return scope.enter_context(nc.sbuf_tensor(name, shape, dt))

        def sem(name):
            return ctx.enter_context(nc.semaphore(name))

        pe, act, dve, pool, sp = (Engine(sem(n)) for n in ("s_pe", "s_act", "s_dve", "s_pool", "s_sp"))
        banks = [ctx.enter_context(nc.psum_tensor(f"bank{i}", [128, 512], F)) for i in range(8)]
        later = deque()

        def drain_later():
            while later:
                later.popleft()()

        raw = [sb(f"raw{i}", [128, 2048]) for i in range(RAWS)]
        hi_s = [sb(f"hi{i}", [128, 2048], R) for i in range(SPLITS)]
        lo_s = [sb(f"lo{i}", [128, 2048], R) for i in range(SPLITS)]
        xres = sb("xres", [128, 2, D])
        nrm = sb("nrm", [128, 2, D])
        xTh = sb("xTh", [128, 8, 256], R)
        xTl = sb("xTl", [128, 8, 256], R)
        const = sb("const", [128, 1408])
        ident = const[:, 0:128]
        dist = const[:, 128:640].rearrange("p (t k) -> p t k", t=2)
        window = const[:, 640:896]
        causal = const[:, 896:1408].rearrange("p (t k) -> p t k", t=2)
        big = sb("big", [128, 6144])
        gbc = sb("gbc", [128, D])
        rows = big[:, 2048:2432].rearrange("p (n d) -> p n d", n=3)
        cols = sb("cols", [128, 128 + 96 + 88])
        small = sb("small", [128, 176])
        junk = sb("junk", [128, 512], mybir.dt.bfloat16)
        junk_done = {"t": None}
        ones = sb("ones", [128, 128])
        stats = [sb(f"stat{i}", [128, 16]) for i in range(4)]
        rmss = [sb(f"rms{i}", [128, 16]) for i in range(9)]

        memsem, nmsem, xsem, rowsem, idsem, consem = (Landing(sem(n)) for n in ("d_mem", "d_norm", "d_x", "d_rows", "d_ident", "d_const"))
        side, rpbsem, relsem, rel1sem, gsem, scrsem, outsem = (Landing(sem(n)) for n in ("d_side", "d_rpb", "d_rel", "d_rel1", "d_g", "d_scr", "d_out"))

        plan = stream_plan(a)
        slots = [Landing(sem(f"d_raw{i}")) for i in range(RAWS)]
        landed, raw_free, ready, released = {}, {}, {}, {}
        state = {"dma": 0, "split": 0, "use": 0, "owed": 0}
        order = [i for i, p in enumerate(plan) if p[0] != "ada"]
        number = {i: m for m, i in enumerate(order)}
        acc_tok = {"t": [None, None, None], "c": None}

        def issue(upto):
            while state["dma"] < min(upto, len(plan)):
                i = state["dma"]
                kind, (src, k0, nk, w) = plan[i]
                dst = raw[i % RAWS][:, 0:2048 if kind == "ada" else nk * w]
                if kind != "ada":
                    dst = dst.rearrange("p (k n) -> p k n", k=nk)
                landed[i] = slots[i % RAWS].load(sp, dst, src, raw_free.get(i - RAWS))
                state["dma"] += 1

        def split(i):
            kind, (_, k0, nk, w) = plan[i]
            if kind == "ada":
                acc = big[:, nk * 2048:(nk + 1) * 2048]
                t = dve.do(lambda e: e.scalar_tensor_tensor(out=acc, in0=raw[i % RAWS][:, :], scalar=small[:, k0:k0 + 1], in1=acc,
                                                            op0=ALU.mult, op1=ALU.add), landed[i], acc_tok["t"][nk], acc_tok["c"])
                acc_tok["t"][nk] = t
                raw_free[i] = [t]
                return
            m = number[i]
            s, n = m % SPLITS, nk * w
            src, h, lo = raw[i % RAWS][:, 0:n], hi_s[s][:, 0:n], lo_s[s][:, 0:n]
            before = released.get(m - SPLITS)
            th = act.do(lambda e: e.activation(h, src, ACT.Copy), landed[i], before)
            engine = pool if m % 3 == 2 and kind in POOLED else dve
            tl = engine.do(lambda e: e.tensor_tensor(lo, src, h.bitcast(F), ALU.subtract), th, landed[i], before)
            raw_free[i] = [th, tl]
            ready[m] = [th, tl]

        def split_through(m):
            upto = order[min(m, len(order) - 1)]
            while state["split"] <= upto:
                issue(state["split"] + 1)
                split(state["split"])
                state["split"] += 1
                issue(state["split"] + RAWS)

        lin_banks = Ring([(banks[0], banks[1]), (banks[2], banks[3])], later)
        work = Ring(banks[4:8], later)

        def pop(n):
            for _ in range(n):
                if later:
                    later.popleft()()

        def run(names):
            for x in names:
                named[x]()

        named = {}

        def linear(kind, parts, xh, xl, xt, evacuate, pops=1, hooks=None):
            slot, pair, free = lin_banks.take()
            hooks = deque(hooks or [])

            def between():
                if hooks:
                    run(hooks.popleft().split())
                else:
                    pop(pops)

            for p in range(parts):
                m = state["use"]
                state["use"] += 1
                what, (_, k0, nk, w) = plan[order[m]]
                assert what == kind, (what, kind)
                h, lo = [x[m % SPLITS][:, 0:nk * w].rearrange("p (k n) -> p k n", k=nk) for x in (hi_s, lo_s)]
                pe.wait(ready[m], free)
                for k in range(nk):
                    while xt[k0 + k] is None:
                        later.popleft()()
                    pe.wait(xt[k0 + k])
                    for t in range(2):
                        o = pair[t][:, 0:w]
                        sh, sl = xh[:, k0 + k, t * 128:(t + 1) * 128], xl[:, k0 + k, t * 128:(t + 1) * 128]
                        begin, end = p == 0 and k == 0, p == parts - 1 and k == nk - 1
                        pe.quiet(lambda e, o=o, s=sh, x=h[:, k, :], b=begin: e.matmul(o, s, x, start=b, stop=False))
                        pe.quiet(lambda e, o=o, s=sh, x=lo[:, k, :]: e.matmul(o, s, x, start=False, stop=False))
                        f = lambda e, o=o, s=sl, x=h[:, k, :], d=end: e.matmul(o, s, x, start=False, stop=d)
                        if k == nk - 1 and t == 1:
                            done = pe.do(f)
                        else:
                            pe.quiet(f)
                    if k == min(1, nk - 1):
                        split_through(state["owed"])
                    if k % 2 == 1 and k < nk - 1:
                        between()
                released[m] = done
                if p == parts - 1:
                    lin_banks.give(slot, *evacuate(pair, done))
                state["owed"] = m + SPLITS
                if p < parts - 1:
                    between()
            return done

        def turn_blocks(bank, blocks, *after):
            pe.wait(*after)
            for i, x in enumerate(blocks):
                f = lambda e, x=x, o=bank[:, i * 128:(i + 1) * 128]: e.transpose(o, x, ident)
                if i == len(blocks) - 1:
                    return pe.do(f)
                pe.quiet(f)

        def turn_piece(src, c0, n, dh, dl, k0, xt, after, before, gain=None, t_gain=None, shift=None, tmp=None):
            slot, bank, free = work.take()
            turned = turn_blocks(bank, [src[:, t, c0 + j * 128:c0 + (j + 1) * 128] for j in range(n) for t in range(2)], after, free, t_ident)
            view = bank[:, 0:n * 256].rearrange("p (k t) -> p k t", k=n)
            if gain is None:
                o, lo = dh[:, k0:k0 + n, :], dl[:, k0:k0 + n, :]
                th = act.do(lambda e: e.activation(o, view, ACT.Copy), turned, before)
                tl = dve.do(lambda e: e.tensor_tensor(lo, view, o.bitcast(F), ALU.subtract), th, before)
                work.give(slot, th, tl)
                for j in range(n):
                    xt[k0 + j] = [th, tl]
                return turned
            parts = [(dh[:, k0 + j, :], dl[:, k0 + j, :], bank[:, j * 256:(j + 1) * 256], gain[:, k0 + j:k0 + j + 1], j) for j in range(n)]
            if shift is None:
                for o, lo, ps, g, j in parts:
                    th = act.do(lambda e, o=o, p=ps, g=g: e.activation(o, p, ACT.Copy, scale=g), turned, before, t_gain)
                for o, lo, ps, g, j in parts:
                    tl = dve.do(lambda e, o=lo, p=ps, g=g, h=o: e.scalar_tensor_tensor(
                        out=o, in0=p, scalar=g, in1=h.bitcast(F), op0=ALU.mult, op1=ALU.subtract), th, before, t_gain)
                    xt[k0 + j] = [th, tl]
                work.give(slot, th, tl)
                return turned
            for o, lo, ps, g, j in parts:
                ts, tb, tf = tmp.take()
                b = shift[:, k0 + j:k0 + j + 1]
                if k0 % 4 == 0:
                    t0 = act.do(lambda e, o=tb, p=ps, g=g, b=b: e.activation(o, p, ACT.Identity, bias=b, scale=g), turned, tf, t_gain)
                else:
                    t0 = dve.do(lambda e, o=tb, p=ps, g=g, b=b: e.tensor_scalar(o, p, g, b, ALU.mult, ALU.add), turned, tf)
                th = act.do(lambda e, o=o, p=tb: e.activation(o, p, ACT.Copy), t0, before)
                tl = dve.do(lambda e, o=lo, p=tb, h=o: e.tensor_tensor(o, p, h.bitcast(F), ALU.subtract), th, before)
                tmp.give(ts, th, tl)
                xt[k0 + j] = [th, tl]
            work.give(slot, t0)
            return turned

        class Rms:

            def __init__(self, st):
                self.st, self.tokens, self.rooted = st, [], None
                self.r = [st[:, 8:9], st[:, 9:10]]

            def square(self, x, t, j, after):
                tok = act.do(lambda e: e.activation(junk[:, :], x, ACT.Square, accum_out=self.st[:, 2 * j + t:2 * j + t + 1]), after, junk_done["t"])
                junk_done["t"] = tok
                self.tokens.append(tok)
                return tok

            def root(self):
                st = self.st
                t = dve.do(lambda e: e.tensor_tensor(st[:, 4:6], st[:, 0:2], st[:, 2:4], ALU.add), self.tokens)
                t = dve.do(lambda e: e.tensor_scalar(st[:, 6:8], st[:, 4:6], 1.0 / D, EPS, ALU.mult, ALU.add), t)
                self.rooted = pool.do(lambda e: e.tensor_tensor(st[:, 8:10], st[:, 6:8], half_[:, :], ALU.pow), t, t_half)
                return self.rooted

            @property
            def done(self):
                while self.rooted is None:
                    later.popleft()()
                return self.rooted

        roots = iter(rmss)

        memx = big[:, 0:2048].rearrange("p (t d) -> p t d", t=2)
        t_mem = [memsem.load(sp, memx, a["mem"][0].rearrange("(t p) d -> p t d", p=128))]
        t_ident = idsem.load(act, ident, a["constants"][:, 0:128])
        memrow = big[0:8, 2432:2560]
        t_memrow = nmsem.load(act, memrow, a["norm_mem"].rearrange("(k p) -> k p", p=128))
        issue(RAWS)
        r = 0
        for name in ("norm_mix", "norm_ffn", "norm_mem", "g_mix_2", "g_ffn_2", "c_2", "conv_rnn_w_2", "conv_rnn_b_2", "b_rg_2", "b_ig_2", "lru_lambda_2"):
            v = a[name]
            if len(v.shape) == 3:
                v = v.rearrange("l n d -> (l n) d")
            v = v.rearrange("l (k p) -> (l k) p", p=128) if len(v.shape) == 2 else v.rearrange("(k p) -> k p", p=128)
            t_rows = rowsem.load(sp, rows[r:r + v.shape[0], 0, :], v)
            r += v.shape[0]
        assert r == 128
        cw = a["conv_ffn_w_2"][0].rearrange("n (k p) -> (n k) p", p=128)
        b_in = a["b_in_2"][0]
        t_rows = rowsem.load(sp, rows[0:88, 1, :], cw[0:88, :])
        t_rows = rowsem.load(sp, rows[88:96, 1, :], b_in[2376:3400].rearrange("(k p) -> k p", p=128))
        t_rows = rowsem.load(sp, rows[0:44, 2, :], cw[88:132, :])
        t_rows = rowsem.load(sp, rows[44:88, 2, :], a["conv_ffn_b_2"][0].rearrange("(k p) -> k p", p=128))
        sink = small[:, 16:28]
        t_rows = rowsem.load(sp, sink, bass.AP(a["sink_a"].tensor, 0, [[0, 128], [1, 12]]))
        t_x = xsem.load(sp, xres[:, :, :], a["x"][0].rearrange("(t p) d -> p t d", p=128))
        t_const = consem.load(pool, const[:, 128:1408], a["constants"][:, 128:1408])
        half_ = small[:, 8:10]
        t_half = pool.do(lambda e: e.memset(half_, -0.5))
        t_ones = pool.do(lambda e: e.memset(ones[:, :], 1.0))

        slot, bank, free = work.take()
        tt = pe.do(lambda e, b=bank: e.transpose(b[:, 0:8], memrow, ident[0:8, 0:8]), free, t_memrow, t_ident)
        memgain = small[:, 144:152]
        t_norm = {"mem": dve.do(lambda e, b=bank: e.tensor_copy(memgain, b[:, 0:8]), tt)}
        work.give(slot, t_norm["mem"])

        def turn_rows():
            slot, bank, free = work.take()
            at = 0
            pe.wait(free, t_rows)
            for i, n in enumerate((128, 96, 88)):
                tt = pe.do(lambda e, b=bank, i=i, n=n, at=at: e.transpose(b[:, at:at + n], rows[0:n, i, :], ident[0:n, 0:n]))
                at += n
            t_norm["cols"] = dve.do(lambda e, b=bank: e.tensor_copy(cols[:, :], b[:, 0:312]), tt)
            work.give(slot, t_norm["cols"])

        def col(i):
            return cols[:, 8 * i:8 * i + 8]

        CVW = lambda n, kt: cols[:, 128 + 44 * n + kt:129 + 44 * n + kt] if n < 2 else cols[:, 224 + kt:225 + kt]
        CVB = lambda kt: cols[:, 268 + kt:269 + kt]
        bias_yr = cols[:, 216:224]

        def fence():
            return [e.now() for e in (pe, act, dve, pool)]

        def pairs_piece(src, c0, n, dst, at, scale, after, before):
            slot, bank, free = work.take()
            tt = turn_blocks(bank, [src[:, t, c0 + j * 128:c0 + (j + 1) * 128] for j in range(n) for t in range(2)], after, free, t_ident)
            view = bank[:, 0:n * 256].rearrange("p (k t) -> p k t", k=n)
            o, lo = dst[0][:, at:at + n, :], dst[1][:, at:at + n, :]
            th = act.do(lambda e: e.activation(o, view, ACT.Copy, scale=scale), tt, before)
            tl = dve.do(lambda e: e.scalar_tensor_tensor(out=lo, in0=view, scalar=scale, in1=o.bitcast(F), op0=ALU.mult, op1=ALU.subtract), th, before)
            work.give(slot, th, tl)
            return [th, tl], tt

        def exact_products(o, a, b, last=True):
            pe.quiet(lambda e: e.matmul(o, a[0], b[0], start=True, stop=False))
            pe.quiet(lambda e: e.matmul(o, a[0], b[1], start=False, stop=False))
            return pe.do(lambda e: e.matmul(o, a[1], b[0], start=False, stop=True))

        def scores_of(q, k, after):
            slot, bank, free = work.take()
            pe.wait(free, after)
            for n in range(2):
                tok = exact_products(bank[:, n * 256:(n + 1) * 256], [x[:, n * 128:(n + 1) * 128] for x in q], k)
            return slot, bank[:, :].rearrange("p (t k) -> p t k", t=2), tok

        stat = Ring(stats, later)

        def softmax_steps(jobs, s_ring, p_ring, o_ring, y, at, y_done):
            so, po, oo = {}, {}, {}

            def scores(i):
                q, k, v, finish, sk, after, vafter = jobs[i]
                so[i] = scores_of(q, k, after())

            def soften(i):
                q, k, v, finish, sk, after, vafter = jobs[i]
                slot, ps, tok = so[i]
                ss, s, sf = s_ring.take()
                ts, st, tf = stat.take()
                if finish is None:
                    src, t, fin = ps, tok, None
                else:
                    t, fin = finish(s, ps, tok, sf)
                    src = s
                t = dve.do(lambda e: e.tensor_reduce(st[:, 0:2], src[:, :, :], AX, ALU.max), t, tf)
                if sk is None:
                    t = dve.do(lambda e: e.tensor_scalar(st[:, 2:4], st[:, 0:2], -1.0, None, ALU.mult), t)
                else:
                    t = dve.do(lambda e: e.tensor_scalar(st[:, 2:4], st[:, 0:2], sk, -1.0, ALU.max, ALU.mult), t, t_rows)
                so[i] = (slot, ss, s, sf, ts, st, src, t, fin)

            def exponentials(i):
                slot, ss, s, sf, ts, st, src, t, fin = so[i]
                sk = jobs[i][4]
                te = [act.do(lambda e, n=n: e.activation(s[:, n, :], src[:, n, :], ACT.Exp, bias=st[:, 2 + n:3 + n],
                                                         accum_out=st[:, 4 + n:5 + n]), t, sf) for n in range(2)]
                work.give(slot, te[1] if fin is None else fin)
                if sk is not None:
                    te.append(act.do(lambda e: e.activation(st[:, 6:8], st[:, 2:4], ACT.Exp, bias=sk), t))
                so[i] = (ss, s, te, ts, st)

            def normalise(i):
                ss, s, td, ts, st = so[i]
                den = st[:, 4:6]
                if jobs[i][4] is not None:
                    td = dve.do(lambda e: e.tensor_tensor(st[:, 8:10], st[:, 4:6], st[:, 6:8], ALU.add), td)
                    den = st[:, 8:10]
                tr = dve.do(lambda e: e.reciprocal(st[:, 10:12], den), td)
                t0 = pool.do(lambda e: e.tensor_scalar(s[:, 0, :], s[:, 0, :], st[:, 10:11], 1.0, ALU.mult, ALU.mult), tr)
                t1 = act.do(lambda e: e.activation(s[:, 1, :], s[:, 1, :], ACT.Copy, scale=st[:, 11:12]), tr)
                stat.give(ts, t0, t1)
                so[i] = (ss, s, [t0, t1])

            def turn(i):
                ss, s, tn = so[i]
                slot, bank, free = work.take()
                tt = turn_blocks(bank, [s[:, n, kt * 128:(kt + 1) * 128] for kt in range(2) for n in range(2)], tn, free)
                s_ring.give(ss, tt)
                so[i] = (slot, bank, tt)

            def high(i):
                slot, bank, tt = so[i]
                ps, (ph, pl), pf = p_ring.take()
                view = bank[:, :].rearrange("p (k q) -> p k q", k=2)
                th = act.do(lambda e: e.activation(ph, view, ACT.Copy), tt, pf)
                po[i] = (slot, view, ps, ph, pl, th, pf)

            def low(i):
                slot, view, ps, ph, pl, th, pf = po[i]
                tl = dve.do(lambda e: e.tensor_tensor(pl, view, ph.bitcast(F), ALU.subtract), th, pf)
                work.give(slot, th, tl)
                po[i] = (ps, ph, pl, [th, tl])

            def values(i):
                q, k, v, finish, sk, after, vafter = jobs[i]
                ps, ph, pl, tp = po[i]
                if i % 2 == 0:
                    oo[i // 2] = o_ring.take()
                slot, bank, free = oo[i // 2]
                o = bank[0:64, 256 * (i % 2):256 * (i % 2) + 256]
                pe.wait(tp, free, vafter())
                for kt in range(2):
                    vh, vl = v(kt)
                    for n, (a_, b_) in enumerate(((vh, ph), (vh, pl), (vl, ph))):
                        f = lambda e, a_=a_, b_=b_, kt=kt, n=n: e.matmul(o, a_, b_[:, kt, :], start=(kt == 0 and n == 0), stop=(kt == 1 and n == 2))
                        if kt == 1 and n == 2:
                            tv = pe.do(f)
                        else:
                            pe.quiet(f)
                p_ring.give(ps, tv)
                oo[i // 2] = (slot, bank, tv if i % 2 else free)

            def finished(i):
                if i % 2 == 1:
                    j = i // 2
                    slot, bank, tv = oo[j]
                    done = []
                    for u in range(2):
                        yh, yl = [x[64 * u:64 * u + 64, at[j], :] for x in y]
                        o = bank[0:64, 256 * u:256 * u + 256]
                        done.append(act.do(lambda e, o=o, yh=yh: e.activation(yh, o, ACT.Copy), tv))
                    for u in range(2):
                        yh, yl = [x[64 * u:64 * u + 64, at[j], :] for x in y]
                        o = bank[0:64, 256 * u:256 * u + 256]
                        done.append(dve.do(lambda e, o=o, yh=yh, yl=yl: e.tensor_tensor(yl, o, yh.bitcast(F), ALU.subtract), done[1]))
                    o_ring.give(slot, *done)
                    y_done[at[j]] = done

            n = len(jobs)

            def step(i):
                for work_of, late in ((finished, 5), (turn, 3), (scores, 0), (values, 4), (soften, 1), (high, 3), (normalise, 2), (exponentials, 1), (low, 3)):
                    if 0 <= i - late < n:
                        work_of(i - late)

            return [lambda i=i: step(i) for i in range(n + 6)]

        def queued(toks, i):
            while toks[i] is None:
                later.popleft()()
            return toks[i]

        def half_of(x, h, at=None):
            return [y[64 * (h % 2):64 * (h % 2) + 64, h // 2 if at is None else at, :] for y in x]

        def scaled_split(oh, ol, pair, c0, c1, rms, done, *after):
            toks = []
            for t in range(2):
                th = act.do(lambda e, t=t: e.activation(oh[:, t, :], pair[t][:, c0:c1], ACT.Copy, scale=rms.r[t]), done, rms.done, *after)
                toks.append(dve.do(lambda e, t=t: e.scalar_tensor_tensor(out=ol[:, t, :], in0=pair[t][:, c0:c1], scalar=rms.r[t], in1=oh[:, t, :].bitcast(F),
                                                                         op0=ALU.mult, op1=ALU.subtract), th, *after))
            return [th] + toks

        def scaled_copy(o, pair, c0, c1, rms, done, *after):
            t0 = act.do(lambda e: e.activation(o[:, 0, :], pair[0][:, c0:c1], ACT.Copy, scale=rms.r[0]), done, rms.done, *after)
            t1 = dve.do(lambda e: e.tensor_scalar(o[:, 1, :], pair[1][:, c0:c1], rms.r[1], None, ALU.mult), done, rms.done, *after)
            return [t0, t1]

        scopes = [ExitStack(), ExitStack()]
        mkT, mv = {}, {}
        for l in (1, 0):
            mkT[l] = [sb(f"mkT{n}{l}", [128, 2, 256], R, scopes[l]) for n in "hl"]
            mv[l] = [sb(f"mv{n}{l}", [128, 2, 256], R, scopes[l]) for n in "hl"]
        first = ExitStack()
        mstage = [sb(f"mstage{l}", [128, 2, 256], F, first) for l in range(2)]
        memTh = sb("memTh", [128, 8, 256], R, first)
        memTl = sb("memTl", [128, 8, 256], R, first)
        mt = [None] * 8
        mrms = Rms(next(roots))
        for k in range(0, 8, 2):
            split_through(min(k // 2, SPLITS - 1))
            turn_piece(memx, k * 128, 2, memTh, memTl, k, mt, t_mem, None, memgain, t_norm["mem"])

        def squares():
            for j in range(2):
                for t in range(2):
                    mrms.square(memx[:, t, j * 512:(j + 1) * 512], t, j, t_mem)
            mrms.root()
        later.append(squares)
        later.append(turn_rows)

        class Input:

            def __init__(self, gain, before):
                self.t, self.gain, self.before, self.turned = [None] * 8, gain, before, None
                self.rms = Rms(next(roots))

            def pieces(self, j, after):
                for k in range(4 * j, 4 * j + 4, 2):
                    def piece(k=k):
                        self.turned = turn_piece(xres, k * 128, 2, xTh, xTl, k, self.t, after, self.before, self.gain, t_norm["cols"])
                    later.append(piece)

                def squares():
                    for t in range(2):
                        self.rms.square(xres[:, t, j * 512:(j + 1) * 512], t, j, after)
                    if j == 1:
                        self.rms.root()
                later.append(squares)

        x_in = Input(col(0), None)
        for j in range(2):
            x_in.pieces(j, t_x)
        t_mkT, t_mv = {}, {}
        for l in range(2):
            def evac(pair, done, l=l):
                ts = scaled_copy(mstage[l], pair, 0, 256, mrms, done)
                tv = scaled_split(mv[l][0], mv[l][1], pair, 256, 512, mrms, done, *ts)
                t_mv[l] = tv

                def piece():
                    t_mkT[l], _ = pairs_piece(mstage[l], 0, 2, mkT[l], 0, 1.0, ts, None)
                later.append(piece)
                return ts + tv
            done = linear("mem", 2 if l else len(FIRST), memTh, memTl, mt, evac, 2 * l)
        drain_later()
        first.close()
        t_first = fence()

        rate = small[:, 136:144]
        t_small = {}

        def small_vectors():
            lam = col(15)
            sp_ = [small[:, 96 + 8 * i:104 + 8 * i] for i in range(6)]
            t = dve.do(lambda e: e.scalar_tensor_tensor(out=sp_[0], in0=lam, scalar=-1.0, in1=lam, op0=ALU.mult, op1=ALU.min), t_norm["cols"])
            t = act.do(lambda e: e.activation(sp_[1], sp_[0], ACT.Exp), t)
            t = dve.do(lambda e: e.tensor_scalar(sp_[2], sp_[1], 2.0, None, ALU.add), t)
            t = dve.do(lambda e: e.reciprocal(sp_[3], sp_[2]), t)
            t = dve.do(lambda e: e.tensor_tensor(sp_[1], sp_[1], sp_[3], ALU.mult), t)
            t = dve.do(lambda e: e.tensor_tensor(sp_[2], sp_[1], sp_[1], ALU.mult), t)
            t = dve.do(lambda e: e.tensor_scalar(sp_[3], sp_[2], 1.0 / 17, 1.0 / 15, ALU.mult, ALU.add), t)
            for n in (13, 11, 9, 7, 5, 3, 1):
                t = dve.do(lambda e: e.tensor_tensor(sp_[3], sp_[3], sp_[2], ALU.mult), t)
                t = dve.do(lambda e, n=n: e.tensor_scalar(sp_[3], sp_[3], 1.0 / n, None, ALU.add), t)
            t = dve.do(lambda e: e.tensor_tensor(sp_[3], sp_[3], sp_[1], ALU.mult), t)
            t = dve.do(lambda e: e.tensor_scalar(sp_[4], lam, -1.0, 0.0, ALU.mult, ALU.max), t)
            t = dve.do(lambda e: e.scalar_tensor_tensor(out=sp_[5], in0=sp_[3], scalar=2.0, in1=sp_[4], op0=ALU.mult, op1=ALU.add), t)
            t_small["rate"] = dve.do(lambda e: e.tensor_scalar(sp_[5], sp_[5], -8.0, None, ALU.mult), t)

        bias = big[:, :].rearrange("p (h t k) -> p h t k", h=12, t=2)
        PITCH = 12 * 15 * 31
        t_bias = {}

        def neighbourhood_bias(after):
            t_rep = scrsem.load(pool, a["scratch_rpb"], bass.AP(a["rpb_b"].tensor, 0, [[0, 64], [1, PITCH]]), after)
            for rr in range(4):
                for i in range(4):
                    src = bass.AP(a["scratch_rpb"].tensor, (i - rr + 7) * 31 + 15, [[PITCH - 1, 64], [15 * 31, 12], [1, 64]])
                    t = rpbsem.load(pool, bias[(rr % 2) * 64:(rr % 2) * 64 + 64, :, rr // 2, i * 64:(i + 1) * 64], src, t_rep)
            for h in range(12):
                for n in range(2):
                    t_bias["t"] = pool.do(lambda e, h=h, n=n: e.tensor_tensor(bias[:, h, n, :], bias[:, h, n, :], window, ALU.add), t, t_const)

        def add_residual(c, following):
            def evac(pair, done):
                toks = [dve.do(lambda e, t=t: e.tensor_tensor(xres[:, t, c:c + 512], pair[t][:, :], xres[:, t, c:c + 512], ALU.add), done, following.turned_before)
                        for t in range(2)]
                following.pieces(c // 512, toks)
                return toks
            return evac

        def mix(l, x_in, following):
            sc = ExitStack()
            t_f = t_first if l == 0 else fence()
            qy = [sb(f"qy{n}{l}", [128, 8, 256], R, sc) for n in "hl"]
            kT = [sb(f"kT{n}{l}", [128, 4 if l == 0 else 6, 256], R, sc) for n in "hl"]
            v = [sb(f"v{n}{l}", [128, 2, 256 if l == 0 else 768], R, sc) for n in "hl"]
            p_ring = Ring([[sb(f"p{n}{l}{i}", [128, 2, 256], R, sc)[:, :, :] for n in "hl"] for i in range(2)], later)
            stage = Ring([nrm[:, :, 0:512], nrm[:, :, 512:1024]], later)
            kd = gbc[:, :].rearrange("p (t d) -> p t d", t=2)
            if l == 0:
                s_slots = [big[:, 2560 + 512 * i:3072 + 512 * i].rearrange("p (t k) -> p t k", t=2) for i in range(4)]
            else:
                s_slots = [dist, kd[:, :, 0:256], kd[:, :, 256:512]]
            s_ring = Ring(s_slots, later)
            tq, tk, tv = [None] * 8, [None] * 6, {}
            rms = x_in.rms

            def staged(pieces, c0=0, c1=512):
                def evac(pair, done):
                    ss, s, sf = stage.take()
                    ts = scaled_copy(s[:, :, 0:c1 - c0], pair, c0, c1, rms, done, sf, t_f)
                    last = []
                    for i, (c, n, dst, at, scale, tok) in enumerate(pieces):
                        def piece(c=c, n=n, dst=dst, at=at, scale=scale, tok=tok, i=i):
                            t, tt = pairs_piece(s, c, n, dst, at, scale, ts, t_f)
                            for j in range(n):
                                tok[at + j] = t
                            if i == len(pieces) - 1:
                                stage.give(ss, tt)
                        later.append(piece)
                    return ts
                return evac

            def scale_q(*at):
                return [(256 * i, 2, qy, j, 0.125, tq) for i, j in enumerate(at)]

            def evac_k(pair, done):
                ss, s, sf = stage.take()
                ts = scaled_copy(s[:, :, :], pair, 0, 512, rms, done, sf, t_f)
                td = []
                for t in range(2):
                    for u in range(2):
                        f = lambda e, t=t, u=u: e.tensor_copy(
                            kd[:, t, :].rearrange("p (h u d) -> p h u d", h=4, u=2)[:, :, u, :],
                            s[:, t, 256:512].rearrange("p (h d) -> p h d", h=4))
                        td.append(dve.do(f, ts, t_f) if u else pool.do(f, ts, t_f))

                def piece_q():
                    tq[4], tt = pairs_piece(s, 0, 2, qy, 4, 0.125, ts, t_f)
                    tq[5] = tq[4]
                    stage.give(ss, tt, *td)
                later.append(piece_q)
                for k in (0, 2):
                    def piece_k(k=k):
                        tk[k], _ = pairs_piece(kd, k * 128, 2, kT, k, 1.0, td, t_f)
                        tk[k + 1] = tk[k]
                    later.append(piece_k)
                return ts

            def evac_v(pair, done):
                tv["first"] = scaled_split(v[0][:, :, 0:512], v[1][:, :, 0:512], pair, 0, 512, rms, done, t_f)
                return tv["first"]

            nv = 256 if l == 0 else 768
            qm_evac = staged([(0, 2, qy, 6, 0.125, tq)], 256, 512)

            def evac_vm(pair, done):
                tv["last"] = scaled_split(v[0][:, :, nv - 256:nv], v[1][:, :, nv - 256:nv], pair, 0, 256, rms, done, t_f)
                return tv["last"] + qm_evac(pair, [done] + tv["last"])

            k4 = lambda c, at: (c, 2, kT, at, 1.0, tk)
            evacs = {1024: evac_vm, 512: evac_k, 0: staged(scale_q(0, 2))} if l == 0 else {
                2048: evac_vm, 1536: evac_v, 512: staged(scale_q(4) + [k4(256, 0)]), 1024: staged([k4(0, 2), k4(256, 4)]), 0: staged(scale_q(0, 2))}
            jobs = []
            slopes = [2.0 ** (-8.0 * (h + 1) / 12) for h in range(12)]
            for h in range(12):
                if l == 0:
                    def finish(s, ps, tok, sf, h=h):
                        t = dve.do(lambda e: e.scalar_tensor_tensor(out=s[:, :, :], in0=dist, scalar=-slopes[h], in1=ps, op0=ALU.mult, op1=ALU.add),
                                   tok, sf, t_f, t_const)
                        return t, t
                    kv = h // 3
                    jobs.append((half_of(qy, h), half_of(kT, h, kv), lambda kt, kv=kv: [x[:, kt, kv * 64:(kv + 1) * 64] for x in v],
                                 finish, sink[:, h:h + 1], lambda h=h, kv=kv: [queued(tq, h // 2), queued(tk, kv)], lambda: tv["last"]))
                else:
                    def finish(s, ps, tok, sf, h=h):
                        t = dve.do(lambda e: e.tensor_tensor(s[:, :, :], ps, bias[:, h, :, :], ALU.add), tok, sf, t_f, t_bias["t"])
                        return t, t
                    jobs.append((half_of(qy, h), half_of(kT, h), lambda kt, h=h: [x[:, kt, h * 64:(h + 1) * 64] for x in v],
                                 finish, None, lambda h=h: [queued(tq, h // 2), queued(tk, h // 2)], lambda h=h: tv["first" if h < 8 else "last"]))
            for h in range(4):
                jobs.append((half_of(qy, 12 + h), half_of(mkT[l], h), lambda kt, h=h: [x[:, kt, h * 64:(h + 1) * 64] for x in mv[l]],
                             None, None, lambda h=h: [queued(tq, 6 + h // 2), t_mkT[l]], lambda: t_mv[l]))
            turns = [12, 13, 14, 15, 8, 9, 10, 11, 0, 1, 2, 3, 4, 5, 6, 7]
            yt = [None] * 8
            steps = deque(softmax_steps([jobs[h] for h in turns], s_ring, p_ring, work, qy, [h // 2 for h in turns[::2]], yt))
            for n, (c, heads) in enumerate(MIX_TILES[l]):
                x_done = linear("in", 2, xTh, xTl, x_in.t, evacs[c], 2)
                for _ in range(heads):
                    later.append(steps.popleft())
            following.before = x_done
            following.turned_before = x_in.turned
            drain_later()
            while steps:
                steps.popleft()()
            for c in (0, 512):
                done = linear("out", 2, qy[0], qy[1], yt, add_residual(c, following))
            sc.close()
            return done

        def ffn(l, x_in, finish, t_f):
            sc = ExitStack()
            hTh = sb(f"hTh{l}", [128, 22, 256], R, sc)
            hTl = sb(f"hTl{l}", [128, 22, 256], R, sc)
            ht = [None] * 22
            rms = x_in.rms
            keep = {"m": t_f, "turned": t_f, "left": 0}
            for c, w in tiles_of(DFF):
                parts = 2 if w == 512 else 1
                tg = []

                def gate(pair, done, w=w, tg=tg):
                    for t in range(2):
                        tg.append(act.do(lambda e, t=t: e.activation(nrm[:, t, 0:w], pair[t][:, 0:w], ACT.Silu, scale=rms.r[t]),
                                         done, keep["m"], rms.done))
                    return tg

                def up(pair, done, w=w, c=c, tg=tg):
                    while keep["left"]:
                        later.popleft()()
                    tm = [dve.do(lambda e, t=t: e.scalar_tensor_tensor(out=nrm[:, t, 512:512 + w], in0=pair[t][:, 0:w], scalar=rms.r[t],
                                                                       in1=nrm[:, t, 0:w], op0=ALU.mult, op1=ALU.mult),
                                 done, tg, keep["turned"], rms.done) for t in range(2)]
                    keep["m"] = tm
                    for k in range(0, w // 128, 2):
                        keep["left"] += 1

                        def piece(k=k, c=c):
                            keep["turned"] = turn_piece(nrm, 512 + k * 128, 2, hTh, hTl, c // 128 + k, ht, tm, t_f)
                            keep["left"] -= 1
                        later.append(piece)
                    return tm
                linear(f"gu{l}", parts, xTh, xTl, x_in.t, gate)
                x_done = linear(f"gu{l}", parts, xTh, xTl, x_in.t, up)
            finish(x_done, x_in.turned)
            for j, c in enumerate((0, 512)):
                done = linear(f"down{l}", 6, hTh, hTl, ht, finish.evac(c))
            sc.close()
            return done

        class ToInput:

            def __init__(self, following):
                self.following = following

            def __call__(self, x_done, turned):
                self.following.before, self.following.turned_before = x_done, turned

            def evac(self, c):
                return add_residual(c, self.following)

        in_f0, in_m1, in_f1 = (Input(col(i), None) for i in (2, 1, 3))
        mix(0, x_in, in_f0)
        scopes[0].close()
        t_f = fence()
        later.append(lambda t_f=t_f: neighbourhood_bias(t_f))
        ffn(0, in_f0, ToInput(in_m1), t_f)
        small_vectors()
        mix(1, in_m1, in_f1)
        drain_later()
        scopes[1].close()

        t_f = fence()
        t0 = act.do(lambda e: e.activation(small[:, 0:8], col(7), ACT.Silu), t_norm["cols"])
        tz = pool.do(lambda e: e.memset(big[:, :], 0.0), t_f)
        t_b = gsem.load(pool, big[0:1, :], a["b_ada_2"], tz)
        acc_tok["c"] = [t0, tz, t_b]
        t_g1 = side.load(pool, gbc[:, :], bass.AP(a["norm_final"].tensor, 0, [[0, 128], [1, D]]))

        class Last:
            def __call__(self, x_done, turned):
                self.before, self.turned = x_done, turned
                self.r1, self.r2, self.out = Rms(next(roots)), Rms(next(roots)), []

            def evac(self, c):
                def run(pair, done):
                    given = []
                    for t in range(2):
                        x = xres[:, t, c:c + 512]
                        t0 = dve.do(lambda e, t=t, x=x: e.tensor_tensor(x, pair[t][:, :], x, ALU.add), done, self.turned)
                        t1 = self.r1.square(x, t, c // 512, t0)
                        t2 = dve.do(lambda e, x=x: e.tensor_tensor(x, x, gbc[:, c:c + 512], ALU.mult), t0, t1, t_g1)
                        self.r2.square(x, t, c // 512, t2)
                        self.out.append(t2)
                        given.append(t0)
                    return given
                return run

        last = Last()
        ffn(1, in_f1, last, fence())
        drain_later()
        t_f = fence()
        t_acc = list(acc_tok["t"])
        last.r1.root()
        st, s2 = last.r1.st, last.r2.st
        t = dve.do(lambda e: e.tensor_tensor(s2[:, 4:6], s2[:, 0:2], s2[:, 2:4], ALU.add), last.r2.tokens)
        t = dve.do(lambda e: e.tensor_tensor(s2[:, 6:8], s2[:, 4:6], st[:, 8:10], ALU.mult), t, last.r1.done)
        t = dve.do(lambda e: e.tensor_tensor(s2[:, 4:6], s2[:, 6:8], st[:, 8:10], ALU.mult), t)
        t = dve.do(lambda e: e.tensor_scalar(s2[:, 6:8], s2[:, 4:6], 1.0 / D, EPS, ALU.mult, ALU.add), t)
        t = pool.do(lambda e: e.tensor_tensor(s2[:, 8:10], s2[:, 6:8], half_, ALU.pow), t, t_half)
        t_r12 = dve.do(lambda e: e.tensor_tensor(s2[:, 10:12], s2[:, 8:10], st[:, 8:10], ALU.mult), t)

        slot, bank, free = work.take()
        pe.wait(free, t_acc, t_ones)
        for n, base in enumerate((0, 1024, 3072, 4096)):
            for k in range(8):
                f = lambda e, n=n, k=k, b=base, bank=bank: e.matmul(bank[:, n * 8 + k:n * 8 + k + 1], big[:, b + k * 128:b + (k + 1) * 128],
                                                                    ones[:, 0:1], start=True, stop=True)
                tc = pe.do(f)
        mod = small[:, 32:64]
        t_mod = dve.do(lambda e, b=bank: e.tensor_copy(mod, b[:, 0:32]), tc)
        work.give(slot, t_mod)
        gates = big[:, 0:2048]
        gain1, gain2 = small[:, 64:72], small[:, 72:80]
        tg1 = dve.do(lambda e: e.scalar_tensor_tensor(out=gain1, in0=mod[:, 8:16], scalar=1.0, in1=col(5), op0=ALU.add, op1=ALU.mult), t_mod)
        tg2 = dve.do(lambda e: e.scalar_tensor_tensor(out=gain2, in0=mod[:, 24:32], scalar=1.0, in1=col(6), op0=ALU.add, op1=ALU.mult), t_mod)

        def normed(src, r, after, before):
            t0 = dve.do(lambda e: e.tensor_scalar(nrm[:, 0, :], src[:, 0, :], r[0], None, ALU.mult), after, before)
            t1 = act.do(lambda e: e.activation(nrm[:, 1, :], src[:, 1, :], ACT.Copy, scale=r[1]), after, before)
            return [t0, t1]

        sc = ExitStack()
        t_z = normed(xres, [s2[:, 10:11], s2[:, 11:12]], [t_r12, last.out], t_f)
        rTh = sb("rTh", [128, 8, 256], R, sc)
        rTl = sb("rTl", [128, 8, 256], R, sc)
        inner = ExitStack()
        acc = sb("acc", [128, 2, 256], F, inner)[:, :, :]
        left = sb("left", [128, 2, 256], F, inner)[:, :, :]
        sgb = sb("sgb", [128, 2, D], F, inner)
        rel = sb("rel", [32, 8], F, inner)
        stage = Ring([sb(f"stage{i}", [128, 2, 512], F, inner) for i in range(2)], later)
        wi = sb("wi", [128, 2, 8], F, inner)
        qy = [sb(f"q2y{n}", [128, 4, 256], R, inner) for n in "hl"]
        kT = [sb(f"k2T{n}", [128, 2, 256], R, inner) for n in "hl"]
        v2 = [sb(f"v2{n}", [128, 2, 128], R, inner) for n in "hl"]
        p_ring = Ring([[sb(f"p2{n}{i}", [128, 2, 256], R, inner)[:, :, :] for n in "hl"] for i in range(2)], later)
        temps = [big[:, 2048 + 1024 * i:3072 + 1024 * i].rearrange("p (k t) -> p k t", k=4) for i in range(4)]
        rg, ig = temps[2:]
        xcs = [temps[0], nrm[:, 0, :].rearrange("p (k t) -> p k t", k=4)]
        gls = [temps[1], nrm[:, 1, :].rearrange("p (k t) -> p k t", k=4)]
        tmp_ring = Ring([gls[0][:, i, :] for i in range(4)], later)
        tmp_ring.free = [[tc] for _ in range(4)]
        xt, xt_turned = [None] * 8, {}
        for k in range(0, 8, 2):
            def piece(k=k):
                xt_turned["t"] = turn_piece(nrm, k * 128, 2, xTh, xTl, k, xt, t_z, [last.before, t_f, tg1, t_mod], gain1, tg1, mod[:, 0:8], tmp_ring)
            piece()
        gb = []
        for n, base in enumerate((2048, 2560, 5120, 5632)):
            slot, bank, free = work.take()
            tc = pe.do(lambda e, b=base, bank=bank: e.matmul(bank[:, :], ones[:, :], big[:, b:b + 512], start=True, stop=True), free, t_acc)
            gb.append((slot, bank, tc))
        t_gate = []
        for n, (slot, bank, tc) in enumerate(gb):
            t_gate.append(act.do(lambda e, n=n, b=bank: e.activation(gates[:, n * 512:(n + 1) * 512], b[:, :], ACT.Copy), tc, gb[-1][2]))
            work.give(slot, t_gate[-1])
        t_big = [tc, t_gate]
        t_x1 = [dve.do(lambda e, t=t: e.tensor_scalar(xres[:, t, :], xres[:, t, :], last.r1.r[t], None, ALU.mult), last.r1.done, t_z) for t in range(2)]

        onehot = acc[0:32, :, :].rearrange("p t k -> p (t k)")
        relrow = left[0:8, :, :].rearrange("p t k -> p (t k)")
        t_rel = relsem.load(pool, rel[:, :], a["rel_bias_2"], t_f)
        t_rel = relsem.load(pool, onehot, a["onehot"], t_f)
        wrg = sgb[:, :, :].rearrange("p g (n d) -> p g n d", n=8)
        t_wg = gsem.load(pool, wrg[:, 0, :, :], a["w_rg_2"][0].rearrange("n c d -> c n d"), t_f)
        t_wg = gsem.load(pool, wrg[:, 1, :, :], a["w_ig_2"][0].rearrange("n c d -> c n d"), t_f)
        t_rb = {}

        def relative_rows():
            slot, bank, free = work.take()
            tb = pe.do(lambda e, b=bank: e.matmul(b[0:8, :], rel[:, :], onehot, start=True, stop=True), free, t_rel)
            tb = dve.do(lambda e, b=bank: e.tensor_copy(relrow, b[0:8, :]), tb, t_f)
            work.give(slot, tb)
            t_rb["row"] = tb
            t_rb["scr"] = scrsem.load(pool, bass.AP(a["scratch"].tensor, 0, [[512, 8], [4096, 128], [1, 512]]),
                                      relrow.unsqueeze(1).to_broadcast([8, 128, 512]), tb)
        named["rel"] = relative_rows

        brings = Ring([(gbc[:, i * 512:(i + 1) * 512], Landing(sem(f"d_brow{i}"))) for i in range(2)], later)
        with_row = [(k, c, w) for k, c, w, _ in IN2 if k != "yr"]
        rows_at = {"n": 0}
        loaded = []

        def bias_row():
            if rows_at["n"] < len(with_row):
                _, c, w = with_row[rows_at["n"]]
                rows_at["n"] += 1
                bs, (br, land), bf = brings.take()
                loaded.append((bs, br, land.load(pool, br[:, 0:w], bass.AP(a["b_in_2"].tensor, c, [[0, 128], [1, w]]), bf, t_f)))

        bias_row()
        bias_row()
        todo = list(IN2)

        def project(kind, target, then):
            what, c, w, between = todo.pop(0)
            assert what == kind

            def evac(pair, done):
                s, before, slot = target()
                if kind == "yr":
                    toks = [act.do(lambda e: e.activation(s[:, 0, 0:w], pair[0][:, 0:w], ACT.Copy), done, before, t_f),
                            dve.do(lambda e: e.tensor_copy(s[:, 1, 0:w], pair[1][:, 0:w]), done, before, t_f)]
                else:
                    bs, br, tb = loaded.pop(0)
                    toks = [dve.do(lambda e, t=t: e.tensor_tensor(s[:, t, 0:w], pair[t][:, 0:w], br[:, 0:w], ALU.add), done, tb, before, t_f)
                            for t in range(2)]
                    brings.give(bs, *toks)
                    bias_row()
                then(s, toks, slot)
                return toks
            return linear("in2", 1 if w <= 256 else 2, xTh, xTl, xt, evac, 0, between)

        def staged():
            slot, s, free = stage.take()
            return s, free, slot

        wrg_read, tcs, t_half_done = {}, {}, {-1: None}
        t_rt = [None] * 8

        def t_turned():
            return xt_turned["t"]

        def after_xr(half):
            xc = xcs[half]

            def then(s, ts, slot):
                tcs[half] = []
                for k in (0, 2):
                    def piece(k=k):
                        bs, bank, free = work.take()
                        tt = turn_blocks(bank, [s[:, t, (k + j) * 128:(k + j + 1) * 128] for j in range(2) for t in range(2)], ts, free)
                        for j in range(2):
                            kk = 4 * half + k + j
                            t = act.do(lambda e, o=xc[:, k + j, :], p=bank[:, j * 256:(j + 1) * 256], kk=kk:
                                       e.activation(o, p, ACT.Identity, bias=col(12)[:, kk:kk + 1], scale=col(11)[:, kk:kk + 1]),
                                       tt, t_z if half else xt, t_turned(), t_big)
                        for j in range(2):
                            kk = 4 * half + k + j
                            for n in (1, 2, 3):
                                t = dve.do(lambda e, o=xc[:, k + j, :], p=bank[:, j * 256:(j + 1) * 256], n=n, kk=kk: e.scalar_tensor_tensor(
                                    out=o[:, n:], in0=p[:, 0:256 - n], scalar=col(11 - n)[:, kk:kk + 1], in1=o[:, n:], op0=ALU.mult, op1=ALU.add), t)
                            tcs[half].append(t)
                        work.give(bs, t)
                        if k == 2:
                            stage.give(slot, tt)
                    named[f"conv{half}{k}"] = piece
            return then

        def after_yr(half):
            xc, gl = xcs[half], gls[half]

            def then(s, ts, slot):
                hold = {}
                for k in (0, 2):
                    def piece(k=k):
                        bs, bank, free = work.take()
                        tt = turn_blocks(bank, [s[:, t, (k + j) * 128:(k + j + 1) * 128] for j in range(2) for t in range(2)], ts, free)
                        for j in range(2):
                            kk = 4 * half + k + j
                            t = act.do(lambda e, o=gl[:, k + j, :], p=bank[:, j * 256:(j + 1) * 256], kk=kk:
                                       e.activation(o, p, ACT.Gelu_apprx_tanh, bias=bias_yr[:, kk:kk + 1]), tt, xt, t_turned(), t_big)
                        work.give(bs, t)
                        hold["gl"] = t
                        if k == 2:
                            stage.give(slot, tt)
                    named[f"gelu{half}{k}"] = piece
                for n, dst in enumerate((rg, ig)):
                    for k in (0, 2):
                        def piece(n=n, dst=dst, k=k):
                            bs, bank, free = work.take()
                            pe.wait(free, tcs[half], t_wg)
                            for j in range(2):
                                kk = 4 * half + k + j
                                f = lambda e, j=j, kk=kk: e.matmul(bank[:, j * 256:(j + 1) * 256], wrg[:, n, kk, :], xc[:, k + j, :], start=True, stop=True)
                                tm = pe.do(f)
                            wrg_read[half] = tm
                            for j in range(2):
                                kk = 4 * half + k + j
                                t = act.do(lambda e, o=dst[:, k + j, :], p=bank[:, j * 256:(j + 1) * 256], b=col(13 + n)[:, kk:kk + 1]:
                                           e.activation(o, p, ACT.Sigmoid, bias=b), tm, t_half_done[half - 1], t_big)
                            work.give(bs, t)
                            hold[n] = t
                        named[f"gate{half}{n}{k}"] = piece

                def recurrence():
                    ti = pool.do(lambda e: e.tensor_tensor(ig, ig, xc, ALU.mult), hold[1])
                    ta_, tt_ = [], []
                    for k in range(4):
                        kk = 4 * half + k
                        ta_.append(act.do(lambda e, k=k, kk=kk: e.activation(xc[:, k, :], rg[:, k, :], ACT.Exp, scale=rate[:, kk:kk + 1]),
                                          hold[0], ti, t_small["rate"]))
                    for k in range(4):
                        kk = 4 * half + k
                        tt_.append(act.do(lambda e, k=k, kk=kk: e.activation(rg[:, k, :], rg[:, k, :], ACT.Tanh, scale=rate[:, kk:kk + 1]), ta_[k]))
                    hold["ti"], hold["a"], hold["m"] = ti, ta_, []
                    for j in range(2):
                        bs, bank, free = work.take()
                        square, tj = bank[:, :].rearrange("p (k t) -> p k t", k=2), rg[:, 2 * j:2 * j + 2, :]
                        t = act.do(lambda e, o=square, j=j: e.activation(o, xc[:, 2 * j:2 * j + 2, :], ACT.Square), ta_, free)
                        t = dve.do(lambda e, q=square, r=tj: e.scalar_tensor_tensor(out=r, in0=q, scalar=1.0, in1=r, op0=ALU.add, op1=ALU.mult), t, tt_)
                        work.give(bs, t)
                        hold["m"].append(t)

                def scan():
                    t3 = act.do(lambda e: e.activation(rg, rg, ACT.Sqrt, scale=-1.0), hold["m"])
                    t5 = dve.do(lambda e: e.tensor_tensor(ig, ig, rg, ALU.mult), t3, hold["ti"])
                    for k in range(4):
                        t6 = dve.do(lambda e, k=k: e.tensor_tensor_scan(rg[:, k, :], xc[:, k, :], ig[:, k, :], 0.0, ALU.mult, ALU.add), t5, hold["a"])
                    hold["h"] = pool.do(lambda e: e.tensor_tensor(gl, gl, rg, ALU.mult), t6, hold["gl"])

                def parts():
                    t7 = hold["h"]
                    o, lo = rTh[:, 4 * half:4 * half + 4, :], rTl[:, 4 * half:4 * half + 4, :]
                    th = act.do(lambda e: e.activation(o, gl, ACT.Copy), t7, t_f)
                    tl = dve.do(lambda e: e.tensor_tensor(lo, gl, o.bitcast(F), ALU.subtract), th, t_f)
                    for k in range(4):
                        t_rt[4 * half + k] = [th, tl]
                    t_half_done[half] = [th, tl, t7]
                named[f"rec{half}"], named[f"scan{half}"], named[f"half{half}"] = recurrence, scan, parts
            return then

        rbias = big[:, 2048:6144].rearrange("p (h t k) -> p h t k", h=8, t=2)

        def relative_bias(half):
            for t in range(2):
                src = bass.AP(a["scratch"].tensor, half * 2048 + 255 - 128 * t, [[4095, 128], [512, 4], [1, 256]])
                t_rb[half] = (relsem, rel1sem)[half].load(pool, rbias[:, 4 * half:4 * half + 4, t, :], src, t_rb["scr"], t_half_done[half])
        named["bias0"], named["bias1"] = lambda: relative_bias(0), lambda: relative_bias(1)

        def after_pairs(name, dst, tok, before):
            def then(s, ts, slot):
                for k in (0, 2):
                    def piece(k=k):
                        t, tt = pairs_piece(s, k * 128, 2, dst, k, 0.125, ts, before())
                        tok[k] = tok[k + 1] = t
                        if k == 2:
                            stage.give(slot, tt)
                    named[f"{name}{k}"] = piece
            return then

        tq, tqi, ta, tki = [None] * 4, [None] * 4, [None, None], {}
        rl_ring = Ring([dist, left], later)
        m8 = small[:, 160:176]

        def after_kw(s, ts, slot):
            tw = dve.do(lambda e: e.tensor_scalar(wi[:, :, :], s[:, :, 64:72], 8.0 ** -0.5, None, ALU.mult), ts, t_f)
            td = [dve.do(lambda e, u=u: e.tensor_copy(s[:, :, 128 + 64 * u:192 + 64 * u], s[:, :, 0:64]), ts) for u in range(2)]

            def piece():
                tki["t"], tt = pairs_piece(s, 128, 1, kT, 0, 1.0, td, t_f)
                stage.give(slot, tt, tw)
            named["ki"] = piece
            for h in range(8):
                def head(h=h):
                    bs, ps, tm = scores_of(half_of(qy, h), half_of(kT, h, 0), [tqi[h // 2], tki["t"]])
                    tki["read"] = tm
                    rs_, o, rf = rl_ring.take()
                    tr = act.do(lambda e: e.activation(o, ps, ACT.Relu), tm, rf, t_f, t_rb["scr"])
                    work.give(bs, tr)
                    for t in range(2):
                        if h == 0:
                            ta[t] = dve.do(lambda e, t=t: e.tensor_scalar(acc[:, t, :], o[:, t, :], wi[:, t, 0:1], None, ALU.mult), tr, tw, t_rb["row"])
                        else:
                            ta[t] = dve.do(lambda e, t=t: e.scalar_tensor_tensor(out=acc[:, t, :], in0=o[:, t, :], scalar=wi[:, t, h:h + 1],
                                                                                 in1=acc[:, t, :], op0=ALU.mult, op1=ALU.add), tr, ta[t])
                    rl_ring.give(rs_, *ta)
                named[f"h{h}"] = head

            best = {}

            def begin():
                t = dve.do(lambda e: e.tensor_tensor(left[:, :, :], acc[:, :, :], causal, ALU.add), ta, t_const, t_rb["scr"])
                best[0] = best[1] = t
            named["top"] = begin
            for n in range(8):
                def rounds():
                    tm = [dve.do(lambda e, t=t: e.max(m8[:, 8 * t:8 * t + 8], left[:, t, :]), best[t]) for t in range(2)]
                    for t in range(2):
                        best[t] = dve.do(lambda e, t=t: e.match_replace(left[:, t, :], m8[:, 8 * t:8 * t + 8], left[:, t, :], TAKEN), tm[t])
                named[f"top{n}"] = rounds

            def mask():
                t = dve.do(lambda e: e.tensor_scalar(acc[:, :, :], left[:, :, :], -1e38, BIG, ALU.is_le, ALU.mult), best[0], best[1])
                t_rb["mask"] = dve.do(lambda e: e.scalar_tensor_tensor(out=left[:, :, :], in0=acc[:, :, :], scalar=-BIG, in1=causal,
                                                                       op0=ALU.add, op1=ALU.add), t)
            named["mask"] = mask

        tkv = {}

        def after_kv(s, ts, slot):
            th = act.do(lambda e: e.activation(v2[0][:, :, :], s[:, :, 128:256], ACT.Copy), ts, t_f)
            tv = [th, dve.do(lambda e: e.tensor_tensor(v2[1][:, :, :], s[:, :, 128:256], v2[0][:, :, :].bitcast(F), ALU.subtract), th, t_f)]
            td = []
            for t in range(2):
                for u in range(2):
                    td.append(dve.do(lambda e, t=t, u=u: e.tensor_copy(
                        s[:, t, 256:512].rearrange("p (h u d) -> p h u d", h=2, u=2)[:, :, u, :],
                        s[:, t, 0:128].rearrange("p (h d) -> p h d", h=2)), ts))
            tkv["v"] = tv

            def piece():
                tkv["k"], tt = pairs_piece(s, 256, 2, kT, 0, 1.0, td, tki["read"])
                stage.give(slot, tt, *tv)
            named["kv"] = piece

        project("qi", staged, after_pairs("qi", qy, tqi, lambda: t_f))
        project("kw", staged, after_kw)
        for half in range(2):
            project("xr", staged, after_xr(half))
            project("yr", staged, after_yr(half))
        project("q", staged, after_pairs("q", qy, tq, lambda: tki["read"]))
        project("kv", staged, after_kv)

        yt = [None] * 4
        hold_y = {}

        def attention_begin():
            other_slot, other, of = stage.take()
            hold_y["other"] = other
            s_ring = Ring([dist, acc, other[:, :, 0:256], other[:, :, 256:512]], later)
            s_ring.free = [rl_ring.free[0], [t_rb["mask"]], list(of), list(of)]
            jobs, masked = [], {}
            for h in range(8):
                masked[h] = pool.do(lambda e, h=h: e.tensor_tensor(rbias[:, h, :, :], rbias[:, h, :, :], left, ALU.add), t_rb[h // 4], t_rb["mask"])
            for h in range(8):
                def finish(s, ps, tok, sf, h=h):
                    t = dve.do(lambda e: e.tensor_tensor(s[:, :, :], ps, rbias[:, h, :, :], ALU.add), tok, sf, masked[h], t_f)
                    return t, t
                kv = h // 4
                jobs.append((half_of(qy, h), half_of(kT, h, kv), lambda kt, kv=kv: [x[:, kt, kv * 64:(kv + 1) * 64] for x in v2],
                             finish, None, lambda h=h: [tq[h // 2], tkv["k"]], lambda: tkv["v"]))
            for n, step in enumerate(softmax_steps(jobs, s_ring, p_ring, work, qy, range(4), yt)):
                if n < 8:
                    named[f"s{n}"] = step
                else:
                    later.append(step)
        named["attend"] = attention_begin

        sga = nrm
        tga, tgb, tmb = [], [], []

        def gate_then(toks):
            return lambda s, ts, slot: toks.extend(ts)

        def sigmoids(s, toks):
            return [act.do(lambda e, t=t: e.activation(s[:, t, :], s[:, t, :], ACT.Sigmoid), toks) for t in range(2)]

        for c in (0, 512):
            project("gb", lambda c=c: (sgb[:, :, c:c + 512], wrg_read[1], None), gate_then(tgb))
        for c in (0, 512):
            project("ga", lambda c=c: (sga[:, :, c:c + 512], [xt_turned["t"], t_half_done[1]], None), gate_then(tga))
        for c in (0, 512):
            def evac(pair, done, c=c):
                if c == 0:
                    tgb[:] = sigmoids(sgb, tgb)
                last_ = [dve.do(lambda e, t=t: e.tensor_tensor(sgb[:, t, c:c + 512], pair[t][:, :], sgb[:, t, c:c + 512], ALU.mult), done, tgb)
                         for t in range(2)]
                tmb.extend(last_)
                return last_
            linear("orn", 2, rTh, rTl, t_rt, evac, 2)
        drain_later()
        tga[:] = sigmoids(sga, tga)
        merged = [None] * 8
        for c in (0, 512):
            def evac(pair, done, c=c):
                given, made = [], []
                for t in range(2):
                    m = dve.do(lambda e, t=t: e.tensor_tensor(sga[:, t, c:c + 512], pair[t][:, :], sga[:, t, c:c + 512], ALU.mult), done, tga)
                    given.append(m)
                    made.append(dve.do(lambda e, t=t: e.tensor_tensor(sga[:, t, c:c + 512], sga[:, t, c:c + 512], sgb[:, t, c:c + 512], ALU.add), m, tmb))
                for k in (0, 2):
                    later.append(lambda k=k, c=c: turn_piece(sga, c + k * 128, 2, rTh, rTl, c // 128 + k, merged, made, orn_done))
                return given
            if c == 0:
                orn_done = pe.now()
            linear("oat", 1, qy[0], qy[1], yt, evac)
        rms2 = Rms(next(roots))
        t_res = []
        other = hold_y["other"]
        t_o = fence()
        for c in (0, 512):
            def evac(pair, done, c=c):
                given = []
                for t in range(2):
                    x = xres[:, t, c:c + 512]
                    m = dve.do(lambda e, t=t: e.tensor_tensor(other[:, t, :], pair[t][:, :], gates[:, c:c + 512], ALU.mult), done, t_o, t_gate, t_res)
                    u = dve.do(lambda e, t=t, x=x: e.tensor_tensor(x, x, other[:, t, :], ALU.add), m, t_x1)
                    rms2.square(x, t, c // 512, u)
                    given.append(m)
                    t_res.append(u)
                return given
            done = linear("out2", 2, rTh, rTl, merged, evac)
        drain_later()
        inner.close()
        sc.close()

        t_f = fence()
        rms2.root()
        t_z = normed(xres, rms2.r, [rms2.done, t_res], t_f)
        hTh = sb("hTh2", [128, 22, 256], R, sc)
        hTl = sb("hTl2", [128, 22, 256], R, sc)
        tmp_ring = Ring([big[:, 2048 + 256 * i:2304 + 256 * i] for i in range(2)], later)
        t_g2 = side.load(pool, gbc[:, :], bass.AP(a["g_final_2"].tensor, 0, [[0, 128], [1, D]]), t_f)
        xt = [None] * 8
        for k in range(0, 8, 2):
            def piece(k=k):
                xt_turned["t"] = turn_piece(nrm, k * 128, 2, xTh, xTl, k, xt, t_z, [done, t_f, tg2], gain2, tg2, mod[:, 16:24], tmp_ring)
            piece()
        cring = Ring([big[:, 2560 + 512 * i:3072 + 512 * i].rearrange("p (k t) -> p k t", k=2) for i in range(6)], later)
        stage = Ring([nrm[:, :, 0:512], nrm[:, :, 512:1024]], later)
        ht = [None] * 22

        pending = deque()

        def flush():
            while pending:
                pending.popleft()()

        def convolved(s, k, kt, after):
            slot, bank, free = work.take()
            tt = turn_blocks(bank, [s[:, t, (k + j) * 128:(k + j + 1) * 128] for j in range(2) for t in range(2)], after, free)
            flush()
            cs, cv, cf = cring.take()
            last_ = []
            for j in range(2):
                t = act.do(lambda e, o=cv[:, j, :], p=bank[:, j * 256:(j + 1) * 256], q=kt + j:
                           e.activation(o, p, ACT.Identity, bias=CVB(q), scale=CVW(2, q)), tt, cf, t_f)
            for j in range(2):
                for n in (1, 2):
                    t = dve.do(lambda e, o=cv[:, j, :], p=bank[:, j * 256:(j + 1) * 256], n=n, q=kt + j: e.scalar_tensor_tensor(
                        out=o[:, n:], in0=p[:, 0:256 - n], scalar=CVW(2 - n, q), in1=o[:, n:], op0=ALU.mult, op1=ALU.add), t)
                last_.append(t)
            work.give(slot, *last_)
            return cs, cv, last_, tt

        def raw_tile(w, then):
            def evac(pair, done, c=c):
                ss, s, sf = stage.take()
                ts = [act.do(lambda e, t=t: e.activation(s[:, t, 0:w], pair[t][:, 0:w], ACT.Copy), done, sf, xt_turned["t"]) for t in range(2)]
                for k in range(0, w // 128, 2):
                    later.append(lambda k=k: then(ss, s, ts, k, k + 2 >= w // 128))
                return ts
            return linear("up2", 2 if w == 512 else 1, xTh, xTl, xt, evac)

        for c, w in UP2:
            made = {}

            def gate(ss, s, ts, k, end, c=c, made=made):
                cs, cv, tc, tt = convolved(s, k, 22 + c // 128 + k, ts)
                pending.append(lambda: made.update({k: (cs, cv, act.do(lambda e: e.activation(cv, cv, ACT.Silu), tc))}))
                if end:
                    stage.give(ss, tt)

            def value(ss, s, ts, k, end, c=c, made=made):
                cs, cv, tc, tt = convolved(s, k, c // 128 + k, ts)

                def rest():
                    gs, gv, tg = made[k]
                    t = pool.do(lambda e: e.tensor_tensor(cv, cv, gv, ALU.mult), tc, tg)
                    kt = c // 128 + k
                    o, lo = hTh[:, kt:kt + 2, :], hTl[:, kt:kt + 2, :]
                    th = act.do(lambda e: e.activation(o, cv, ACT.Copy), t, t_f)
                    tl = dve.do(lambda e: e.tensor_tensor(lo, cv, o.bitcast(F), ALU.subtract), th, t_f)
                    ht[kt] = ht[kt + 1] = [th, tl]
                    cring.give(gs, t)
                    cring.give(cs, th, tl)
                pending.append(rest)
                if end:
                    stage.give(ss, tt)
            raw_tile(w, gate)
            raw_tile(w, value)
        later.append(flush)
        rms3 = Rms(next(roots))
        t_res = []
        tmps = sb("lasttmp", [128, 2, 512], F, sc)
        for c in (0, 512):
            def evac(pair, done, c=c):
                given = []
                for t in range(2):
                    x = xres[:, t, c:c + 512]
                    m = dve.do(lambda e, t=t: e.tensor_tensor(tmps[:, t, :], pair[t][:, :], gates[:, 1024 + c:1536 + c], ALU.mult), done, t_res, t_f)
                    u = dve.do(lambda e, t=t, x=x: e.tensor_tensor(x, x, tmps[:, t, :], ALU.add), m)
                    rms3.square(x, t, c // 512, u)
                    given.append(m)
                    t_res.append(u)
                return given
            linear("down2", 6, hTh, hTl, ht, evac)
        drain_later()

        rms3.root()
        t_end = fence()
        for t in range(2):
            to = dve.do(lambda e, t=t: e.scalar_tensor_tensor(out=nrm[:, t, :], in0=xres[:, t, :], scalar=rms3.r[t], in1=gbc[:, :],
                                                              op0=ALU.mult, op1=ALU.mult), rms3.done, t_res, t_end, t_g2)
            t_out = outsem.load(sp, out[0, t * 128:(t + 1) * 128, :], nrm[:, t, :], to)
        sp.wait(t_out)
        pool.wait((scrsem.sem, scrsem.n))

        sc.close()
        block = ctx.enter_context(nc.Block())

        @block.sync
        def _(e):
            for f in sp.program:
                f(e)

        @block.scalar
        def _(e):
            for f in act.program:
                f(e)

        @block.vector
        def _(e):
            for f in dve.program:
                f(e)

        @block.gpsimd
        def _(e):
            for f in pool.program:
                f(e)

        @block.tensor
        def _(e):
            for f in pe.program:
                f(e)


def shape_constants():
    p = np.arange(128)
    key = np.arange(256)
    c = np.zeros((128, 1408), np.float32)
    c[:, 0:128] = np.eye(128)
    for t in range(2):
        q = p + 128 * t
        d = np.abs(q[:, None] - key[None, :])
        c[:, 128 + 256 * t:384 + 256 * t] = np.where(d <= 128, d, 1e33)
        c[:, 896 + 256 * t:1152 + 256 * t] = np.where(key[None, :] <= q[:, None], 0.0, -BIG)
    col, kcol = p % 64, key % 64
    start = np.clip(col - 8, 0, 48)
    inside = (kcol[None, :] >= start[:, None]) & (kcol[None, :] < start[:, None] + 16)
    c[:, 640:896] = np.where(inside, 0.0, -BIG)
    return c


def distance_buckets():
    n = np.arange(256)
    nf = np.maximum(n, 1).astype(np.float32)
    big = 16 + (np.log(nf / np.float32(16)) / np.float32(np.log(8.0)) * np.float32(16)).astype(np.int32)
    b = np.where(n < 16, n, np.minimum(big, 31))
    hot = np.zeros((32, 512), np.float32)
    hot[b[::-1], np.arange(256)] = 1.0
    hot[0, 256:] = 1.0
    return hot


def kernel(**inputs):
    import concourse.bacc as _bacc
    from concourse.bass_utils import run_bass_kernel_spmd as _run

    nc = _bacc.Bacc("TRN2", target_bir_lowering=False, num_devices=1)
    arrays, args = {}, {}
    given = {n: np.ascontiguousarray(v) for n, v in inputs.items()}
    given["constants"] = shape_constants()
    given["onehot"] = distance_buckets()
    for name, v in given.items():
        arrays[f"in_{name}"] = v
        args[name] = nc.dram_tensor(f"in_{name}", v.shape, mybir.dt.from_np(v.dtype), kind="ExternalInput").ap()
    args["scratch"] = nc.dram_tensor("scratch", (128, 8, 512), F, kind="Internal").ap()
    args["scratch_rpb"] = nc.dram_tensor("scratch_rpb", (64, 12 * 15 * 31), F, kind="Internal").ap()
    out = nc.dram_tensor("out_0", (1, 256, 1024), F, kind="ExternalOutput").ap()
    build(nc, args, out)
    r = _run(nc, [arrays], core_ids=[0])
    return r.results[0]["out_0"]
```

```python
from collections import deque
from contextlib import ExitStack

import numpy as np

import concourse.bass as bass
from concourse import mybir

F = mybir.dt.float32
R = mybir.dt.float32r
ALU = mybir.AluOpType
ACT = mybir.ActivationFunctionType
AX = mybir.AxisListType.X

D = 1024
DFF = 2816
EPS = 1e-6
BIG = 1e30
TAKEN = -3e38
RAWS, SPLITS = 4, 3
POOLED = ("gu1", "down1", "up2")


class Engine:

    def __init__(self, sem):
        self.sem, self.n, self.program, self.seen = sem, 0, [], {}

    def wait(self, *tokens):
        for t in tokens:
            if t is None:
                continue
            if isinstance(t, list):
                self.wait(*t)
                continue
            sem, value = t
            if self.seen.get(sem.name, 0) < value:
                self.seen[sem.name] = value
                self.program.append(lambda e, s=sem, v=value: e.wait_ge(s, v))

    def quiet(self, fn, *after):
        self.wait(*after)
        self.program.append(fn)

    def do(self, fn, *after):
        self.wait(*after)
        self.n += 1
        self.program.append(lambda e, f=fn, s=self.sem: f(e).then_inc(s, 1))
        return self.sem, self.n

    def now(self):
        return self.sem, self.n


class Landing:

    def __init__(self, sem):
        self.sem, self.n = sem, 0

    def load(self, queue, out, src, *after):
        queue.wait(*after)
        self.n += 16
        queue.program.append(lambda e, o=out, i=src, s=self.sem: e.dma_start(o, i).then_inc(s, 16))
        return self.sem, self.n


class Ring:

    def __init__(self, items, later):
        self.items, self.free, self.later = items, [[] for _ in items], later
        self.idle = deque(range(len(items)))

    def take(self):
        while not self.idle:
            self.later.popleft()()
        at = self.idle.popleft()
        after, self.free[at] = self.free[at], []
        return at, self.items[at], after

    def give(self, slot, *tokens):
        self.idle.append(slot)
        self.free[slot] += list(tokens)


def weight_parts(w, k0, nk, c0, nc_):
    return w[k0 * 128:(k0 + nk) * 128, c0:c0 + nc_].rearrange("(k p) n -> p k n", p=128)


def columns(w, c0, width):
    nk = w.shape[0] // 128
    step = min(nk, 2048 // width)
    return [(weight_parts(w, k, min(step, nk - k), c0, width), k, min(step, nk - k), width) for k in range(0, nk, step)]


def tiles_of(n):
    return [(c, min(512, n - c)) for c in range(0, n, 512)]


IN2 = [("qi", 768, 512, ["gates", "rel", ""]),
       ("kw", 1280, 72, ["qi0", "qi2", "x1"]),
       ("xr", 1352, 512, ["ki", "h0", "h1"]),
       ("yr", 2376, 512, ["conv00 h2", "conv02 h3", "h4 h5"]),
       ("xr", 1864, 512, ["gelu00 h6", "gelu02 gate000 h7", "gate002 top"]),
       ("yr", 2888, 512, ["gate010 gate012 top0", "conv10 top1", "rec0"]),
       ("q", 0, 512, ["conv12 top2", "gelu10 inc0 top3", "gelu12 scan0"]),
       ("kv", 512, 256, ["top4", "half0 bias0 q0 gate100 top5", "q2 gate102 gate110 gate112"]),
       ("gb", 4424, 512, ["kv top6 top7", "rec1 mask", "attend inc1 s0"]),
       ("gb", 4936, 512, ["s1 scan1", "s2", "half1 bias1"]),
       ("ga", 3400, 512, ["", "s3", "s4"]),
       ("ga", 3912, 512, ["s5", "s6", "s7"])]
MIX_TILES = [[(1024, 4, 2), (512, 4, 1), (0, 0, 1)], [(2048, 4, 2), (1536, 0, 1), (512, 0, 1), (1024, 4, 1), (0, 0, 1)]]
UP2 = tiles_of(DFF)[-1:] + tiles_of(DFF)[:-1]
FIRST = [(0, 1), (1, 1), (2, 2), (4, 4)]


def stream_plan(a):
    plan = []
    w = a["w_mem_kv"]
    plan += [("mem", (weight_parts(w[0], k, nk, 0, 512), k, nk, 512)) for k, nk in FIRST]

    def block(w_in, l):
        p = []
        for c, _, _ in MIX_TILES[l]:
            p += [("in", x) for x in columns(w_in, c, 512)]
        if l == 0:
            p += [("mem", x) for x in columns(a["w_mem_kv"][1], 0, 512)]
        for k in (4, 0):
            p += [("out", (weight_parts(a["w_out"][l], k, 4, c, 512), k, 4, 512)) for c in (0, 512)]
        for c, w in tiles_of(DFF):
            p += [(f"gu{l}", x) for x in columns(a["w_gate_up"][l], c, w)]
            p += [(f"gu{l}", x) for x in columns(a["w_gate_up"][l], DFF + c, w)]
        for c in (0, 512):
            p += [(f"down{l}", x) for x in columns(a["w_down"][l], c, 512)]
        return p

    plan += block(a["w_in_a"][0], 0)
    w_ada = a["w_ada_2"][0]
    ada = [("ada", (w_ada[k * 128:(k + 1) * 128, c * 2048:(c + 1) * 2048], k, c, 2048)) for k in range(8) for c in range(3)]
    n = 0
    for p in block(a["w_in_b"][0], 1):
        plan.append(p)
        if p[0] in ("gu1", "down1"):
            n += 1
            if n > 4 and n % 6 != 0 and ada:
                plan.append(ada.pop(0))
    assert not ada
    for _, c, w, _ in IN2:
        plan += [("in2", x) for x in columns(a["w_in_2"][0], c, w)]
    for kind, w in (("orn", "w_o_rnn_2"), ("oat", "w_o_attn_2"), ("out2", "w_out_2")):
        for c in (0, 512):
            plan += [(kind, x) for x in columns(a[w][0], c, 512)]
    for c, w in UP2:
        plan += [("up2", x) for x in columns(a["w_up_2"][0], DFF + c, w)]
        plan += [("up2", x) for x in columns(a["w_up_2"][0], c, w)]
    for c in (0, 512):
        plan += [("down2", x) for x in columns(a["w_down_2"][0], c, 512)]
    return plan


def build(nc, a, out):
    ctx = ExitStack()
    with ctx:
        def sb(name, shape, dt=F, scope=ctx):
            return scope.enter_context(nc.sbuf_tensor(name, shape, dt))

        def sem(name):
            return ctx.enter_context(nc.semaphore(name))

        pe, act, dve, pool, sp = (Engine(sem(n)) for n in ("s_pe", "s_act", "s_dve", "s_pool", "s_sp"))
        banks = [ctx.enter_context(nc.psum_tensor(f"bank{i}", [128, 512], F)) for i in range(8)]
        later = deque()

        def drain_later():
            while later:
                later.popleft()()

        raw = [sb(f"raw{i}", [128, 2048]) for i in range(RAWS)]
        hi_s = [sb(f"hi{i}", [128, 2048], R) for i in range(SPLITS)]
        lo_s = [sb(f"lo{i}", [128, 2048], R) for i in range(SPLITS)]
        xres = sb("xres", [128, 2, D])
        nrm = sb("nrm", [128, 2, D])
        xTh = sb("xTh", [128, 8, 256], R)
        xTl = sb("xTl", [128, 8, 256], R)
        const = sb("const", [128, 1408])
        ident = const[:, 0:128]
        dist = const[:, 128:640].rearrange("p (t k) -> p t k", t=2)
        window = const[:, 640:896]
        causal = const[:, 896:1408].rearrange("p (t k) -> p t k", t=2)
        gbc = sb("gbc", [128, D])
        keep = sb("keep", [128, 8, 256], R)
        cols = sb("cols", [128, 128 + 96 + 88])
        small = sb("small", [128, 176])
        junk = sb("junk", [128, 512], mybir.dt.bfloat16)
        junk_done = {"t": None}
        ones = sb("ones", [128, 128])
        stats = [sb(f"stat{i}", [128, 16]) for i in range(4)]
        rmss = [sb(f"rms{i}", [128, 16]) for i in range(9)]
        opening = ExitStack()
        early = sb("early", [128, 3584], F, opening)
        rows = early[:, 2048:2432].rearrange("p (n d) -> p n d", n=3)

        memsem, nmsem, xsem, rowsem, idsem, consem = (Landing(sem(n)) for n in ("d_mem", "d_norm", "d_x", "d_rows", "d_ident", "d_const"))
        side, rpbsem, relsem, rel1sem, gsem, scrsem, outsem = (Landing(sem(n)) for n in ("d_side", "d_rpb", "d_rel", "d_rel1", "d_g", "d_scr", "d_out"))

        plan = stream_plan(a)
        slots = [Landing(sem(f"d_raw{i}")) for i in range(RAWS)]
        landed, raw_free, ready, released = {}, {}, {}, {}
        state = {"dma": 0, "split": 0, "use": 0, "owed": 0}
        order = [i for i, p in enumerate(plan) if p[0] != "ada"]
        number = {i: m for m, i in enumerate(order)}
        acc_tok = {"t": [None, None, None], "c": None}

        def issue(upto):
            while state["dma"] < min(upto, len(plan)):
                i = state["dma"]
                kind, (src, k0, nk, w) = plan[i]
                dst = raw[i % RAWS][:, 0:2048 if kind == "ada" else nk * w]
                if kind != "ada":
                    dst = dst.rearrange("p (k n) -> p k n", k=nk)
                landed[i] = slots[i % RAWS].load(sp, dst, src, raw_free.get(i - RAWS))
                state["dma"] += 1

        def split(i):
            kind, (_, k0, nk, w) = plan[i]
            if kind == "ada":
                acc = big[:, nk * 2048:(nk + 1) * 2048]
                t = dve.do(lambda e: e.scalar_tensor_tensor(out=acc, in0=raw[i % RAWS][:, :], scalar=small[:, k0:k0 + 1], in1=acc,
                                                            op0=ALU.mult, op1=ALU.add), landed[i], acc_tok["t"][nk], acc_tok["c"])
                acc_tok["t"][nk] = t
                raw_free[i] = [t]
                return
            m = number[i]
            s, n = m % SPLITS, nk * w
            src, h, lo = raw[i % RAWS][:, 0:n], hi_s[s][:, 0:n], lo_s[s][:, 0:n]
            before = released.get(m - SPLITS)
            th = act.do(lambda e: e.activation(h, src, ACT.Copy), landed[i], before)
            engine = pool if m % 3 == 2 and kind in POOLED else dve
            tl = engine.do(lambda e: e.tensor_tensor(lo, src, h.bitcast(F), ALU.subtract), th, landed[i], before)
            raw_free[i] = [th, tl]
            ready[m] = [th, tl]

        def split_through(m):
            upto = order[min(m, len(order) - 1)]
            while state["split"] <= upto:
                issue(state["split"] + 1)
                split(state["split"])
                state["split"] += 1
                issue(state["split"] + RAWS)

        work = Ring(banks, later)

        def pop(n):
            for _ in range(n):
                if later:
                    later.popleft()()

        def run(names):
            for x in names:
                named[x]()

        named = {}

        def part(kind, taken, xh, xl, xt, begin, end, between):
            m = state["use"]
            state["use"] += 1
            what, (_, k0, nk, w) = plan[order[m]]
            assert what == kind, (what, kind)
            h, lo = [x[m % SPLITS][:, 0:nk * w].rearrange("p (k n) -> p k n", k=nk) for x in (hi_s, lo_s)]
            pe.wait(ready[m])
            done = []
            for n, (t, k) in enumerate((t, k) for t in range(2) for k in range(nk)):
                while xt[k0 + k] is None:
                    later.popleft()()
                _, bank, free = taken[t]
                pe.wait(xt[k0 + k], free)
                o = bank[:, 0:w]
                sh, sl = xh[:, k0 + k, t * 128:(t + 1) * 128], xl[:, k0 + k, t * 128:(t + 1) * 128]
                first_, last_ = begin and k == 0, end and k == nk - 1
                pe.quiet(lambda e, o=o, s=sh, x=h[:, k, :], b=first_: e.matmul(o, s, x, start=b, stop=False))
                pe.quiet(lambda e, o=o, s=sh, x=lo[:, k, :]: e.matmul(o, s, x, start=False, stop=False))
                f = lambda e, o=o, s=sl, x=h[:, k, :], d=last_: e.matmul(o, s, x, start=False, stop=d)
                if k == nk - 1:
                    done.append(pe.do(f))
                else:
                    pe.quiet(f)
                if n == min(3, 2 * nk - 1):
                    split_through(state["owed"])
                if n % 4 == 3 and n < 2 * nk - 1:
                    between()
            released[m] = done[1]
            state["owed"] = m + SPLITS
            return done

        def evacuated(taken, evacuate, done):
            for (slot, _, _), t in zip(taken, evacuate([bank for _, bank, _ in taken], done)):
                work.give(slot, t)

        def linear(kind, parts, xh, xl, xt, evacuate, pops=1, hooks=None):
            taken = [work.take() for _ in range(2)]
            hooks = deque(hooks or [])

            def between():
                if hooks:
                    run(hooks.popleft().split())
                else:
                    pop(pops)

            for p in range(parts):
                done = part(kind, taken, xh, xl, xt, p == 0, p == parts - 1, between)
                if p == parts - 1:
                    evacuated(taken, evacuate, done)
                else:
                    between()
            return done[1]

        def turn_blocks(bank, blocks, *after):
            pe.wait(*after)
            for i, x in enumerate(blocks):
                f = lambda e, x=x, o=bank[:, i * 128:(i + 1) * 128]: e.transpose(o, x, ident)
                if i == len(blocks) - 1:
                    return pe.do(f)
                pe.quiet(f)

        def turn_piece(src, c0, n, dh, dl, k0, xt, after, before, gain=None, t_gain=None):
            slot, bank, free = work.take()
            turned = turn_blocks(bank, [src[:, t, c0 + j * 128:c0 + (j + 1) * 128] for j in range(n) for t in range(2)], after, free, t_ident)
            view = bank[:, 0:n * 256].rearrange("p (k t) -> p k t", k=n)
            if gain is None:
                o, lo = dh[:, k0:k0 + n, :], dl[:, k0:k0 + n, :]
                th = act.do(lambda e: e.activation(o, view, ACT.Copy), turned, before)
                tl = dve.do(lambda e: e.tensor_tensor(lo, view, o.bitcast(F), ALU.subtract), th, before)
                work.give(slot, th, tl)
                for j in range(n):
                    xt[k0 + j] = [th, tl]
                return turned
            parts = [(dh[:, k0 + j, :], dl[:, k0 + j, :], bank[:, j * 256:(j + 1) * 256], gain[:, k0 + j:k0 + j + 1], j) for j in range(n)]
            for o, lo, ps, g, j in parts:
                th = act.do(lambda e, o=o, p=ps, g=g: e.activation(o, p, ACT.Copy, scale=g), turned, before, t_gain)
            for o, lo, ps, g, j in parts:
                tl = dve.do(lambda e, o=lo, p=ps, g=g, h=o: e.scalar_tensor_tensor(
                    out=o, in0=p, scalar=g, in1=h.bitcast(F), op0=ALU.mult, op1=ALU.subtract), th, before, t_gain)
                xt[k0 + j] = [th, tl]
            work.give(slot, th, tl)
            return turned

        def turn_shifted(src, k0, xt, after, before, gain, t_gain, shift, tmp):
            made = []
            for k in (k0, k0 + 2):
                slot, bank, free = work.take()
                turned = turn_blocks(bank, [src[:, t, (k + j) * 128:(k + j + 1) * 128] for j in range(2) for t in range(2)], after, free)
                made.append((slot, bank, turned))
            z = []
            for i, (slot, bank, tt) in enumerate(made):
                for j in range(2):
                    k = k0 + 2 * i + j
                    ts, tb, tf = tmp.take()
                    ps, g, b = bank[:, j * 256:(j + 1) * 256], gain[:, k:k + 1], shift[:, k:k + 1]
                    if i == 0:
                        t0 = act.do(lambda e, o=tb, p=ps, g=g, b=b: e.activation(o, p, ACT.Identity, bias=b, scale=g), tt, tf, t_gain)
                    else:
                        t0 = dve.do(lambda e, o=tb, p=ps, g=g, b=b: e.tensor_scalar(o, p, g, b, ALU.mult, ALU.add), tt, tf, t_gain)
                    z.append((k, ts, tb, t0))
                work.give(slot, t0)
            ths = [act.do(lambda e, o=xTh[:, k, :], p=tb: e.activation(o, p, ACT.Copy), t0, before) for k, ts, tb, t0 in z]
            for (k, ts, tb, t0), th in zip(z, ths):
                tl = dve.do(lambda e, o=xTl[:, k, :], p=tb, h=xTh[:, k, :]: e.tensor_tensor(o, p, h.bitcast(F), ALU.subtract), th, before)
                tmp.give(ts, th, tl)
                xt[k] = [th, tl]
            return turned

        class Rms:

            def __init__(self, st):
                self.st, self.tokens, self.rooted = st, [], None
                self.r = [st[:, 8:9], st[:, 9:10]]

            def square(self, x, t, j, after):
                tok = act.do(lambda e: e.activation(junk[:, :], x, ACT.Square, accum_out=self.st[:, 2 * j + t:2 * j + t + 1]), after, junk_done["t"])
                junk_done["t"] = tok
                self.tokens.append(tok)
                return tok

            def root(self):
                st = self.st
                t = dve.do(lambda e: e.tensor_tensor(st[:, 4:6], st[:, 0:2], st[:, 2:4], ALU.add), self.tokens)
                t = dve.do(lambda e: e.tensor_scalar(st[:, 6:8], st[:, 4:6], 1.0 / D, EPS, ALU.mult, ALU.add), t)
                self.rooted = pool.do(lambda e: e.tensor_tensor(st[:, 8:10], st[:, 6:8], half_[:, :], ALU.pow), t, t_half)
                return self.rooted

            @property
            def done(self):
                while self.rooted is None:
                    later.popleft()()
                return self.rooted

        roots = iter(rmss)

        memx = early[:, 0:2048].rearrange("p (t d) -> p t d", t=2)
        t_mem = [memsem.load(sp, memx, a["mem"][0].rearrange("(t p) d -> p t d", p=128))]
        t_ident = idsem.load(act, ident, a["constants"][:, 0:128])
        memrow = early[0:8, 2432:2560]
        t_memrow = nmsem.load(act, memrow, a["norm_mem"].rearrange("(k p) -> k p", p=128))
        issue(RAWS)
        r = 0
        for name in ("norm_mix", "norm_ffn", "norm_mem", "g_mix_2", "g_ffn_2", "c_2", "conv_rnn_w_2", "conv_rnn_b_2", "b_rg_2", "b_ig_2", "lru_lambda_2"):
            v = a[name]
            if len(v.shape) == 3:
                v = v.rearrange("l n d -> (l n) d")
            v = v.rearrange("l (k p) -> (l k) p", p=128) if len(v.shape) == 2 else v.rearrange("(k p) -> k p", p=128)
            t_rows = rowsem.load(sp, rows[r:r + v.shape[0], 0, :], v)
            r += v.shape[0]
        assert r == 128
        cw = a["conv_ffn_w_2"][0].rearrange("n (k p) -> (n k) p", p=128)
        b_in = a["b_in_2"][0]
        t_rows = rowsem.load(sp, rows[0:88, 1, :], cw[0:88, :])
        t_rows = rowsem.load(sp, rows[88:96, 1, :], b_in[2376:3400].rearrange("(k p) -> k p", p=128))
        t_rows = rowsem.load(sp, rows[0:44, 2, :], cw[88:132, :])
        t_rows = rowsem.load(sp, rows[44:88, 2, :], a["conv_ffn_b_2"][0].rearrange("(k p) -> k p", p=128))
        sink = small[:, 16:28]
        t_rows = rowsem.load(sp, sink, bass.AP(a["sink_a"].tensor, 0, [[0, 128], [1, 12]]))
        t_x = xsem.load(sp, xres[:, :, :], a["x"][0].rearrange("(t p) d -> p t d", p=128))
        t_const = consem.load(pool, const[:, 128:1408], a["constants"][:, 128:1408])
        half_ = small[:, 8:10]
        t_half = pool.do(lambda e: e.memset(half_, -0.5))
        t_ones = pool.do(lambda e: e.memset(ones[:, :], 1.0))

        slot, bank, free = work.take()
        tt = pe.do(lambda e, b=bank: e.transpose(b[:, 0:8], memrow, ident[0:8, 0:8]), free, t_memrow, t_ident)
        memgain = small[:, 144:152]
        t_norm = {"mem": dve.do(lambda e, b=bank: e.tensor_copy(memgain, b[:, 0:8]), tt)}
        work.give(slot, t_norm["mem"])

        def turn_rows():
            slot, bank, free = work.take()
            at = 0
            pe.wait(free, t_rows)
            for i, n in enumerate((128, 96, 88)):
                tt = pe.do(lambda e, b=bank, i=i, n=n, at=at: e.transpose(b[:, at:at + n], rows[0:n, i, :], ident[0:n, 0:n]))
                at += n
            t_norm["cols"] = dve.do(lambda e, b=bank: e.tensor_copy(cols[:, :], b[:, 0:312]), tt)
            work.give(slot, t_norm["cols"])

        def col(i):
            return cols[:, 8 * i:8 * i + 8]

        CVW = lambda n, kt: cols[:, 128 + 44 * n + kt:129 + 44 * n + kt] if n < 2 else cols[:, 224 + kt:225 + kt]
        CVB = lambda kt: cols[:, 268 + kt:269 + kt]
        bias_yr = cols[:, 216:224]

        def fence():
            return [e.now() for e in (pe, act, dve, pool)]

        def pairs_piece(src, c0, n, dst, at, scale, after, before):
            slot, bank, free = work.take()
            tt = turn_blocks(bank, [src[:, t, c0 + j * 128:c0 + (j + 1) * 128] for j in range(n) for t in range(2)], after, free, t_ident)
            view = bank[:, 0:n * 256].rearrange("p (k t) -> p k t", k=n)
            o, lo = dst[0][:, at:at + n, :], dst[1][:, at:at + n, :]
            th = act.do(lambda e: e.activation(o, view, ACT.Copy, scale=scale), tt, before)
            tl = dve.do(lambda e: e.scalar_tensor_tensor(out=lo, in0=view, scalar=scale, in1=o.bitcast(F), op0=ALU.mult, op1=ALU.subtract), th, before)
            work.give(slot, th, tl)
            return [th, tl], tt

        def exact_products(o, a, b, last=True):
            pe.quiet(lambda e: e.matmul(o, a[0], b[0], start=True, stop=False))
            pe.quiet(lambda e: e.matmul(o, a[0], b[1], start=False, stop=False))
            return pe.do(lambda e: e.matmul(o, a[1], b[0], start=False, stop=True))

        def scores_of(q, k, after):
            slot, bank, free = work.take()
            pe.wait(free, after)
            for n in range(2):
                tok = exact_products(bank[:, n * 256:(n + 1) * 256], [x[:, n * 128:(n + 1) * 128] for x in q], k)
            return slot, bank[:, :].rearrange("p (t k) -> p t k", t=2), tok

        stat = Ring(stats, later)

        def softmax_steps(jobs, s_ring, p_ring, o_ring, y, at, y_done):
            so, po, oo = {}, {}, {}

            def scores(i):
                q, k, v, finish, sk, after, vafter = jobs[i]
                so[i] = scores_of(q, k, after())

            def soften(i):
                q, k, v, finish, sk, after, vafter = jobs[i]
                slot, ps, tok = so[i]
                ss, s, sf = s_ring.take()
                ts, st, tf = stat.take()
                if finish is None:
                    src, t, fin = ps, tok, None
                else:
                    t, fin = finish(s, ps, tok, sf)
                    src = s
                t = dve.do(lambda e: e.tensor_reduce(st[:, 0:2], src[:, :, :], AX, ALU.max), t, tf)
                if sk is None:
                    t = dve.do(lambda e: e.tensor_scalar(st[:, 2:4], st[:, 0:2], -1.0, None, ALU.mult), t)
                else:
                    t = dve.do(lambda e: e.tensor_scalar(st[:, 2:4], st[:, 0:2], sk, -1.0, ALU.max, ALU.mult), t, t_rows)
                so[i] = (slot, ss, s, sf, ts, st, src, t, fin)

            def exponentials(i):
                slot, ss, s, sf, ts, st, src, t, fin = so[i]
                sk = jobs[i][4]
                te = [act.do(lambda e, n=n: e.activation(s[:, n, :], src[:, n, :], ACT.Exp, bias=st[:, 2 + n:3 + n],
                                                         accum_out=st[:, 4 + n:5 + n]), t, sf) for n in range(2)]
                work.give(slot, te[1] if fin is None else fin)
                if sk is not None:
                    te.append(act.do(lambda e: e.activation(st[:, 6:8], st[:, 2:4], ACT.Exp, bias=sk), t))
                so[i] = (ss, s, te, ts, st)

            def normalise(i):
                ss, s, td, ts, st = so[i]
                den = st[:, 4:6]
                if jobs[i][4] is not None:
                    td = dve.do(lambda e: e.tensor_tensor(st[:, 8:10], st[:, 4:6], st[:, 6:8], ALU.add), td)
                    den = st[:, 8:10]
                tr = dve.do(lambda e: e.reciprocal(st[:, 10:12], den), td)
                t0 = pool.do(lambda e: e.tensor_scalar(s[:, 0, :], s[:, 0, :], st[:, 10:11], 1.0, ALU.mult, ALU.mult), tr)
                t1 = pool.do(lambda e: e.tensor_scalar(s[:, 1, :], s[:, 1, :], st[:, 11:12], 1.0, ALU.mult, ALU.mult), tr)
                stat.give(ts, t0, t1)
                so[i] = (ss, s, [t0, t1])

            def turn(i):
                ss, s, tn = so[i]
                slot, bank, free = work.take()
                tt = turn_blocks(bank, [s[:, n, kt * 128:(kt + 1) * 128] for kt in range(2) for n in range(2)], tn, free)
                s_ring.give(ss, tt)
                so[i] = (slot, bank, tt)

            def high(i):
                slot, bank, tt = so[i]
                ps, (ph, pl), pf = p_ring.take()
                view = bank[:, :].rearrange("p (k q) -> p k q", k=2)
                th = act.do(lambda e: e.activation(ph, view, ACT.Copy), tt, pf)
                po[i] = (slot, view, ps, ph, pl, th, pf)

            def low(i):
                slot, view, ps, ph, pl, th, pf = po[i]
                tl = dve.do(lambda e: e.tensor_tensor(pl, view, ph.bitcast(F), ALU.subtract), th, pf)
                work.give(slot, th, tl)
                po[i] = (ps, ph, pl, [th, tl])

            def values(i):
                q, k, v, finish, sk, after, vafter = jobs[i]
                ps, ph, pl, tp = po[i]
                if i % 2 == 0:
                    oo[i // 2] = o_ring.take()
                slot, bank, free = oo[i // 2]
                o = bank[0:64, 256 * (i % 2):256 * (i % 2) + 256]
                pe.wait(tp, free, vafter())
                for kt in range(2):
                    vh, vl = v(kt)
                    for n, (a_, b_) in enumerate(((vh, ph), (vh, pl), (vl, ph))):
                        f = lambda e, a_=a_, b_=b_, kt=kt, n=n: e.matmul(o, a_, b_[:, kt, :], start=(kt == 0 and n == 0), stop=(kt == 1 and n == 2))
                        if kt == 1 and n == 2:
                            tv = pe.do(f)
                        else:
                            pe.quiet(f)
                p_ring.give(ps, tv)
                oo[i // 2] = (slot, bank, tv if i % 2 else free)

            def finished(i):
                if i % 2 == 1:
                    j = i // 2
                    slot, bank, tv = oo[j]
                    done = []
                    for u in range(2):
                        yh, yl = [x[64 * u:64 * u + 64, at[j], :] for x in y]
                        o = bank[0:64, 256 * u:256 * u + 256]
                        done.append(act.do(lambda e, o=o, yh=yh: e.activation(yh, o, ACT.Copy), tv))
                    for u in range(2):
                        yh, yl = [x[64 * u:64 * u + 64, at[j], :] for x in y]
                        o = bank[0:64, 256 * u:256 * u + 256]
                        done.append(dve.do(lambda e, o=o, yh=yh, yl=yl: e.tensor_tensor(yl, o, yh.bitcast(F), ALU.subtract), done[1]))
                    o_ring.give(slot, *done)
                    y_done[at[j]] = done

            n = len(jobs)

            def step(i):
                for work_of, late in ((high, 4), (normalise, 2), (soften, 1), (low, 4), (finished, 6), (exponentials, 1), (turn, 3), (scores, 0), (values, 5)):
                    if 0 <= i - late < n:
                        work_of(i - late)

            return [lambda i=i: step(i) for i in range(n + 7)]

        def queued(toks, i):
            while toks[i] is None:
                later.popleft()()
            return toks[i]

        def half_of(x, h, at=None):
            return [y[64 * (h % 2):64 * (h % 2) + 64, h // 2 if at is None else at, :] for y in x]

        def scaled_split(oh, ol, pair, c0, c1, rms, done, *after):
            toks = []
            for t in range(2):
                th = act.do(lambda e, t=t: e.activation(oh[:, t, :], pair[t][:, c0:c1], ACT.Copy, scale=rms.r[t]), done[t], rms.done, *after)
                toks.append(dve.do(lambda e, t=t: e.scalar_tensor_tensor(out=ol[:, t, :], in0=pair[t][:, c0:c1], scalar=rms.r[t], in1=oh[:, t, :].bitcast(F),
                                                                         op0=ALU.mult, op1=ALU.subtract), th, *after))
            return toks

        def scaled_copy(o, pair, c0, c1, rms, done, *after):
            t0 = act.do(lambda e: e.activation(o[:, 0, :], pair[0][:, c0:c1], ACT.Copy, scale=rms.r[0]), done[0], rms.done, *after)
            t1 = dve.do(lambda e: e.tensor_scalar(o[:, 1, :], pair[1][:, c0:c1], rms.r[1], None, ALU.mult), done[1], rms.done, *after)
            return [t0, t1]

        mkT = {0: [sb(f"mkT{n}0", [128, 2, 256], R, opening) for n in "hl"], 1: [keep[:, 0:2, :], keep[:, 2:4, :]]}
        mv = {0: [sb(f"mv{n}0", [128, 2, 256], R, opening) for n in "hl"], 1: [keep[:, 4:6, :], keep[:, 6:8, :]]}
        mstage = [early[:, 2560 + 512 * l:3072 + 512 * l].rearrange("p (t d) -> p t d", t=2) for l in range(2)]
        memTh = sb("memTh", [128, 8, 256], R, opening)
        memTl = sb("memTl", [128, 8, 256], R, opening)
        mt = [None] * 8
        mrms = Rms(next(roots))
        for k in range(0, 8, 2):
            split_through(min(k // 2, SPLITS - 1))
            mem_turned = turn_piece(memx, k * 128, 2, memTh, memTl, k, mt, t_mem, None, memgain, t_norm["mem"])

        def squares():
            for j in range(2):
                for t in range(2):
                    mrms.square(memx[:, t, j * 512:(j + 1) * 512], t, j, t_mem)
            mrms.root()
        later.append(squares)
        later.append(turn_rows)

        class Input:

            def __init__(self, gain, before):
                self.t, self.gain, self.before, self.turned = [None] * 8, gain, before, None
                self.rms = Rms(next(roots))

            def pieces(self, j, after):
                for k in range(4 * j, 4 * j + 4, 2):
                    def piece(k=k):
                        self.turned = turn_piece(xres, k * 128, 2, xTh, xTl, k, self.t, after, self.before, self.gain, t_norm["cols"])
                    later.append(piece)

                def squares():
                    for t in range(2):
                        self.rms.square(xres[:, t, j * 512:(j + 1) * 512], t, j, after)
                    if j == 1:
                        self.rms.root()
                later.append(squares)

        x_in = Input(col(0), None)
        for j in range(2):
            x_in.pieces(j, t_x)
        t_mkT, t_mv = {}, {}

        def memory(l, pops):
            def evac(pair, done):
                ts = scaled_copy(mstage[l], pair, 0, 256, mrms, done)
                tv = scaled_split(mv[l][0], mv[l][1], pair, 256, 512, mrms, done, *ts)
                t_mv[l] = tv

                def piece():
                    t_mkT[l], _ = pairs_piece(mstage[l], 0, 2, mkT[l], 0, 1.0, ts, None)
                later.append(piece)
                return tv
            linear("mem", 2 if l else len(FIRST), memTh, memTl, mt, evac, pops)

        memory(0, 2)

        rate = small[:, 136:144]
        t_small = {}

        def small_vectors():
            lam = col(15)
            sp_ = [small[:, 96 + 8 * i:104 + 8 * i] for i in range(6)]
            t = dve.do(lambda e: e.scalar_tensor_tensor(out=sp_[0], in0=lam, scalar=-1.0, in1=lam, op0=ALU.mult, op1=ALU.min), t_norm["cols"])
            t = act.do(lambda e: e.activation(sp_[1], sp_[0], ACT.Exp), t)
            t = dve.do(lambda e: e.tensor_scalar(sp_[2], sp_[1], 2.0, None, ALU.add), t)
            t = dve.do(lambda e: e.reciprocal(sp_[3], sp_[2]), t)
            t = dve.do(lambda e: e.tensor_tensor(sp_[1], sp_[1], sp_[3], ALU.mult), t)
            t = dve.do(lambda e: e.tensor_tensor(sp_[2], sp_[1], sp_[1], ALU.mult), t)
            t = dve.do(lambda e: e.tensor_scalar(sp_[3], sp_[2], 1.0 / 17, 1.0 / 15, ALU.mult, ALU.add), t)
            for n in (13, 11, 9, 7, 5, 3, 1):
                t = dve.do(lambda e: e.tensor_tensor(sp_[3], sp_[3], sp_[2], ALU.mult), t)
                t = dve.do(lambda e, n=n: e.tensor_scalar(sp_[3], sp_[3], 1.0 / n, None, ALU.add), t)
            t = dve.do(lambda e: e.tensor_tensor(sp_[3], sp_[3], sp_[1], ALU.mult), t)
            t = dve.do(lambda e: e.tensor_scalar(sp_[4], lam, -1.0, 0.0, ALU.mult, ALU.max), t)
            t = dve.do(lambda e: e.scalar_tensor_tensor(out=sp_[5], in0=sp_[3], scalar=2.0, in1=sp_[4], op0=ALU.mult, op1=ALU.add), t)
            t_small["rate"] = dve.do(lambda e: e.tensor_scalar(sp_[5], sp_[5], -8.0, None, ALU.mult), t)

        PITCH = 12 * 15 * 31
        t_bias = {}

        def neighbourhood_bias(bias, after):
            t_rep = scrsem.load(pool, a["scratch_rpb"], bass.AP(a["rpb_b"].tensor, 0, [[0, 64], [1, PITCH]]), after)
            for rr in range(4):
                for i in range(4):
                    src = bass.AP(a["scratch_rpb"].tensor, (i - rr + 7) * 31 + 15, [[PITCH - 1, 64], [15 * 31, 12], [1, 64]])
                    t = rpbsem.load(pool, bias[(rr % 2) * 64:(rr % 2) * 64 + 64, :, rr // 2, i * 64:(i + 1) * 64], src, t_rep)
            for h in range(12):
                for n in range(2):
                    t_bias["t"] = pool.do(lambda e, h=h, n=n: e.tensor_tensor(bias[:, h, n, :], bias[:, h, n, :], window, ALU.add), t, t_const)

        def add_residual(c, following):
            def evac(pair, done):
                toks = [dve.do(lambda e, t=t: e.tensor_tensor(xres[:, t, c:c + 512], pair[t][:, :], xres[:, t, c:c + 512], ALU.add), done[t], following.turned_before)
                        for t in range(2)]
                following.pieces(c // 512, toks)
                return toks
            return evac

        def mix(l, x_in, following):
            sc = ExitStack()
            t_f = None if l == 0 else fence()
            qy = [sb(f"qy{n}{l}", [128, 8, 256], R, sc) for n in "hl"]
            kT = [sb(f"kT{n}{l}", [128, 4 if l == 0 else 6, 256], R, sc) for n in "hl"]
            v = [sb(f"v{n}{l}", [128, 2, 256 if l == 0 else 768], R, sc) for n in "hl"]
            p_ring = Ring([[sb(f"p{n}{l}{i}", [128, 2, 256], R, sc)[:, :, :] for n in "hl"] for i in range(2)], later)
            stage = Ring([nrm[:, :, 0:512], nrm[:, :, 512:1024]], later)
            kd = gbc[:, :].rearrange("p (t d) -> p t d", t=2)
            if l == 0:
                s_slots = [early[:, 512 * i:512 * i + 512].rearrange("p (t k) -> p t k", t=2) for i in range(4)]
            else:
                s_slots = [dist, kd[:, :, 0:256], kd[:, :, 256:512]]
            s_ring = Ring(s_slots, later)
            if l == 0:
                s_ring.free = [[mem_turned, mrms.done] for _ in s_slots]
            tq, tk, tv = [None] * 8, [None] * 6, {}
            rms = x_in.rms

            def staged(pieces, c0=0, c1=512):
                def evac(pair, done):
                    ss, s, sf = stage.take()
                    ts = scaled_copy(s[:, :, 0:c1 - c0], pair, c0, c1, rms, done, sf, t_f)
                    last = []
                    for i, (c, n, dst, at, scale, tok) in enumerate(pieces):
                        def piece(c=c, n=n, dst=dst, at=at, scale=scale, tok=tok, i=i):
                            t, tt = pairs_piece(s, c, n, dst, at, scale, ts, t_f)
                            for j in range(n):
                                tok[at + j] = t
                            if i == len(pieces) - 1:
                                stage.give(ss, tt)
                        later.append(piece)
                    return ts
                return evac

            def scale_q(*at):
                return [(256 * i, 2, qy, j, 0.125, tq) for i, j in enumerate(at)]

            def evac_k(pair, done):
                ss, s, sf = stage.take()
                ts = scaled_copy(s[:, :, :], pair, 0, 512, rms, done, sf, t_f)
                td = []
                for t in range(2):
                    for u in range(2):
                        f = lambda e, t=t, u=u: e.tensor_copy(
                            kd[:, t, :].rearrange("p (h u d) -> p h u d", h=4, u=2)[:, :, u, :],
                            s[:, t, 256:512].rearrange("p (h d) -> p h d", h=4))
                        td.append(dve.do(f, ts, t_f) if u else pool.do(f, ts, t_f))

                def piece_q():
                    tq[4], tt = pairs_piece(s, 0, 2, qy, 4, 0.125, ts, t_f)
                    tq[5] = tq[4]
                    stage.give(ss, tt, *td)
                later.append(piece_q)
                for k in (0, 2):
                    def piece_k(k=k):
                        tk[k], _ = pairs_piece(kd, k * 128, 2, kT, k, 1.0, td, t_f)
                        tk[k + 1] = tk[k]
                    later.append(piece_k)
                return ts

            def evac_v(pair, done):
                tv["first"] = scaled_split(v[0][:, :, 0:512], v[1][:, :, 0:512], pair, 0, 512, rms, done, t_f)
                return tv["first"]

            nv = 256 if l == 0 else 768
            qm_evac = staged([(0, 2, qy, 6, 0.125, tq)], 256, 512)

            def evac_vm(pair, done):
                tv["last"] = scaled_split(v[0][:, :, nv - 256:nv], v[1][:, :, nv - 256:nv], pair, 0, 256, rms, done, t_f)
                return qm_evac(pair, [[d] + tv["last"] for d in done])

            k4 = lambda c, at: (c, 2, kT, at, 1.0, tk)
            evacs = {1024: evac_vm, 512: evac_k, 0: staged(scale_q(0, 2))} if l == 0 else {
                2048: evac_vm, 1536: evac_v, 512: staged(scale_q(4) + [k4(256, 0)]), 1024: staged([k4(0, 2), k4(256, 4)]), 0: staged(scale_q(0, 2))}
            jobs = []
            slopes = [2.0 ** (-8.0 * (h + 1) / 12) for h in range(12)]
            for h in range(12):
                if l == 0:
                    def finish(s, ps, tok, sf, h=h):
                        t = dve.do(lambda e: e.scalar_tensor_tensor(out=s[:, :, :], in0=dist, scalar=-slopes[h], in1=ps, op0=ALU.mult, op1=ALU.add),
                                   tok, sf, t_f, t_const)
                        return t, t
                    kv = h // 3
                    jobs.append((half_of(qy, h), half_of(kT, h, kv), lambda kt, kv=kv: [x[:, kt, kv * 64:(kv + 1) * 64] for x in v],
                                 finish, sink[:, h:h + 1], lambda h=h, kv=kv: [queued(tq, h // 2), queued(tk, kv)], lambda: tv["last"]))
                else:
                    def finish(s, ps, tok, sf, h=h):
                        t = dve.do(lambda e: e.tensor_tensor(s[:, :, :], ps, bias[:, h, :, :], ALU.add), tok, sf, t_f, t_bias["t"])
                        return t, t
                    jobs.append((half_of(qy, h), half_of(kT, h), lambda kt, h=h: [x[:, kt, h * 64:(h + 1) * 64] for x in v],
                                 finish, None, lambda h=h: [queued(tq, h // 2), queued(tk, h // 2)], lambda h=h: tv["first" if h < 8 else "last"]))
            for h in range(4):
                jobs.append((half_of(qy, 12 + h), half_of(mkT[l], h), lambda kt, h=h: [x[:, kt, h * 64:(h + 1) * 64] for x in mv[l]],
                             None, None, lambda h=h: [queued(tq, 6 + h // 2), t_mkT[l]], lambda: t_mv[l]))
            turns = [12, 13, 14, 15, 8, 9, 10, 11, 0, 1, 2, 3, 4, 5, 6, 7]
            yt = [None] * 8
            steps = deque(softmax_steps([jobs[h] for h in turns], s_ring, p_ring, work, qy, [h // 2 for h in turns[::2]], yt))
            t_blank = []
            for c, heads, pops in MIX_TILES[l]:
                x_done = linear("in", 2, xTh, xTl, x_in.t, evacs[c], pops)
                if heads and not t_blank:
                    t_blank.append(True)
                    later.append(lambda: None)
                for _ in range(heads):
                    later.append(steps.popleft())
            following.before = x_done
            following.turned_before = x_in.turned
            later.extend(steps)
            if l == 0:
                memory(1, 1)
            made = []
            for k in range(2):
                for n in range(2):
                    if k == 0:
                        while None in yt[4:8]:
                            later.popleft()()
                        made.append([work.take() for _ in range(2)])
                    taken = made[n]
                    done = part("out", taken, qy[0], qy[1], yt, k == 0, k == 1, lambda: pop(1))
                    if k == 1:
                        evacuated(taken, add_residual(512 * n, following), done)
                    pop(3)
            drain_later()
            sc.close()

        def ffn(l, x_in, finish, t_f):
            sc = ExitStack()
            hTh = sb(f"hTh{l}", [128, 22, 256], R, sc)
            hTl = sb(f"hTl{l}", [128, 22, 256], R, sc)
            ht = [None] * 22
            rms = x_in.rms
            keep = {"m": t_f, "turned": t_f, "left": 0}
            for c, w in tiles_of(DFF):
                parts = 2 if w == 512 else 1
                tg = []

                def gate(pair, done, w=w, tg=tg):
                    for t in range(2):
                        tg.append(act.do(lambda e, t=t: e.activation(nrm[:, t, 0:w], pair[t][:, 0:w], ACT.Silu, scale=rms.r[t]),
                                         done[t], keep["m"], rms.done))
                    return tg

                def up(pair, done, w=w, c=c, tg=tg):
                    while keep["left"]:
                        later.popleft()()
                    tm = [dve.do(lambda e, t=t: e.scalar_tensor_tensor(out=nrm[:, t, 512:512 + w], in0=pair[t][:, 0:w], scalar=rms.r[t],
                                                                       in1=nrm[:, t, 0:w], op0=ALU.mult, op1=ALU.mult),
                                 done[t], tg[t], keep["turned"], rms.done) for t in range(2)]
                    keep["m"] = tm
                    for k in range(0, w // 128, 2):
                        keep["left"] += 1

                        def piece(k=k, c=c):
                            keep["turned"] = turn_piece(nrm, 512 + k * 128, 2, hTh, hTl, c // 128 + k, ht, tm, t_f)
                            keep["left"] -= 1
                        later.append(piece)
                    return tm
                linear(f"gu{l}", parts, xTh, xTl, x_in.t, gate)
                x_done = linear(f"gu{l}", parts, xTh, xTl, x_in.t, up)
            finish(x_done, x_in.turned)
            for j, c in enumerate((0, 512)):
                done = linear(f"down{l}", 6, hTh, hTl, ht, finish.evac(c))
            sc.close()
            return done

        class ToInput:

            def __init__(self, following):
                self.following = following

            def __call__(self, x_done, turned):
                self.following.before, self.following.turned_before = x_done, turned

            def evac(self, c):
                return add_residual(c, self.following)

        in_f0, in_m1, in_f1 = (Input(col(i), None) for i in (2, 1, 3))
        mix(0, x_in, in_f0)
        opening.close()
        t_f = fence()
        big = sb("big", [128, 6144])
        bias = big[:, :].rearrange("p (h t k) -> p h t k", h=12, t=2)
        later.append(lambda t_f=t_f: neighbourhood_bias(bias, t_f))
        later.append(small_vectors)
        ffn(0, in_f0, ToInput(in_m1), t_f)
        mix(1, in_m1, in_f1)
        drain_later()

        t_f = fence()
        t0 = act.do(lambda e: e.activation(small[:, 0:8], col(7), ACT.Silu), t_norm["cols"])
        tz = pool.do(lambda e: e.memset(big[:, :], 0.0), t_f)
        t_b = gsem.load(pool, big[0:1, :], a["b_ada_2"], tz)
        acc_tok["c"] = [t0, tz, t_b]
        t_g1 = side.load(pool, gbc[:, :], bass.AP(a["norm_final"].tensor, 0, [[0, 128], [1, D]]))

        class Last:
            def __call__(self, x_done, turned):
                self.before, self.turned = x_done, turned
                self.r1, self.r2, self.out = Rms(next(roots)), Rms(next(roots)), []

            def evac(self, c):
                def run(pair, done):
                    given = []
                    for t in range(2):
                        x = xres[:, t, c:c + 512]
                        t0 = dve.do(lambda e, t=t, x=x: e.tensor_tensor(x, pair[t][:, :], x, ALU.add), done[t], self.turned)
                        t1 = self.r1.square(x, t, c // 512, t0)
                        t2 = dve.do(lambda e, x=x: e.tensor_tensor(x, x, gbc[:, c:c + 512], ALU.mult), t0, t1, t_g1)
                        self.r2.square(x, t, c // 512, t2)
                        self.out.append(t2)
                        given.append(t0)
                    return given
                return run

        last = Last()
        ffn(1, in_f1, last, fence())
        drain_later()
        t_f = fence()
        t_acc = list(acc_tok["t"])
        slot, bank, free = work.take()
        pe.wait(free, t_acc, t_ones)
        for n, base in enumerate((0, 1024, 3072, 4096)):
            for k in range(8):
                f = lambda e, n=n, k=k, b=base, bank=bank: e.matmul(bank[:, n * 8 + k:n * 8 + k + 1], big[:, b + k * 128:b + (k + 1) * 128],
                                                                    ones[:, 0:1], start=True, stop=True)
                tc = pe.do(f)
        st, s2 = last.r1.st, last.r2.st
        t = dve.do(lambda e: e.tensor_tensor(s2[:, 4:6], s2[:, 0:2], s2[:, 2:4], ALU.add), last.r2.tokens)
        u = dve.do(lambda e: e.tensor_tensor(st[:, 4:6], st[:, 0:2], st[:, 2:4], ALU.add), last.r1.tokens)
        t = dve.do(lambda e: e.tensor_scalar(s2[:, 4:6], s2[:, 4:6], 1.0 / D, EPS * EPS, ALU.mult, ALU.add), t)
        u = dve.do(lambda e: e.tensor_scalar(st[:, 6:8], st[:, 4:6], 1.0 / D, EPS, ALU.mult, ALU.add), u)
        t = dve.do(lambda e: e.scalar_tensor_tensor(out=s2[:, 6:8], in0=st[:, 4:6], scalar=EPS / D, in1=s2[:, 4:6], op0=ALU.mult, op1=ALU.add), t, u)
        t_r12 = pool.do(lambda e: e.tensor_tensor(s2[:, 8:10], s2[:, 6:8], half_, ALU.pow), t, t_half)
        t_r1 = pool.do(lambda e: e.tensor_tensor(st[:, 8:10], st[:, 6:8], half_, ALU.pow), u, t_half)
        mod = small[:, 32:64]
        t_mod = dve.do(lambda e, b=bank: e.tensor_copy(mod, b[:, 0:32]), tc)
        work.give(slot, t_mod)
        gates = big[:, 0:2048]
        gain1, gain2 = small[:, 64:72], small[:, 72:80]
        tg1 = dve.do(lambda e: e.scalar_tensor_tensor(out=gain1, in0=mod[:, 8:16], scalar=1.0, in1=col(5), op0=ALU.add, op1=ALU.mult), t_mod)
        tg2 = dve.do(lambda e: e.scalar_tensor_tensor(out=gain2, in0=mod[:, 24:32], scalar=1.0, in1=col(6), op0=ALU.add, op1=ALU.mult), t_mod)
        t_gate = []

        def gate_rows():
            made = []
            for base in (2048, 2560, 5120, 5632):
                slot, bank, free = work.take()
                made.append((slot, bank, pe.do(lambda e, b=base, bank=bank: e.matmul(bank[:, :], ones[:, :], big[:, b:b + 512], start=True, stop=True), free, t_acc)))
            for n, (slot, bank, t) in enumerate(made):
                t_gate.append(act.do(lambda e, n=n, b=bank: e.activation(gates[:, n * 512:(n + 1) * 512], b[:, :], ACT.Copy), made[-1][2]))
                work.give(slot, t_gate[-1])
        named["gates"] = gate_rows

        def normed(src, r, after, before):
            toks = []
            for c in (0, 512):
                t0 = dve.do(lambda e, c=c: e.tensor_scalar(nrm[:, 0, c:c + 512], src[:, 0, c:c + 512], r[0], None, ALU.mult), after, before)
                t1 = act.do(lambda e, c=c: e.activation(nrm[:, 1, c:c + 512], src[:, 1, c:c + 512], ACT.Copy, scale=r[1]), after, before)
                toks.append([t0, t1])
            return toks

        sc = ExitStack()
        t_z = normed(xres, [s2[:, 8:9], s2[:, 9:10]], [t_r12, last.out], t_f)
        rTh = keep
        rTl = sb("rTl", [128, 8, 256], R, sc)
        inner = ExitStack()
        acc = sb("acc", [128, 2, 256], F, inner)[:, :, :]
        left = sb("left", [128, 2, 256], F, inner)[:, :, :]
        sgb = sb("sgb", [128, 2, D], F, inner)
        rel = sb("rel", [32, 8], F, inner)
        stage = Ring([sb(f"stage{i}", [128, 2, 512], F, inner) for i in range(2)], later)
        wi = sb("wi", [128, 2, 8], F, inner)
        qy = [sb(f"q2y{n}", [128, 4, 256], R, inner) for n in "hl"]
        kT = [sb(f"k2T{n}", [128, 2, 256], R, inner) for n in "hl"]
        v2 = [sb(f"v2{n}", [128, 2, 128], R, inner) for n in "hl"]
        p_ring = Ring([[sb(f"p2{n}{i}", [128, 2, 256], R, inner)[:, :, :] for n in "hl"] for i in range(2)], later)
        temps = [big[:, 2048 + 1024 * i:3072 + 1024 * i].rearrange("p (k t) -> p k t", k=4) for i in range(4)]
        rg, ig = temps[2:]
        xcs = [temps[0], nrm[:, 0, :].rearrange("p (k t) -> p k t", k=4)]
        gls = [temps[1], nrm[:, 1, :].rearrange("p (k t) -> p k t", k=4)]
        tmp_ring = Ring([gls[0][:, i, :] for i in range(4)], later)
        tmp_ring.free = [[tc] for _ in range(4)]
        xt, xt_turned = [None] * 8, {}
        for k in (0, 4):
            xt_turned["t"] = turn_shifted(nrm, k, xt, t_z[k // 4], [last.before, t_f, t_mod], gain1, tg1, mod[:, 0:8], tmp_ring)
        t_x1 = []

        def first_output():
            t_x1.extend(pool.do(lambda e, t=t: e.tensor_scalar(xres[:, t, :], xres[:, t, :], last.r1.r[t], 1.0, ALU.mult, ALU.mult), t_r1, t_z) for t in range(2))
        named["x1"] = first_output

        onehot = acc[0:32, :, :].rearrange("p t k -> p (t k)")
        relrow = left[0:8, :, :].rearrange("p t k -> p (t k)")
        t_rel = relsem.load(pool, rel[:, :], a["rel_bias_2"], t_f)
        t_rel = relsem.load(pool, onehot, a["onehot"], t_f)
        wrg = sgb[:, :, :].rearrange("p g (n d) -> p g n d", n=8)
        t_wg = gsem.load(pool, wrg[:, 0, :, :], a["w_rg_2"][0].rearrange("n c d -> c n d"), t_f)
        t_wg = gsem.load(pool, wrg[:, 1, :, :], a["w_ig_2"][0].rearrange("n c d -> c n d"), t_f)
        t_rb = {}

        def relative_rows():
            slot, bank, free = work.take()
            tb = pe.do(lambda e, b=bank: e.matmul(b[0:8, :], rel[:, :], onehot, start=True, stop=True), free, t_rel)
            tb = dve.do(lambda e, b=bank: e.tensor_copy(relrow, b[0:8, :]), tb, t_f)
            work.give(slot, tb)
            t_rb["row"] = tb
            t_rb["scr"] = scrsem.load(pool, bass.AP(a["scratch"].tensor, 0, [[512, 8], [4096, 128], [1, 512]]),
                                      relrow.unsqueeze(1).to_broadcast([8, 128, 512]), tb)
        named["rel"] = relative_rows

        brings = Ring([(gbc[:, i * 512:(i + 1) * 512], Landing(sem(f"d_brow{i}"))) for i in range(2)], later)
        with_row = [(k, c, w) for k, c, w, _ in IN2 if k != "yr"]
        rows_at = {"n": 0}
        loaded = []

        def bias_row():
            if rows_at["n"] < len(with_row):
                _, c, w = with_row[rows_at["n"]]
                rows_at["n"] += 1
                bs, (br, land), bf = brings.take()
                loaded.append((bs, br, land.load(pool, br[:, 0:w], bass.AP(a["b_in_2"].tensor, c, [[0, 128], [1, w]]), bf, t_f)))

        bias_row()
        bias_row()
        todo = list(IN2)

        def project(kind, target, then):
            what, c, w, between = todo.pop(0)
            assert what == kind

            def evac(pair, done):
                s, before, slot = target()
                if kind == "yr":
                    toks = [act.do(lambda e: e.activation(s[:, 0, 0:w], pair[0][:, 0:w], ACT.Copy), done[0], before, t_f),
                            dve.do(lambda e: e.tensor_copy(s[:, 1, 0:w], pair[1][:, 0:w]), done[1], before, t_f)]
                else:
                    bs, br, tb = loaded.pop(0)
                    toks = [dve.do(lambda e, t=t: e.tensor_tensor(s[:, t, 0:w], pair[t][:, 0:w], br[:, 0:w], ALU.add), done[t], tb, before, t_f)
                            for t in range(2)]
                    brings.give(bs, *toks)
                    bias_row()
                then(s, toks, slot)
                return toks
            return linear("in2", 1 if w <= 256 else 2, xTh, xTl, xt, evac, 0, between)

        def staged():
            slot, s, free = stage.take()
            return s, free, slot

        wrg_read, tcs, t_half_done = {}, {}, {-1: None}
        t_rt = [None] * 8

        def t_turned():
            return xt_turned["t"]

        def after_xr(half):
            xc = xcs[half]

            def then(s, ts, slot):
                tcs[half] = []
                for k in (0, 2):
                    def piece(k=k):
                        bs, bank, free = work.take()
                        tt = turn_blocks(bank, [s[:, t, (k + j) * 128:(k + j + 1) * 128] for j in range(2) for t in range(2)], ts, free)
                        for j in range(2):
                            kk = 4 * half + k + j
                            t = act.do(lambda e, o=xc[:, k + j, :], p=bank[:, j * 256:(j + 1) * 256], kk=kk:
                                       e.activation(o, p, ACT.Identity, bias=col(12)[:, kk:kk + 1], scale=col(11)[:, kk:kk + 1]),
                                       tt, t_z if half else xt, t_turned(), t_gate)
                        for j in range(2):
                            kk = 4 * half + k + j
                            for n in (1, 2, 3):
                                t = dve.do(lambda e, o=xc[:, k + j, :], p=bank[:, j * 256:(j + 1) * 256], n=n, kk=kk: e.scalar_tensor_tensor(
                                    out=o[:, n:], in0=p[:, 0:256 - n], scalar=col(11 - n)[:, kk:kk + 1], in1=o[:, n:], op0=ALU.mult, op1=ALU.add), t)
                            tcs[half].append(t)
                        work.give(bs, t)
                        if k == 2:
                            stage.give(slot, tt)
                    named[f"conv{half}{k}"] = piece
            return then

        def after_yr(half):
            xc, gl = xcs[half], gls[half]

            def then(s, ts, slot):
                hold = {}
                for k in (0, 2):
                    def piece(k=k):
                        bs, bank, free = work.take()
                        tt = turn_blocks(bank, [s[:, t, (k + j) * 128:(k + j + 1) * 128] for j in range(2) for t in range(2)], ts, free)
                        for j in range(2):
                            kk = 4 * half + k + j
                            t = act.do(lambda e, o=gl[:, k + j, :], p=bank[:, j * 256:(j + 1) * 256], kk=kk:
                                       e.activation(o, p, ACT.Gelu_apprx_tanh, bias=bias_yr[:, kk:kk + 1]), tt, xt, t_turned(), t_gate)
                        work.give(bs, t)
                        hold["gl"] = t
                        if k == 2:
                            stage.give(slot, tt)
                    named[f"gelu{half}{k}"] = piece
                for n, dst in enumerate((rg, ig)):
                    for k in (0, 2):
                        def piece(n=n, dst=dst, k=k):
                            bs, bank, free = work.take()
                            pe.wait(free, tcs[half], t_wg)
                            for j in range(2):
                                kk = 4 * half + k + j
                                f = lambda e, j=j, kk=kk: e.matmul(bank[:, j * 256:(j + 1) * 256], wrg[:, n, kk, :], xc[:, k + j, :], start=True, stop=True)
                                tm = pe.do(f)
                            wrg_read[half] = tm
                            for j in range(2):
                                kk = 4 * half + k + j
                                t = act.do(lambda e, o=dst[:, k + j, :], p=bank[:, j * 256:(j + 1) * 256], b=col(13 + n)[:, kk:kk + 1]:
                                           e.activation(o, p, ACT.Sigmoid, bias=b), tm, t_half_done[half - 1], t_gate)
                            work.give(bs, t)
                            hold[n] = t
                        named[f"gate{half}{n}{k}"] = piece

                def recurrence():
                    ti = pool.do(lambda e: e.tensor_tensor(ig, ig, xc, ALU.mult), hold[1])
                    ta_, tt_ = [], []
                    for k in range(4):
                        kk = 4 * half + k
                        ta_.append(act.do(lambda e, k=k, kk=kk: e.activation(xc[:, k, :], rg[:, k, :], ACT.Exp, scale=rate[:, kk:kk + 1]),
                                          hold[0], ti, t_small["rate"]))
                    for k in range(4):
                        kk = 4 * half + k
                        tt_.append(act.do(lambda e, k=k, kk=kk: e.activation(rg[:, k, :], rg[:, k, :], ACT.Tanh, scale=rate[:, kk:kk + 1]), ta_[k]))
                    hold["ti"], hold["a"], hold["m"] = ti, ta_, []
                    for j in range(2):
                        bs, bank, free = work.take()
                        square, tj = bank[:, :].rearrange("p (k t) -> p k t", k=2), rg[:, 2 * j:2 * j + 2, :]
                        t = act.do(lambda e, o=square, j=j: e.activation(o, xc[:, 2 * j:2 * j + 2, :], ACT.Square), ta_, free)
                        t = dve.do(lambda e, q=square, r=tj: e.scalar_tensor_tensor(out=r, in0=q, scalar=1.0, in1=r, op0=ALU.add, op1=ALU.mult), t, tt_)
                        work.give(bs, t)
                        hold["m"].append(t)

                def increments():
                    t3 = act.do(lambda e: e.activation(rg, rg, ACT.Sqrt, scale=-1.0), hold["m"])
                    hold["u"] = pool.do(lambda e: e.tensor_tensor(ig, ig, rg, ALU.mult), t3, hold["ti"])

                def scan():
                    for k in range(4):
                        t6 = dve.do(lambda e, k=k: e.tensor_tensor_scan(rg[:, k, :], xc[:, k, :], ig[:, k, :], 0.0, ALU.mult, ALU.add), hold["u"], hold["a"])
                    hold["h"] = pool.do(lambda e: e.tensor_tensor(gl, gl, rg, ALU.mult), t6, hold["gl"])

                def parts():
                    t7 = hold["h"]
                    o, lo = rTh[:, 4 * half:4 * half + 4, :], rTl[:, 4 * half:4 * half + 4, :]
                    th = act.do(lambda e: e.activation(o, gl, ACT.Copy), t7, t_f)
                    tl = dve.do(lambda e: e.tensor_tensor(lo, gl, o.bitcast(F), ALU.subtract), th, t_f)
                    for k in range(4):
                        t_rt[4 * half + k] = [th, tl]
                    t_half_done[half] = [th, tl, t7]
                named[f"rec{half}"], named[f"inc{half}"], named[f"scan{half}"], named[f"half{half}"] = recurrence, increments, scan, parts
            return then

        rbias = big[:, 2048:6144].rearrange("p (h t k) -> p h t k", h=8, t=2)

        def relative_bias(half):
            for t in range(2):
                src = bass.AP(a["scratch"].tensor, half * 2048 + 255 - 128 * t, [[4095, 128], [512, 4], [1, 256]])
                t_rb[half] = (relsem, rel1sem)[half].load(pool, rbias[:, 4 * half:4 * half + 4, t, :], src, t_rb["scr"], t_half_done[half])
        named["bias0"], named["bias1"] = lambda: relative_bias(0), lambda: relative_bias(1)

        def after_pairs(name, dst, tok, before):
            def then(s, ts, slot):
                for k in (0, 2):
                    def piece(k=k):
                        t, tt = pairs_piece(s, k * 128, 2, dst, k, 0.125, ts, before())
                        tok[k] = tok[k + 1] = t
                        if k == 2:
                            stage.give(slot, tt)
                    named[f"{name}{k}"] = piece
            return then

        tq, tqi, ta, tki = [None] * 4, [None] * 4, [None, None], {}
        rl_ring = Ring([dist, left], later)
        m8 = small[:, 160:176]

        def after_kw(s, ts, slot):
            tw = dve.do(lambda e: e.tensor_scalar(wi[:, :, :], s[:, :, 64:72], 8.0 ** -0.5, None, ALU.mult), ts, t_f)
            td = [dve.do(lambda e, u=u: e.tensor_copy(s[:, :, 128 + 64 * u:192 + 64 * u], s[:, :, 0:64]), ts) for u in range(2)]

            def piece():
                tki["t"], tt = pairs_piece(s, 128, 1, kT, 0, 1.0, td, t_f)
                stage.give(slot, tt, tw)
            named["ki"] = piece
            for h in range(8):
                def head(h=h):
                    bs, ps, tm = scores_of(half_of(qy, h), half_of(kT, h, 0), [tqi[h // 2], tki["t"]])
                    tki["read"] = tm
                    rs_, o, rf = rl_ring.take()
                    tr = act.do(lambda e: e.activation(o, ps, ACT.Relu), tm, rf, t_f, t_rb["scr"])
                    work.give(bs, tr)
                    for t in range(2):
                        if h == 0:
                            ta[t] = dve.do(lambda e, t=t: e.tensor_scalar(acc[:, t, :], o[:, t, :], wi[:, t, 0:1], None, ALU.mult), tr, tw, t_rb["row"])
                        else:
                            ta[t] = dve.do(lambda e, t=t: e.scalar_tensor_tensor(out=acc[:, t, :], in0=o[:, t, :], scalar=wi[:, t, h:h + 1],
                                                                                 in1=acc[:, t, :], op0=ALU.mult, op1=ALU.add), tr, ta[t])
                    rl_ring.give(rs_, *ta)
                named[f"h{h}"] = head

            best = {}

            def begin():
                t = dve.do(lambda e: e.tensor_tensor(left[:, :, :], acc[:, :, :], causal, ALU.add), ta, t_const, t_rb["scr"])
                best[0] = best[1] = t
            named["top"] = begin
            for n in range(8):
                def rounds():
                    tm = [dve.do(lambda e, t=t: e.max(m8[:, 8 * t:8 * t + 8], left[:, t, :]), best[t]) for t in range(2)]
                    for t in range(2):
                        best[t] = dve.do(lambda e, t=t: e.match_replace(left[:, t, :], m8[:, 8 * t:8 * t + 8], left[:, t, :], TAKEN), tm[t])
                named[f"top{n}"] = rounds

            def mask():
                t = dve.do(lambda e: e.tensor_scalar(acc[:, :, :], left[:, :, :], -1e38, BIG, ALU.is_le, ALU.mult), best[0], best[1])
                t_rb["mask"] = dve.do(lambda e: e.scalar_tensor_tensor(out=left[:, :, :], in0=acc[:, :, :], scalar=-BIG, in1=causal,
                                                                       op0=ALU.add, op1=ALU.add), t)
            named["mask"] = mask

        tkv = {}

        def after_kv(s, ts, slot):
            th = act.do(lambda e: e.activation(v2[0][:, :, :], s[:, :, 128:256], ACT.Copy), ts, t_f)
            tv = [th, dve.do(lambda e: e.tensor_tensor(v2[1][:, :, :], s[:, :, 128:256], v2[0][:, :, :].bitcast(F), ALU.subtract), th, t_f)]
            td = []
            for t in range(2):
                for u in range(2):
                    td.append(dve.do(lambda e, t=t, u=u: e.tensor_copy(
                        s[:, t, 256:512].rearrange("p (h u d) -> p h u d", h=2, u=2)[:, :, u, :],
                        s[:, t, 0:128].rearrange("p (h d) -> p h d", h=2)), ts))
            tkv["v"] = tv

            def piece():
                tkv["k"], tt = pairs_piece(s, 256, 2, kT, 0, 1.0, td, tki["read"])
                stage.give(slot, tt, *tv)
            named["kv"] = piece

        project("qi", staged, after_pairs("qi", qy, tqi, lambda: t_f))
        project("kw", staged, after_kw)
        for half in range(2):
            project("xr", staged, after_xr(half))
            project("yr", staged, after_yr(half))
        project("q", staged, after_pairs("q", qy, tq, lambda: tki["read"]))
        project("kv", staged, after_kv)

        yt = [None] * 4
        hold_y = {}

        def attention_begin():
            _, other, of = stage.take()
            hold_y["other"] = other
            s_ring = Ring([dist, acc, other[:, :, 0:256], other[:, :, 256:512]], later)
            s_ring.free = [rl_ring.free[0], [t_rb["mask"]], list(of), list(of)]
            jobs, masked = [], {}

            def mask(h):
                if h < 8:
                    masked[h] = pool.do(lambda e: e.tensor_tensor(rbias[:, h, :, :], rbias[:, h, :, :], left, ALU.add), t_rb[h // 4], t_rb["mask"])
            mask(0)
            mask(1)
            for h in range(8):
                def finish(s, ps, tok, sf, h=h):
                    mask(h + 2)
                    t = dve.do(lambda e: e.tensor_tensor(s[:, :, :], ps, rbias[:, h, :, :], ALU.add), tok, sf, masked[h], t_f)
                    return t, t
                kv = h // 4
                jobs.append((half_of(qy, h), half_of(kT, h, kv), lambda kt, kv=kv: [x[:, kt, kv * 64:(kv + 1) * 64] for x in v2],
                             finish, None, lambda h=h: [tq[h // 2], tkv["k"]], lambda: tkv["v"]))
            for n, step in enumerate(softmax_steps(jobs, s_ring, p_ring, work, qy, range(4), yt)):
                if n < 8:
                    named[f"s{n}"] = step
                else:
                    later.append(step)
        named["attend"] = attention_begin

        sga = nrm
        tga, tgb, tmb = [], [], []

        def gate_then(toks):
            return lambda s, ts, slot: toks.extend(ts)

        def sigmoids(s, toks):
            return [act.do(lambda e, t=t: e.activation(s[:, t, :], s[:, t, :], ACT.Sigmoid), toks) for t in range(2)]

        for c in (0, 512):
            project("gb", lambda c=c: (sgb[:, :, c:c + 512], wrg_read[1], None), gate_then(tgb))
        for c in (0, 512):
            project("ga", lambda c=c: (sga[:, :, c:c + 512], [xt_turned["t"], t_half_done[1]], None), gate_then(tga))
        for c in (0, 512):
            def evac(pair, done, c=c):
                if c == 0:
                    tgb[:] = sigmoids(sgb, tgb)
                last_ = [dve.do(lambda e, t=t: e.tensor_tensor(sgb[:, t, c:c + 512], pair[t][:, :], sgb[:, t, c:c + 512], ALU.mult), done[t], tgb)
                         for t in range(2)]
                tmb.extend(last_)
                return last_
            linear("orn", 2, rTh, rTl, t_rt, evac, 2)
        drain_later()
        tga[:] = sigmoids(sga, tga)
        merged = [None] * 8
        for c in (0, 512):
            def evac(pair, done, c=c):
                given, made = [], []
                for t in range(2):
                    m = dve.do(lambda e, t=t: e.tensor_tensor(sga[:, t, c:c + 512], pair[t][:, :], sga[:, t, c:c + 512], ALU.mult), done[t], tga)
                    given.append(m)
                    made.append(dve.do(lambda e, t=t: e.tensor_tensor(sga[:, t, c:c + 512], sga[:, t, c:c + 512], sgb[:, t, c:c + 512], ALU.add), m, tmb))
                for k in (0, 2):
                    later.append(lambda k=k, c=c: turn_piece(sga, c + k * 128, 2, rTh, rTl, c // 128 + k, merged, made, orn_done))
                return given
            if c == 0:
                orn_done = pe.now()
            linear("oat", 1, qy[0], qy[1], yt, evac)
        rms2 = Rms(next(roots))
        t_res = []
        other = hold_y["other"]
        t_o = fence()
        for c in (0, 512):
            def evac(pair, done, c=c):
                given = []
                for t in range(2):
                    x = xres[:, t, c:c + 512]
                    m = dve.do(lambda e, t=t: e.tensor_tensor(other[:, t, :], pair[t][:, :], gates[:, c:c + 512], ALU.mult), done[t], t_o, t_gate, t_res)
                    u = dve.do(lambda e, t=t, x=x: e.tensor_tensor(x, x, other[:, t, :], ALU.add), m, t_x1)
                    rms2.square(x, t, c // 512, u)
                    given.append(m)
                    t_res.append(u)
                return given
            done = linear("out2", 2, rTh, rTl, merged, evac)
        drain_later()
        inner.close()
        sc.close()

        t_f = fence()
        rms2.root()
        t_z = normed(xres, rms2.r, [rms2.done, t_res], t_f)
        hTh = sb("hTh2", [128, 22, 256], R, sc)
        hTl = sb("hTl2", [128, 22, 256], R, sc)
        tmp_ring = Ring([big[:, c:c + 256] for c in (2048, 2304, 5632, 5888)], later)
        t_g2 = side.load(pool, gbc[:, :], bass.AP(a["g_final_2"].tensor, 0, [[0, 128], [1, D]]), t_f)
        xt = [None] * 8
        for k in (0, 4):
            xt_turned["t"] = turn_shifted(nrm, k, xt, t_z[k // 4], [done, t_f], gain2, tg2, mod[:, 16:24], tmp_ring)
        cring = Ring([big[:, 2560 + 512 * i:3072 + 512 * i].rearrange("p (k t) -> p k t", k=2) for i in range(6)], later)
        stage = Ring([nrm[:, :, 0:512], nrm[:, :, 512:1024]], later)
        ht = [None] * 22

        pending = deque()

        def flush():
            while pending:
                pending.popleft()()

        def convolved(s, k, kt, after):
            slot, bank, free = work.take()
            tt = turn_blocks(bank, [s[:, t, (k + j) * 128:(k + j + 1) * 128] for j in range(2) for t in range(2)], after, free)
            flush()
            cs, cv, cf = cring.take()
            last_ = []
            for j in range(2):
                t = act.do(lambda e, o=cv[:, j, :], p=bank[:, j * 256:(j + 1) * 256], q=kt + j:
                           e.activation(o, p, ACT.Identity, bias=CVB(q), scale=CVW(2, q)), tt, cf, t_f)
            for j in range(2):
                for n in (1, 2):
                    t = dve.do(lambda e, o=cv[:, j, :], p=bank[:, j * 256:(j + 1) * 256], n=n, q=kt + j: e.scalar_tensor_tensor(
                        out=o[:, n:], in0=p[:, 0:256 - n], scalar=CVW(2 - n, q), in1=o[:, n:], op0=ALU.mult, op1=ALU.add), t)
                last_.append(t)
            work.give(slot, *last_)
            return cs, cv, last_, tt

        def raw_tile(w, then):
            def evac(pair, done, c=c):
                ss, s, sf = stage.take()
                ts = [act.do(lambda e, t=t: e.activation(s[:, t, 0:w], pair[t][:, 0:w], ACT.Copy), done[t], sf, xt_turned["t"]) for t in range(2)]
                for k in range(0, w // 128, 2):
                    later.append(lambda k=k: then(ss, s, ts, k, k + 2 >= w // 128))
                return ts
            return linear("up2", 2 if w == 512 else 1, xTh, xTl, xt, evac)

        for c, w in UP2:
            made = {}

            def gate(ss, s, ts, k, end, c=c, made=made):
                cs, cv, tc, tt = convolved(s, k, 22 + c // 128 + k, ts)
                pending.append(lambda: made.update({k: (cs, cv, act.do(lambda e: e.activation(cv, cv, ACT.Silu), tc))}))
                if end:
                    stage.give(ss, tt)

            def value(ss, s, ts, k, end, c=c, made=made):
                cs, cv, tc, tt = convolved(s, k, c // 128 + k, ts)

                def rest():
                    gs, gv, tg = made[k]
                    t = pool.do(lambda e: e.tensor_tensor(cv, cv, gv, ALU.mult), tc, tg)
                    kt = c // 128 + k
                    o, lo = hTh[:, kt:kt + 2, :], hTl[:, kt:kt + 2, :]
                    th = act.do(lambda e: e.activation(o, cv, ACT.Copy), t, t_f)
                    tl = dve.do(lambda e: e.tensor_tensor(lo, cv, o.bitcast(F), ALU.subtract), th, t_f)
                    ht[kt] = ht[kt + 1] = [th, tl]
                    cring.give(gs, t)
                    cring.give(cs, th, tl)
                pending.append(rest)
                if end:
                    stage.give(ss, tt)
            raw_tile(w, gate)
            raw_tile(w, value)
        later.append(flush)
        rms3 = Rms(next(roots))
        t_res, t_gain = [], [[], []]
        tmps = sb("lasttmp", [128, 2, 512], F, sc)
        for c in (0, 512):
            def evac(pair, done, c=c):
                given = []
                for t in range(2):
                    x = xres[:, t, c:c + 512]
                    m = dve.do(lambda e, t=t: e.tensor_tensor(tmps[:, t, :], pair[t][:, :], gates[:, 1024 + c:1536 + c], ALU.mult), done[t], t_res, t_f)
                    u = dve.do(lambda e, t=t, x=x: e.tensor_tensor(x, x, tmps[:, t, :], ALU.add), m)
                    rms3.square(x, t, c // 512, u)
                    t_gain[t].append(pool.do(lambda e, t=t, x=x: e.tensor_tensor(nrm[:, t, c:c + 512], x, gbc[:, c:c + 512], ALU.mult), u, t_g2))
                    given.append(m)
                    t_res.append(u)
                return given
            linear("down2", 6, hTh, hTl, ht, evac)
        drain_later()

        rms3.root()
        for c in (0, 512):
            x0, x1 = nrm[:, 0, c:c + 512], nrm[:, 1, c:c + 512]
            t0 = act.do(lambda e, x=x0: e.activation(x, x, ACT.Copy, scale=rms3.r[0]), rms3.done, t_gain[0])
            t1 = dve.do(lambda e, x=x1: e.tensor_scalar(x, x, rms3.r[1], None, ALU.mult), rms3.done, t_gain[1])
            for t, x, to in ((0, x0, t0), (1, x1, t1)):
                t_out = outsem.load(sp, out[0, t * 128:(t + 1) * 128, c:c + 512], x, to)
        sp.wait(t_out)
        pool.wait((scrsem.sem, scrsem.n))

        sc.close()
        block = ctx.enter_context(nc.Block())

        @block.sync
        def _(e):
            for f in sp.program:
                f(e)

        @block.scalar
        def _(e):
            for f in act.program:
                f(e)

        @block.vector
        def _(e):
            for f in dve.program:
                f(e)

        @block.gpsimd
        def _(e):
            for f in pool.program:
                f(e)

        @block.tensor
        def _(e):
            for f in pe.program:
                f(e)


def shape_constants():
    p = np.arange(128)
    key = np.arange(256)
    c = np.zeros((128, 1408), np.float32)
    c[:, 0:128] = np.eye(128)
    for t in range(2):
        q = p + 128 * t
        d = np.abs(q[:, None] - key[None, :])
        c[:, 128 + 256 * t:384 + 256 * t] = np.where(d <= 128, d, 1e33)
        c[:, 896 + 256 * t:1152 + 256 * t] = np.where(key[None, :] <= q[:, None], 0.0, -BIG)
    col, kcol = p % 64, key % 64
    start = np.clip(col - 8, 0, 48)
    inside = (kcol[None, :] >= start[:, None]) & (kcol[None, :] < start[:, None] + 16)
    c[:, 640:896] = np.where(inside, 0.0, -BIG)
    return c


def distance_buckets():
    n = np.arange(256)
    nf = np.maximum(n, 1).astype(np.float32)
    big = 16 + (np.log(nf / np.float32(16)) / np.float32(np.log(8.0)) * np.float32(16)).astype(np.int32)
    b = np.where(n < 16, n, np.minimum(big, 31))
    hot = np.zeros((32, 512), np.float32)
    hot[b[::-1], np.arange(256)] = 1.0
    hot[0, 256:] = 1.0
    return hot


def kernel(**inputs):
    import concourse.bacc as _bacc
    from concourse.bass_utils import run_bass_kernel_spmd as _run

    nc = _bacc.Bacc("TRN2", target_bir_lowering=False, num_devices=1)
    arrays, args = {}, {}
    given = {n: np.ascontiguousarray(v) for n, v in inputs.items()}
    given["constants"] = shape_constants()
    given["onehot"] = distance_buckets()
    for name, v in given.items():
        arrays[f"in_{name}"] = v
        args[name] = nc.dram_tensor(f"in_{name}", v.shape, mybir.dt.from_np(v.dtype), kind="ExternalInput").ap()
    args["scratch"] = nc.dram_tensor("scratch", (128, 8, 512), F, kind="Internal").ap()
    args["scratch_rpb"] = nc.dram_tensor("scratch_rpb", (64, 12 * 15 * 31), F, kind="Internal").ap()
    out = nc.dram_tensor("out_0", (1, 256, 1024), F, kind="ExternalOutput").ap()
    build(nc, args, out)
    r = _run(nc, [arrays], core_ids=[0])
    return r.results[0]["out_0"]
```
